# Optimizing a Trainium2 kernel written in Bass

```python
import jax, jax.numpy as jnp
from jax import lax
import numpy as np

D_MODEL = 1024
BATCH = 1
SEQ = 512
DEPTH = 1

HEAD_DIM = 64
N_HEADS_A = 8
N_KV_A = 2
N_HEADS_B = 8
N_KV_B = 2
WIDTH_A = N_HEADS_A * HEAD_DIM
WIDTH_B = N_HEADS_B * HEAD_DIM
MIX_WIDTH = WIDTH_A + WIDTH_B
Q_BLOCK = 128
WINDOW = 128
GRID_W = 64
ROPE_THETA = 10000.0
EPS = 1e-6
D_FF = ((8 * D_MODEL + 3 * 256 - 1) // (3 * 256)) * 256
IN_COLS = (N_HEADS_A + 2 * N_KV_A + N_HEADS_B + 2 * N_KV_B) * HEAD_DIM
SPLITS = tuple(int(s) for s in np.cumsum([WIDTH_A, N_KV_A * HEAD_DIM, N_KV_A * HEAD_DIM,
                                           WIDTH_B, N_KV_B * HEAD_DIM])[:])


def rms_norm(x, g):
    xf = x.astype(jnp.float32)
    y = xf * lax.rsqrt(jnp.mean(xf * xf, axis=-1, keepdims=True) + EPS)
    return (y * g.astype(jnp.float32)).astype(x.dtype)

def apply_rope(x, ang):
    cos = jnp.cos(ang)[None, :, None, :].astype(x.dtype)
    sin = jnp.sin(ang)[None, :, None, :].astype(x.dtype)
    x1, x2 = jnp.split(x, 2, axis=-1)
    return jnp.concatenate([x1 * cos - x2 * sin, x2 * cos + x1 * sin], axis=-1)

def global_attention(q, k, v):
    B, S, Hq, D = q.shape
    Hkv = k.shape[2]
    G = Hq // Hkv
    nb = S // Q_BLOCK
    qb = q.reshape(B, nb, Q_BLOCK, Hkv, G, D).transpose(1, 0, 2, 3, 4, 5)
    scale = D ** -0.5

    def one_block(qi):
        s = jnp.einsum('bqkgd,bskd->bkgqs', qi, k).astype(jnp.float32) * scale
        p = jax.nn.softmax(s, axis=-1).astype(v.dtype)
        return jnp.einsum('bkgqs,bskd->bqkgd', p, v)

    o = lax.map(one_block, qb)
    return o.transpose(1, 0, 2, 3, 4, 5).reshape(B, S, Hq * D)

def window_attention(q, k, v, sink):
    B, S, Hq, D = q.shape
    Hkv = k.shape[2]
    G = Hq // Hkv
    nb = S // Q_BLOCK
    C = 3 * Q_BLOCK
    qb = q.reshape(B, nb, Q_BLOCK, Hkv, G, D)
    pad = ((0, 0), (Q_BLOCK, Q_BLOCK), (0, 0), (0, 0))
    kp = jnp.pad(k, pad).reshape(B, nb + 2, Q_BLOCK, Hkv, D)
    vp = jnp.pad(v, pad).reshape(B, nb + 2, Q_BLOCK, Hkv, D)
    kb = jnp.concatenate([kp[:, :-2], kp[:, 1:-1], kp[:, 2:]], axis=2)
    vb = jnp.concatenate([vp[:, :-2], vp[:, 1:-1], vp[:, 2:]], axis=2)
    scale = D ** -0.5
    s = jnp.einsum('bnqkgd,bnckd->bnkgqc', qb, kb).astype(jnp.float32) * scale
    blk = jnp.arange(nb)[:, None, None]
    qpos = blk * Q_BLOCK + jnp.arange(Q_BLOCK)[None, :, None]
    kpos = (blk - 1) * Q_BLOCK + jnp.arange(C)[None, None, :]
    valid = (jnp.abs(kpos - qpos) <= WINDOW) & (kpos >= 0) & (kpos < S)
    s = jnp.where(valid[None, :, None, None], s, -jnp.inf)
    sink_l = sink.astype(jnp.float32).reshape(1, 1, Hkv, G, 1, 1)
    m = jnp.maximum(jnp.max(s, axis=-1, keepdims=True), sink_l)
    e = jnp.exp(s - m)
    den = jnp.sum(e, axis=-1, keepdims=True) + jnp.exp(sink_l - m)
    p = (e / den).astype(v.dtype)
    o = jnp.einsum('bnkgqc,bnckd->bnqkgd', p, vb)
    return o.reshape(B, S, Hq * D)

def first_inputs(seed: int = 0) -> dict:
    key = jax.random.key(seed)
    ks = jax.random.split(key, 16)
    f32 = jnp.float32

    def gain(k, n):
        return 1.0 + 0.05 * jax.random.normal(k, (DEPTH, n), f32)

    def dense(k, fan_in, fan_out):
        return jax.random.normal(k, (DEPTH, fan_in, fan_out), f32) * fan_in ** -0.5

    return {
        "x": jax.random.normal(ks[0], (BATCH, SEQ, D_MODEL), f32),
        "norm_mix_pre": gain(ks[1], D_MODEL),
        "w_in": dense(ks[2], D_MODEL, IN_COLS),
        "q_norm_a": gain(ks[3], HEAD_DIM),
        "k_norm_a": gain(ks[4], HEAD_DIM),
        "sink_b": 0.5 * jax.random.normal(ks[5], (DEPTH, N_HEADS_B), f32),
        "group_norm_a": gain(ks[6], WIDTH_A),
        "group_norm_b": gain(ks[7], WIDTH_B),
        "w_out": dense(ks[8], MIX_WIDTH, D_MODEL),
        "norm_mix_post": gain(ks[9], D_MODEL),
        "norm_ffn_pre": gain(ks[10], D_MODEL),
        "w_gate": dense(ks[11], D_MODEL, D_FF),
        "w_up": dense(ks[12], D_MODEL, D_FF),
        "w_down": dense(ks[13], D_FF, D_MODEL),
        "norm_ffn_post": gain(ks[14], D_MODEL),
    }

def first_block(x, norm_mix_pre, w_in, q_norm_a, k_norm_a, sink_b, group_norm_a, group_norm_b,
              w_out, norm_mix_post, norm_ffn_pre, w_gate, w_up, w_down, norm_ffn_post):
    B, S, _ = x.shape
    rows = S // GRID_W
    t = jnp.arange(S, dtype=jnp.float32)
    row = jnp.broadcast_to(jnp.arange(rows, dtype=jnp.float32)[:, None], (rows, GRID_W)).reshape(S)
    col = jnp.broadcast_to(jnp.arange(GRID_W, dtype=jnp.float32)[None, :], (rows, GRID_W)).reshape(S)
    ax_pairs = HEAD_DIM // 4
    freq_ax = ROPE_THETA ** (-jnp.arange(ax_pairs, dtype=jnp.float32) / ax_pairs)
    ang_axial = jnp.concatenate([row[:, None] * freq_ax[None, :], col[:, None] * freq_ax[None, :]], axis=-1)
    n_pairs = HEAD_DIM // 2
    freq_1d = ROPE_THETA ** (-jnp.arange(n_pairs, dtype=jnp.float32) / n_pairs)
    ang_1d = t[:, None] * freq_1d[None, :]

    for l in range(DEPTH):
        h = rms_norm(x, norm_mix_pre[l])
        proj = h @ w_in[l]
        qa, ka, va, qb, kb, vb = jnp.split(proj, SPLITS, axis=-1)

        qa = apply_rope(rms_norm(qa.reshape(B, S, N_HEADS_A, HEAD_DIM), q_norm_a[l]), ang_axial)
        ka = apply_rope(rms_norm(ka.reshape(B, S, N_KV_A, HEAD_DIM), k_norm_a[l]), ang_axial)
        va = va.reshape(B, S, N_KV_A, HEAD_DIM)
        out_a = global_attention(qa, ka, va)

        qb = apply_rope(qb.reshape(B, S, N_HEADS_B, HEAD_DIM), ang_1d)
        kb = apply_rope(kb.reshape(B, S, N_KV_B, HEAD_DIM), ang_1d)
        vb = vb.reshape(B, S, N_KV_B, HEAD_DIM)
        out_b = window_attention(qb, kb, vb, sink_b[l])

        mixed = jnp.concatenate([rms_norm(out_a, group_norm_a[l]),
                                 rms_norm(out_b, group_norm_b[l])], axis=-1) @ w_out[l]
        x = x + rms_norm(mixed, norm_mix_post[l])

        h = rms_norm(x, norm_ffn_pre[l])
        f = (jax.nn.silu(h @ w_gate[l]) * (h @ w_up[l])) @ w_down[l]
        x = x + rms_norm(f, norm_ffn_post[l])
    return x


CHUNK = 64
MIX_WIDTH_2 = D_MODEL
ATTN_WIDTH = MIX_WIDTH_2 // 2
N_HEADS = 8
HEAD_DIM_2 = ATTN_WIDTH // N_HEADS
POOL_WIDTH = MIX_WIDTH_2 - ATTN_WIDTH
POOL_WINDOWS = (2, 4, 8, 16)
N_POOL_GROUPS = len(POOL_WINDOWS)
POOL_GROUP = POOL_WIDTH // N_POOL_GROUPS
IN_WIDTH = 3 * ATTN_WIDTH + N_HEADS + POOL_WIDTH
D_FF_2 = -(-(8 * D_MODEL) // (3 * 256)) * 256


def rmsnorm(x, g):
    xf = x.astype(jnp.float32)
    y = xf * lax.rsqrt(jnp.mean(xf * xf, axis=-1, keepdims=True) + EPS)
    return (y * g.astype(jnp.float32)).astype(x.dtype)

def forgetting_attention(q, k, v, log_f):
    S, Dh = q.shape[2], q.shape[3]
    c = jnp.cumsum(log_f, axis=-1)
    qf = q.astype(jnp.float32) * (Dh ** -0.5)
    kf = k.astype(jnp.float32)
    vf = v.astype(jnp.float32)
    outs = []
    for i in range(S // Q_BLOCK):
        q0, q1 = i * Q_BLOCK, (i + 1) * Q_BLOCK
        logits = jnp.einsum('bhqd,bhkd->bhqk', qf[:, :, q0:q1], kf[:, :, :q1])
        logits = logits + c[:, :, q0:q1, None] - c[:, :, None, :q1]
        t_pos = jnp.arange(q0, q1)[:, None]
        s_pos = jnp.arange(q1)[None, :]
        logits = jnp.where(s_pos <= t_pos, logits, -jnp.inf)
        p = jax.nn.softmax(logits, axis=-1)
        outs.append(jnp.einsum('bhqk,bhkd->bhqd', p, vf[:, :, :q1]))
    return jnp.concatenate(outs, axis=2).astype(q.dtype)

def multiscale_pool(u, w_pool, pool_scale):
    B, S, C = u.shape
    uf = u.astype(jnp.float32)
    cs = jnp.concatenate([jnp.zeros((B, 1, C), jnp.float32), jnp.cumsum(uf, axis=1)], axis=1)
    t = jnp.arange(S)
    groups = []
    for g, w in enumerate(POOL_WINDOWS):
        lo, hi = g * POOL_GROUP, (g + 1) * POOL_GROUP
        start = jnp.maximum(t + 1 - w, 0)
        csg = cs[:, :, lo:hi]
        window_sum = csg[:, 1:] - csg[:, start]
        count = (t + 1 - start).astype(jnp.float32)[None, :, None]
        groups.append(window_sum / count - uf[:, :, lo:hi])
    pooled = jnp.stack(groups, axis=2)
    mixed = jnp.einsum('bsgc,gcd->bsgd', pooled, w_pool.astype(jnp.float32)).reshape(B, S, C)
    return (mixed * pool_scale.astype(jnp.float32)).astype(u.dtype)

def second_inputs(seed: int = 0) -> dict:
    key = jax.random.key(seed)
    ks = jax.random.split(key, 13)
    f32 = jnp.float32
    nrm = lambda k, shape, scale: jax.random.normal(k, shape, f32) * scale
    return {
        "x": jax.random.normal(ks[0], (BATCH, SEQ, D_MODEL), f32),
        "norm1_g": 1.0 + nrm(ks[1], (DEPTH, D_MODEL), 0.05),
        "w_in": nrm(ks[2], (DEPTH, D_MODEL, IN_WIDTH), D_MODEL ** -0.5),
        "b_forget": 2.0 + nrm(ks[3], (DEPTH, N_HEADS), 0.5),
        "w_pool": nrm(ks[4], (DEPTH, N_POOL_GROUPS, POOL_GROUP, POOL_GROUP), POOL_GROUP ** -0.5),
        "pool_scale": 1.0 + nrm(ks[5], (DEPTH, POOL_WIDTH), 0.1),
        "w_out": nrm(ks[6], (DEPTH, MIX_WIDTH_2, D_MODEL), MIX_WIDTH_2 ** -0.5),
        "norm2_g": 1.0 + nrm(ks[7], (DEPTH, D_MODEL), 0.05),
        "w_gate": nrm(ks[8], (DEPTH, D_MODEL, D_FF_2), D_MODEL ** -0.5),
        "w_up": nrm(ks[9], (DEPTH, D_MODEL, D_FF_2), D_MODEL ** -0.5),
        "w_down": nrm(ks[10], (DEPTH, D_FF_2, D_MODEL), D_FF_2 ** -0.5),
        "final_g": 1.0 + nrm(ks[11], (D_MODEL,), 0.05),
    }

def second_block(x, norm1_g, w_in, b_forget, w_pool, pool_scale, w_out, norm2_g, w_gate, w_up, w_down, final_g):
    B, S, _ = x.shape
    for layer in range(DEPTH):
        h = rmsnorm(x, norm1_g[layer])
        proj = jnp.einsum('bsd,de->bse', h, w_in[layer])
        a0 = ATTN_WIDTH
        q = proj[..., 0:a0]
        k = proj[..., a0:2 * a0]
        v = proj[..., 2 * a0:3 * a0]
        f_logit = proj[..., 3 * a0:3 * a0 + N_HEADS]
        u = proj[..., 3 * a0 + N_HEADS:]
        to_heads = lambda t: t.reshape(B, S, N_HEADS, HEAD_DIM_2).transpose(0, 2, 1, 3)
        log_f = jax.nn.log_sigmoid(f_logit.astype(jnp.float32) + b_forget[layer].astype(jnp.float32))
        log_f = log_f.transpose(0, 2, 1)
        attn = forgetting_attention(to_heads(q), to_heads(k), to_heads(v), log_f)
        attn = attn.transpose(0, 2, 1, 3).reshape(B, S, ATTN_WIDTH)
        pool = multiscale_pool(u, w_pool[layer], pool_scale[layer])
        mixed = jnp.concatenate([attn, pool], axis=-1)
        x = x + jnp.einsum('bse,ed->bsd', mixed, w_out[layer])
        h2 = rmsnorm(x, norm2_g[layer])
        gate = jnp.einsum('bsd,df->bsf', h2, w_gate[layer])
        up = jnp.einsum('bsd,df->bsf', h2, w_up[layer])
        x = x + jnp.einsum('bsf,fd->bsd', jax.nn.silu(gate) * up, w_down[layer])
    return rmsnorm(x, final_g)


def setup_inputs(seed=0):
    out = dict(first_inputs(seed))
    for name, value in second_inputs(seed + 1).items():
        if name != "x":
            out[name + "_2"] = value
    return out


def reference(
    x, norm_mix_pre, w_in, q_norm_a, k_norm_a, sink_b, group_norm_a, group_norm_b, w_out,
    norm_mix_post, norm_ffn_pre, w_gate, w_up, w_down, norm_ffn_post, norm1_g_2, w_in_2,
    b_forget_2, w_pool_2, pool_scale_2, w_out_2, norm2_g_2, w_gate_2, w_up_2, w_down_2,
    final_g_2,
):
    x = first_block(
        x, norm_mix_pre, w_in, q_norm_a, k_norm_a, sink_b, group_norm_a, group_norm_b, w_out,
        norm_mix_post, norm_ffn_pre, w_gate, w_up, w_down, norm_ffn_post,
    )
    return second_block(
        x, norm1_g_2, w_in_2, b_forget_2, w_pool_2, pool_scale_2, w_out_2, norm2_g_2, w_gate_2,
        w_up_2, w_down_2, final_g_2,
    )


_drawn_inputs = setup_inputs


def setup_inputs(seed=0):
    import zlib

    import numpy as np

    out = dict(_drawn_inputs(seed))
    spreads = {}
    factors = {'sink_b': 8.0}
    for name, (base, spread) in spreads.items():
        noise = np.random.default_rng([zlib.crc32(name.encode()), seed]).standard_normal(out[name].shape)
        drawn = base * np.exp(spread * noise) if base else spread * noise
        out[name] = __import__('jax').numpy.asarray(drawn.astype(out[name].dtype))
    for name, factor in factors.items():
        out[name] = (out[name] * factor).astype(out[name].dtype)
    return out
```

```python
from contextlib import ExitStack

import numpy as np
import concourse.bass as bass
from concourse import mybir

ACT = mybir.ActivationFunctionType
ALU = mybir.AluOpType
AX = mybir.AxisListType
F32 = mybir.dt.float32
F32R = mybir.dt.float32r
BF16 = mybir.dt.bfloat16

EPS = 1e-6
NEG = -3.0e38
D = 1024
FF = 2816
NF = FF // 128
BASE = 16640
NRAW = 3
NSPLIT = 4
WCOLS = 1056

G_PRE, G_POST, G_FPRE, G_FPOST, G_N1, G_N2, G_A, G_B, G_PS = 0, 8, 16, 24, 32, 40, 48, 52, 56
NG = 60


class Signal:

    def __init__(self, handle):
        self.handle, self.value, self.owner = handle, 0, None

    def up(self, owner, by):
        assert self.owner in (None, owner)
        self.owner = owner
        self.value += by
        return (self, self.value)


class Queue:

    def __init__(self, name):
        self.name, self.ops, self.seen = name, [], {}

    def __call__(self, fn, *waits, sig=None, by=1):
        need = []
        todo = list(waits)
        while todo:
            w = todo.pop()
            if w is None:
                continue
            if isinstance(w, list):
                todo += w
                continue
            s, v = w
            if self.seen.get(s, 0) < v:
                self.seen[s] = v
                need.append(w)
        self.ops.append((need, fn, sig, by))
        return sig.up(self.name, by) if sig is not None else None

    def play(self, engine):
        for need, fn, sig, by in self.ops:
            best = {}
            for s, v in need:
                best[s] = max(best.get(s, 0), v)
            for s, v in best.items():
                engine.wait_ge(s.handle, v)
            ins = fn(engine)
            if sig is not None:
                ins.then_inc(sig.handle, by)


def rope_and_masks():
    r = np.arange(128)[:, None]
    c = np.arange(128)[None, :]
    ident = np.eye(128, dtype=np.float32)
    left = np.where(c >= r, 0.0, NEG).astype(np.float32)
    right = np.where(c <= r, 0.0, NEG).astype(np.float32)
    upper = (r <= c).astype(np.float32)
    count = np.zeros((128, 4, 16), np.float32)
    for g in range(4):
        count[:, g, :] = 1.0 / np.minimum(np.arange(16) + 1, 2 ** (g + 1))
    sel = np.zeros((128, 8), np.float32)
    for h in range(8):
        sel[h, h] = sel[8 + h, h] = 1.0
    t = np.arange(512, dtype=np.float32)
    theta = np.float64(10000.0)
    fa = (theta ** (-np.arange(16, dtype=np.float64) / 16)).astype(np.float32)
    f1 = (theta ** (-np.arange(32, dtype=np.float64) / 32)).astype(np.float32)
    row, col = np.floor(t / 64).astype(np.float32), (t % 64).astype(np.float32)
    ax = np.concatenate([row[:, None] * fa[None], col[:, None] * fa[None]], axis=1)
    a1 = t[:, None] * f1[None]
    tabs = []
    for ang in (ax, a1):
        cs, sn = np.cos(ang.astype(np.float64)), np.sin(ang.astype(np.float64))
        for full in (np.concatenate([cs, cs], 1), np.concatenate([-sn, sn], 1)):
            tabs.append(full.astype(np.float32).reshape(4, 128, 64).transpose(1, 0, 2).reshape(128, 256))
    small = np.concatenate([left, right, upper, count.reshape(128, 64), sel], axis=1)
    return ident, np.ascontiguousarray(small), np.ascontiguousarray(np.concatenate(tabs, axis=1))


def program(nc, x_t, gain_cols, w_in, q_norm_a, k_norm_a, sink_b, w_out, w_gate, w_up, w_down, w_in_2, b_forget_2,
            w_pool_2, w_out_2, w_gate_2, w_up_2, w_down_2, final_g_2, c_ident, c_small, c_rope, out):
    ctx = ExitStack()
    signals = {}

    def sg(name):
        if name not in signals:
            signals[name] = Signal(ctx.enter_context(nc.semaphore(name)))
        return signals[name]

    PE, SCA, VEC, POOL, SP = (Queue(n) for n in ("pe", "act", "dve", "pool", "sp"))

    def sb(name, shape, dt, off):
        return nc.alloc_sbuf_tensor_at(name, shape, dt, offset=BASE + off)

    o_xt, o_hh, o_hl = 0, 16384, 32768
    XT = sb("XT", [128, 8, 512], F32, o_xt)
    HH = sb("HH", [128, 8, 512], F32R, o_hh)
    HL = sb("HL", [128, 8, 512], F32R, o_hl)
    o_raw = 49152
    RAW = [sb(f"RAW{i}", [128, WCOLS], F32, o_raw + 4224 * i) for i in range(NRAW)]
    o_w = o_raw + 4224 * NRAW
    WH = [sb(f"WH{i}", [128, WCOLS], F32R, o_w + 8448 * i) for i in range(NSPLIT)]
    WL = [sb(f"WL{i}", [128, WCOLS], F32R, o_w + 8448 * i + 4224) for i in range(NSPLIT)]
    o_c = o_w + 8448 * NSPLIT
    cur = [o_c]

    def const(name, shape, dt, nbytes):
        t = sb(name, shape, dt, cur[0])
        cur[0] += (nbytes + 31) // 32 * 32
        return t

    IDENT = const("IDENT", [128, 128], F32, 512)
    ONES = const("ONES", [128, 128], F32, 512)
    UPPER = const("UPPER", [128, 128], F32, 512)
    IDB = const("IDB", [128, 128], BF16, 256)
    MLB = const("MLB", [128, 128], BF16, 256)
    MRB = const("MRB", [128, 128], BF16, 256)
    ONB = const("ONB", [128, 128], BF16, 256)
    GC = const("GC", [128, NG], F32, 240)
    ICNT = const("ICNT", [128, 4, 16], F32, 256)
    SEL = const("SEL", [128, 8], F32R, 32)
    SKB = const("SKB", [128, 8], BF16, 16)
    BF = const("BF", [128, 8], F32, 32)
    HALF = const("HALF", [128, 1], F32, 4)
    RN = const("RN", [128, 4], F32, 16)
    RN8 = const("RN8", [128, 4], F32, 16)
    SSH = const("SSH", [128, 16], F32, 64)
    FH16 = const("FH16", [128, 16], F32, 64)
    NM = const("NM", [128, 8], F32, 32)
    DEN = const("DEN", [128, 8], F32, 32)
    RD = const("RD", [128, 8], F32, 32)
    RSC = const("RSC", [128, 12, 8], F32, 384)
    SKF = const("SKF", [128, 8], F32, 32)
    SKT = const("SKT", [128, 8], F32, 32)
    SKT2 = const("SKT2", [128, 8], BF16, 16)
    o_r = cur[0]
    REG = 229368 - BASE - o_r

    def rg(name, shape, dt, off):
        t = sb(name, shape, dt, o_r + off)
        n = 4 if dt != BF16 else 2
        for s in shape[1:]:
            n *= s
        assert off + n <= REG, (name, off + n, REG)
        return t

    PTH = [rg(f"PTH{i}", [128, 4, 256], F32R, 8192 * i) for i in range(2)]
    PTL = [rg(f"PTL{i}", [128, 4, 256], F32R, 8192 * i + 4096) for i in range(2)]
    MIX1 = rg("MIX1", [128, 8, 512], F32, 0)
    OR = rg("OR", [128, 8, 512], F32, 16384)
    QS = rg("QS", [128, 8, 512], F32R, 32768)
    K1 = rg("K1", [128, 4, 512], F32R, 49152)
    K2 = rg("K2", [128, 2, 512], F32R, 57344)
    VS = rg("VS", [128, 4, 4, 128], F32R, 61440)
    PR = [rg(f"PR{i}", [128, 516], F32, 69632 + 2080 * i) for i in range(4)]
    OT = [rg(f"OT{i}", [128, 256], F32, 77952 + 1024 * i) for i in range(2)]
    TQ1 = rg("TQ1", [128, 4, 64], F32, 80000)
    TQ2 = rg("TQ2", [128, 4, 64], F32, 81024)
    TAB = rg("TAB", [128, 4, 4, 64], F32, 82048)
    RW = [rg(f"RW{i}", [128, 512], F32, 86144 + 2048 * i) for i in range(2)]
    QRAW = rg("QRAW", [128, 4, 256], F32, 90240)
    WA = rg("WA", [128, 4, 256], F32, 94336)
    WB = rg("WB", [128, 4, 256], F32, 98432)
    KLN = rg("KLN", [128, 4, 256], F32R, 28672)
    STK = rg("STK", [128, 4, 4, 128], F32R, 102528)
    SQ4 = rg("SQ4", [128, 4, 512], F32, 102528)
    CSM = rg("CSM", [128, 456], F32, 104576)
    QKG = rg("QKG", [128, 2, 64], F32, 106496)

    TS = [rg(f"TS{i}", [128, 512], F32, 2048 * i) for i in range(2)]
    TU = [rg(f"TU{i}", [128, 512], F32, 4096 + 2048 * i) for i in range(2)]
    FFH = rg("FFH", [128, NF, 512], F32R, 8192)
    FFL = rg("FFL", [128, NF, 512], F32R, 8192 + 2048 * NF)
    o_n = 8192 + 4096 * NF
    NSQ = [rg(f"NSQ{i}", [128, 512], F32, o_n + 2048 * i) for i in range(2)]
    NSUM = rg("NSUM", [128, 512], F32, o_n + 4096)
    NRP = rg("NRP", [128, 512], F32, o_n + 6144)
    NU = [rg(f"NU{i}", [128, 256], F32, o_n + 8192 + 1024 * i) for i in range(2)]
    NSUM2 = rg("NSUM2", [128, 512], F32, o_n + 10240)
    R2 = rg("R2", [128, 512], F32, o_n + 12288)
    MIX2 = sb("MIX2", [128, 8, 512], F32, o_hl)

    QS2 = rg("QS2", [128, 8, 512], F32R, 16384)
    K1B = rg("K1B", [128, 8, 512], F32R, 32768)
    K2B = rg("K2B", [128, 4, 512], F32R, 49152)
    VSB = rg("VSB", [128, 8, 4, 128], F32R, 57344)
    PRB = [rg(f"PRB{i}", [128, 512], F32, 73728 + 2048 * i) for i in range(4)]
    OTB = [rg(f"OTB{i}", [128, 256], F32, 81920 + 1024 * i) for i in range(2)]
    FLG, FL1, FL2, FL3 = (rg(f"FLG{i}", [128, 4, 8], F32, 81920 + 128 * i) for i in range(4))
    CN = rg("CN", [128, 4, 16], F32R, 82432)
    ORB = rg("ORB", [128, 4, 512], F32, 83968)
    CT = rg("CT", [16, 512], F32R, 92160)
    STK2 = rg("STK2", [128, 4, 4, 128], F32R, 94208)
    KLN2 = rg("KLN2", [128, 4, 256], F32R, 102400)
    AH = [rg(f"AH{i}", [128, 512], F32R, 94208 + 4096 * i if i < 3 else 73728) for i in range(4)]
    AL = [rg(f"AL{i}", [128, 512], F32R, 94208 + 4096 * i + 2048 if i < 3 else 75776) for i in range(4)]
    UR = rg("UR", [128, 4, 512], F32, 16384)
    _pl = [32768, 36864, 49152, 83968]
    PLH = [rg(f"PLH{i}", [128, 512], F32R, _pl[i]) for i in range(4)]
    PLL = [rg(f"PLL{i}", [128, 512], F32R, _pl[i] + 2048) for i in range(4)]
    PS1 = rg("PS1", [128, 512], F32, 57344)
    PS2 = rg("PS2", [128, 512], F32, 59392)
    PDH = rg("PDH", [128, 512], F32R, 61440)
    PDL = rg("PDL", [128, 512], F32R, 63488)

    X3N = sb("X3N", [128, 4, 1024], F32, o_hh)
    YO = sb("YO", [128, 4, 1024], F32, o_hl)
    FG = rg("FG", [128, 1024], F32, o_n)
    JNK = rg("JNK", [128, 512], F32, o_n + 4096)
    SSF = rg("SSF", [128, 8], F32, o_n + 6144)
    SSG = rg("SSG", [128, 4], F32, o_n + 6176)
    RFN = rg("RFN", [128, 4], F32, o_n + 6208)

    B = [ctx.enter_context(nc.psum_tensor(f"B{i}", [128, 512], F32)) for i in range(8)]
    bank_free = [[] for _ in range(8)]

    def f32(ap):
        return ap.bitcast(F32)

    chunks = []

    def wchunk(w, k0, nk, c0, nc_):
        chunks.append(([(w[0, 128 * k0:128 * (k0 + nk), c0:c0 + nc_].rearrange("(k p) c -> p k c", p=128), 0, nc_)],
                       nk, nc_))

    def wchunk2(w, k0, nk, ca, cb):
        chunks.append(([(w[0, 128 * k0:128 * (k0 + nk), c:c + 128].rearrange("(k p) c -> p k c", p=128), 128 * i, 128)
                        for i, c in enumerate((ca, cb))], nk, 256))

    for kh in range(2):
        wchunk2(w_in, 4 * kh, 4, 512, 1280)
        wchunk2(w_in, 4 * kh, 4, 640, 1408)
    for c0 in (0, 256, 768, 1024):
        for kh in range(2):
            wchunk(w_in, 4 * kh, 4, c0, 256)
    for kh, mps in ((0, (0, 1, 2)), (1, (0, 1, 2))):
        for mp in mps:
            wchunk(w_out, 4 * kh, 4, 256 * mp, 256)
    for kh in range(2):
        wchunk(w_out, 4 * kh, 4, 768, 256)

    def ffn_chunks(wg, wu, interleave):
        for p in range(NF // 2):
            order = [(w, kh) for kh in range(2) for w in (wg, wu)] if p == 0 and interleave else \
                [(w, kh) for w in (wg, wu) for kh in range(2)]
            for w, kh in order:
                wchunk(w, 4 * kh, 4, 256 * p, 256)

    ffn_chunks(w_gate, w_up, True)
    KD = [(k, min(4, NF - k)) for k in range(0, NF, 4)]
    for mp in range(4):
        for k0, nk in KD:
            wchunk(w_down, k0, nk, 256 * mp, 256)
    for kh in range(2):
        for c0 in (0, 512):
            wchunk(w_in_2, 4 * kh, 4, c0, 256)
    for c0, n in ((1024, 256), (1280, 264), (256, 256), (768, 256), (1544, 256), (1800, 256)):
        for kh in range(2):
            wchunk(w_in_2, 4 * kh, 4, c0, n)
    chunks.append(([(w_pool_2[0].rearrange("g p c -> p g c"), 0, 128)], 4, 128))
    for kh, mps in ((1, (0, 1, 2)), (0, (0, 1, 2))):
        for mp in mps:
            wchunk(w_out_2, 4 * kh, 4, 256 * mp, 256)
    for kh in (1, 0):
        wchunk(w_out_2, 4 * kh, 4, 768, 256)
    ffn_chunks(w_gate_2, w_up_2, True)
    for fh in range(2):
        for k0 in range(0, NF, 2):
            wchunk(w_down_2, k0, 2, 512 * fh, 512)

    class Weights:
        def __init__(self):
            self.loaded, self.split_n, self.next = 0, 0, 0
            self.lo_queue, self.low, self.defer = VEC, [], False
            self.dma, self.hi, self.lo, self.free = {}, {}, {}, {}

        def view(self, t, j):
            _, nk, n = chunks[j]
            return t[:, :nk * n].rearrange("p (k c) -> p k c", k=nk)

        def load(self):
            j = self.loaded
            if j >= len(chunks) or (j >= NRAW and (j - NRAW) not in self.lo):
                return False
            pieces, nk, n = chunks[j]
            dst = self.view(RAW[j % NRAW], j)
            raw_free = [self.hi[j - NRAW], self.lo[j - NRAW]] if j >= NRAW else None
            for ap, c0, cn in pieces:
                self.dma[j] = SP(lambda e, ap=ap, c0=c0, cn=cn: e.dma_start(dst[:, :, c0:c0 + cn], ap),
                                 raw_free, sig=sg(f"dma_w{j % NRAW}"), by=16)
            self.loaded += 1
            return True

        def split(self):
            j = self.split_n
            if j >= self.loaded or (j >= NSPLIT and (j - NSPLIT) not in self.free):
                return False
            _, nk, n = chunks[j]
            raw, hi, lo = (t[:, :nk * n] for t in (RAW[j % NRAW], WH[j % NSPLIT], WL[j % NSPLIT]))
            slot_free = self.free.get(j - NSPLIT)
            self.hi[j] = SCA(lambda e: e.activation(hi, raw, ACT.Copy), self.dma[j], slot_free, sig=sg("act_w"))
            q = self.lo_queue

            def low():
                self.lo[j] = q(lambda e: e.tensor_tensor(lo, raw, f32(hi), ALU.subtract), self.hi[j], slot_free,
                               sig=sg(q.name + "_w"))
            self.low.append(low)
            self.split_n += 1
            return True

        def flush(self):
            while self.low:
                self.low.pop(0)()

        def ahead(self, n):
            self.flush()
            while self.loaded < min(n, len(chunks)) and self.load():
                pass
            while self.split_n < min(n, len(chunks)):
                if not self.split():
                    break
                if not self.defer:
                    self.flush()
                self.load()
            while self.load():
                pass

        def take(self, more=2):
            j = self.next
            self.next += 1
            while self.split_n <= j:
                if not self.split():
                    self.flush()
                    if self.split_n <= j and not self.split():
                        assert self.load()
            if j not in self.lo or not more:
                self.flush()
            while self.load():
                pass
            if more:
                self.ahead(j + 1 + more)
            assert self.split_n > j
            return j, self.view(WH[j % NSPLIT], j), self.view(WL[j % NSPLIT], j), [self.hi[j], self.lo[j]]

    W = Weights()

    def mm3(dst, sta, mov, start, stop, *waits, sig=None):
        (sh, sl), (mh, ml) = sta, mov
        PE(lambda e: e.matmul(dst, sh, mh, start=start, stop=False), *waits)
        PE(lambda e: e.matmul(dst, sh, ml, start=False, stop=False))
        return PE(lambda e: e.matmul(dst, sl, mh, start=False, stop=stop), sig=sig)

    def transpose(dst, src, *waits, sig=None):
        n = src.shape[0]
        return PE(lambda e: e.transpose(dst, src, IDENT[0:n, 0:n]), *waits, sig=sig)

    ld_gains = SP(lambda e: e.dma_start(GC[:, :], gain_cols), sig=sg("dma_gains"), by=16)
    ld_x = {}

    def load_x(k0, n):
        t = SP(lambda e: e.dma_start(XT[:, k0:k0 + n, :], x_t[:, k0:k0 + n, :]), sig=sg(f"dma_x{k0}"), by=16)
        for k in range(k0, k0 + n):
            ld_x[k] = t

    load_x(0, 1)
    W.load()
    load_x(1, 1)
    W.load()
    load_x(2, 2)
    W.load()
    load_x(4, 2)
    load_x(6, 2)
    ld_ident = SCA(lambda e: e.dma_start(IDENT[:, :], c_ident), sig=sg("dma_ident"), by=16)
    ld_csm = SCA(lambda e: e.dma_start(CSM[:, :], c_small), ld_x[2], sig=sg("dma_csm"), by=16)
    cst = sg("pool_const")
    POOL(lambda e: e.memset(HALF[:, :], -0.5), sig=cst)
    onb_ready = POOL(lambda e: e.memset(ONB[:, :], 1.0), sig=cst)
    POOL(lambda e: e.memset(SKB[:, :], 0.0), sig=cst)
    ones_ready = POOL(lambda e: e.memset(ONES[:, :], 1.0), sig=cst)
    ld_tab = POOL(lambda e: e.dma_start(TAB[:, :, :, :].rearrange("p a b c -> p (a b c)"), c_rope), ld_x[2],
                  sig=sg("dma_tab"), by=16)
    ld_qkg = None
    for i, g in enumerate((q_norm_a, k_norm_a)):
        ld_qkg = POOL(lambda e, i=i, g=g: e.dma_start(QKG[:, i, :], g[0:1, :].broadcast_to([128, 64])),
                      sig=sg("dma_qkg"), by=16)
    ld_sink = POOL(lambda e: e.dma_start(SKF[:, :], sink_b[0:1, :].broadcast_to([128, 8])), sig=sg("dma_sink"), by=16)
    ld_bf = POOL(lambda e: e.dma_start(BF[:, :], b_forget_2[0:1, :].broadcast_to([128, 8])), sig=sg("dma_bf"), by=16)
    gains = ld_gains

    def half_col(shape):
        return HALF[:, 0:1].to_broadcast(shape)

    def gcol(g, k):
        return GC[:, g + k:g + k + 1]

    h_ready = [None] * 8
    xs = {"sum": None, "sq": [None, None]}
    XSUM, XSQ = WA[:, 0:2, :].rearrange("p a c -> p (a c)"), [WB[:, 0:2, :].rearrange("p a c -> p (a c)"),
                                                             WB[:, 2:4, :].rearrange("p a c -> p (a c)")]

    def prep(kt):
        hi = SCA(lambda e: e.activation(HH[:, kt, :], XT[:, kt, :], ACT.Copy, scale=gcol(G_PRE, kt)),
                 ld_x[kt], gains, sig=sg("act_h"))
        h_ready[kt] = VEC(lambda e: e.scalar_tensor_tensor(HL[:, kt, :], XT[:, kt, :], gcol(G_PRE, kt),
                                                           f32(HH[:, kt, :]), ALU.mult, ALU.subtract),
                          hi, ld_x[kt], gains, sig=sg("dve_h"))

    def square(kt):
        if kt == 0:
            xs["sum"] = SCA(lambda e: e.activation(XSUM, XT[:, 0, :], ACT.Square), ld_x[0], sig=sg("act_xsq"))
            return
        i = kt % 2
        q = SCA(lambda e: e.activation(XSQ[i], XT[:, kt, :], ACT.Square), ld_x[kt], xs["sq"][i], sig=sg("act_xsq"))
        xs["sum"] = xs["sq"][i] = VEC(lambda e: e.tensor_tensor(XSUM, XSUM, XSQ[i], ALU.add), q, xs["sum"],
                                      sig=sg("dve_xsum"))

    kv_chunk = {}
    kv_done = [None]

    def kv_mm(kt):
        for g in range(2):
            j, wh, wl, wt = kv_chunk[g]
            for b in range(4):
                tok = slice(128 * b, 128 * b + 128)
                dst = B[2 * g + b // 2][:, 256 * (b % 2):256 * (b % 2) + 256]
                end = kt % 4 == 3 and b == 3
                t = mm3(dst, (HH[:, kt, tok], HL[:, kt, tok]), (wh[:, kt % 4, :], wl[:, kt % 4, :]),
                        kt == 0 and b % 2 == 0, kt == 7 and b % 2 == 1, h_ready[kt], wt, sig=sg("pe_kv") if end else None)
                if end:
                    W.free[j] = kv_done[0] = t

    def other_constants():
        VEC(lambda e: e.tensor_copy(IDB[:, :], IDENT[:, :]), ld_ident, sig=sg("dve_c"))
        VEC(lambda e: e.tensor_copy(MLB[:, :], CSM[:, 0:128]), ld_csm, sig=sg("dve_c"))
        VEC(lambda e: e.tensor_copy(MRB[:, :], CSM[:, 128:256]), sig=sg("dve_c"))
        VEC(lambda e: e.tensor_copy(UPPER[:, :], CSM[:, 256:384]), sig=sg("dve_c"))
        VEC(lambda e: e.tensor_copy(ICNT[:, :, :].rearrange("p g t -> p (g t)"), CSM[:, 384:448]), sig=sg("dve_c"))
        A.consts = VEC(lambda e: e.tensor_copy(SEL[:, :], CSM[:, 448:456]), sig=sg("dve_c"))
        s0 = VEC(lambda e: e.tensor_copy(SKB[0:1, :], SKF[0:1, :]), ld_sink, ones_ready, sig=sg("dve_sk"))
        s1 = VEC(lambda e: e.tensor_tensor(SKT[0:1, :], SKF[0:1, :], SKB[0:1, :], ALU.subtract), s0, sig=sg("dve_sk"))
        s2 = VEC(lambda e: e.tensor_copy(SKB[32:33, :], SKT[0:1, :]), s1, sig=sg("dve_sk"))
        s2b = VEC(lambda e: e.tensor_copy(SKT2[0:1, :], SKT[0:1, :]), s1, sig=sg("dve_sk"))
        s3 = VEC(lambda e: e.tensor_tensor(SKT[0:1, :], SKT[0:1, :], SKT2[0:1, :], ALU.subtract), s2, s2b,
                 sig=sg("dve_sk"))
        A.sink_ready = VEC(lambda e: e.tensor_copy(SKB[64:65, :], SKT[0:1, :]), s3, sig=sg("dve_sk"))
        tq = VEC(lambda e: e.tensor_tensor(TQ1[:, :, :], TAB[:, 0, :, :], QKG[:, 0:1, :].to_broadcast([128, 4, 64]),
                                           ALU.mult), ld_tab, ld_qkg, sig=sg("dve_tab"))
        for s in range(2):
            a, z = 32 * s, 32 * (1 - s)
            tq = VEC(lambda e, a=a, z=z: e.tensor_tensor(
                TQ2[:, :, a:a + 32], TAB[:, 1, :, a:a + 32],
                QKG[:, 0:1, z:z + 32].to_broadcast([128, 4, 32]), ALU.mult), sig=sg("dve_tab"))
        tk = VEC(lambda e: e.tensor_tensor(TAB[:, 0, :, :], TAB[:, 0, :, :],
                                           QKG[:, 1:2, :].to_broadcast([128, 4, 64]), ALU.mult), tq, sig=sg("dve_tab"))
        for s in range(2):
            a, z = 32 * s, 32 * (1 - s)
            tk = VEC(lambda e, a=a, z=z: e.tensor_tensor(
                TAB[:, 1, :, a:a + 32], TAB[:, 1, :, a:a + 32],
                QKG[:, 1:2, z:z + 32].to_broadcast([128, 4, 32]), ALU.mult), tq, sig=sg("dve_tab"))
        A.tables = tk

    class Bag:
        pass

    A = Bag()
    prep(0)
    kv_chunk[0] = W.take(0)
    prep(1)
    kv_chunk[1] = W.take(0)
    kv_mm(0)
    prep(2)
    kv_mm(1)
    prep(3)
    kv_mm(2)
    prep(4)
    kv_mm(3)
    kv_chunk[0] = W.take(0)
    prep(5)
    kv_chunk[1] = W.take(0)
    prep(6)
    prep(7)
    W.ahead(5)
    kv_mm(4)
    for kt in range(4):
        square(kt)
    W.ahead(6)
    kv_mm(5)
    for kt in range(4, 8):
        square(kt)
    kv_mm(6)

    rstd_use = [0]

    def rstd_tokens(sums, n, bank, done):
        nb = sums.shape[1] // 128
        i = rstd_use[0]
        rstd_use[0] += 1
        v, r = RSC[:, i, 0:nb], RSC[:, i, 4:4 + nb]
        for b in range(nb):
            m = PE(lambda e, b=b: e.matmul(B[bank][:, b:b + 1], sums[:, 128 * b:128 * b + 128], ONES[:, 0:1],
                                           start=True, stop=True), done, ones_ready, bank_free[bank],
                   sig=sg("pe_misc") if b == nb - 1 else None)
        a = VEC(lambda e: e.tensor_scalar(v, B[bank][:, 0:nb], 1.0 / n, EPS, ALU.mult, ALU.add), m, sig=sg("dve_row"))
        bank_free[bank] = [a]
        return r, POOL(lambda e: e.tensor_tensor(r, v, half_col([128, nb]), ALU.pow), a, sig=sg("pool_row"))

    def rstd_rows(dst, r, done, bank, dst_free):
        nb = r.shape[1]
        for b in range(nb):
            m = PE(lambda e, b=b: e.matmul(B[bank][:, 128 * b:128 * b + 128], r[:, b:b + 1].to_broadcast([128, 128]),
                                           IDENT[:, :], start=True, stop=True), done, ld_ident, bank_free[bank],
                   sig=sg("pe_misc") if b == nb - 1 else None)
        c = VEC(lambda e: e.tensor_copy(dst, B[bank][:, 0:128 * nb]), m, dst_free, sig=sg("dve_row"))
        bank_free[bank] = [c]
        return c

    def nat_rstd(r, done):
        a = VEC(lambda e: e.tensor_copy(RN[:, :], r), done, sig=sg("dve_rn"))
        return VEC(lambda e: e.tensor_scalar(RN8[:, :], RN[:, :], 0.125, None, ALU.mult), a, sig=sg("dve_rn"))

    r_nat = rstd_tokens(XSUM, D, 5, xs["sum"])
    other_constants()
    kv_mm(7)
    rn = nat_rstd(*r_nat)

    t_ring = [3, 4]
    t_count = [0]

    def t_bank():
        bk = t_ring[t_count[0] % 2]
        t_count[0] += 1
        return bk

    A.q_ready, A.k_ready, A.v_ready = {}, None, None
    A.qraw_free = A.wb_free = A.stk_free = None
    A.qs_free = {}

    def v_evac(banks, vs, r, h0, nh, step, done, waits):
        for bk in sorted({bk for bk, _ in banks}):
            mine = [(b, B[bk][:, off:off + 64 * nh].rearrange("p (h c) -> p h c", c=64))
                    for b, (bank, off) in enumerate(banks) if bank == bk]
            for b, src in mine:
                hi = SCA(lambda e, src=src, b=b: e.activation(vs[:, h0:h0 + nh, b, 0:64], src, ACT.Copy,
                                                              scale=r[:, b:b + 1]), done, waits, sig=sg("act_v"))
            for b, src in mine:
                tok = VEC(lambda e, src=src, b=b: e.scalar_tensor_tensor(
                    vs[:, h0:h0 + nh, b, 64:128], src, r[:, b:b + 1], f32(vs[:, h0:h0 + nh, b, 0:64]),
                    ALU.mult, ALU.subtract), hi, waits, sig=sg("dve_v"))
            bank_free[bk] = [tok]
        return tok

    def rope(kind, banks, done, slot, turn_banks):
        n_a = {"qa": 4, "qb": 0, "k": 2}[kind]
        scale = RN8 if kind == "qb" else RN
        ev = []
        for b in range(4):
            bk, off = banks[b]
            ev.append(SCA(lambda e, bk=bk, off=off, b=b: e.activation(
                QRAW[:, b, :], B[bk][:, off:off + 256], ACT.Copy, scale=scale[:, b:b + 1]),
                done, rn, A.qraw_free, sig=sg("act_q")))
        for b in range(4):
            bank_free[banks[b][0]] = [ev[b]]
        src_t = ev[3]
        yield
        q4 = QRAW[:, :, :].rearrange("p b (h c) -> p b h c", c=64)
        a4 = WA[:, :, :].rearrange("p b (h c) -> p b h c", c=64)
        b4 = WB[:, :, :].rearrange("p b (h c) -> p b h c", c=64)
        if n_a:
            ncol = 4 * n_a
            ssh = SSH[:, 0:ncol].rearrange("p (b h) -> p b h", b=4)
            f16 = FH16[:, 0:ncol].rearrange("p (b h) -> p b h", b=4)
            sq = SCA(lambda e: e.activation(b4[:, :, 0:n_a, :], q4[:, :, 0:n_a, :], ACT.Square), src_t, A.wb_free,
                     sig=sg("act_qsq"))
            yield
            s = VEC(lambda e: e.tensor_reduce(ssh, b4[:, :, 0:n_a, :], AX.X, ALU.add), sq, sig=sg("dve_q"))
            if kind == "qa":
                s = VEC(lambda e: e.tensor_scalar(ssh, ssh, 1.0, 64 * EPS, ALU.mult, ALU.add), s, sig=sg("dve_q"))
            else:
                s = VEC(lambda e: e.tensor_scalar(ssh, ssh, 1.0 / 64, EPS, ALU.mult, ALU.add), s, sig=sg("dve_q"))
            yield
            for c in range(0, ncol, 8):
                f = POOL(lambda e, c=c: e.tensor_tensor(FH16[:, c:c + 8], SSH[:, c:c + 8], half_col([128, 8]), ALU.pow),
                         s, sig=sg("pool_q"))
                yield
            fb = f16.unsqueeze(3).to_broadcast([128, 4, n_a, 64])
            src_t = VEC(lambda e: e.tensor_tensor(q4[:, :, 0:n_a, :], q4[:, :, 0:n_a, :], fb, ALU.mult), f, src_t,
                        sig=sg("dve_q"))
            yield
        parts = {"qa": [(0, 4, TQ1[:, :, :], TQ2[:, :, :])],
                 "qb": [(0, 4, TAB[:, 2, :, :], TAB[:, 3, :, :])],
                 "k": [(0, 2, TAB[:, 0, :, :], TAB[:, 1, :, :]), (2, 2, TAB[:, 2, :, :], TAB[:, 3, :, :])]}[kind]
        ta = []
        for h0, nh, t1, t2 in parts:
            for b0 in (0, 2):
                c1 = t1[:, b0:b0 + 2, :].unsqueeze(2).to_broadcast([128, 2, nh, 64])
                ta.append(POOL(lambda e, h0=h0, nh=nh, c1=c1, b0=b0: e.tensor_tensor(
                    a4[:, b0:b0 + 2, h0:h0 + nh, :], q4[:, b0:b0 + 2, h0:h0 + nh, :], c1, ALU.mult), src_t, A.tables,
                    A.stk_free, sig=sg("pool_q")))
            for s in range(2):
                a, z = 32 * s, 32 * (1 - s)
                c2 = t2[:, :, a:a + 32].unsqueeze(2).to_broadcast([128, 4, nh, 32])
                ta.append(VEC(lambda e, h0=h0, nh=nh, a=a, z=z, c2=c2: e.tensor_tensor(
                    b4[:, :, h0:h0 + nh, a:a + 32], q4[:, :, h0:h0 + nh, z:z + 32], c2, ALU.mult),
                    src_t, A.tables, A.wb_free, sig=sg("dve_q")))
                yield
        A.qraw_free = ta
        yield
        rot = VEC(lambda e: e.tensor_tensor(WA[:, :, :], WA[:, :, :], WB[:, :, :], ALU.add), ta, sig=sg("dve_q"))
        A.wb_free = rot
        yield
        st = STK[:, :, :, :].rearrange("p b h c -> p (b h) c")
        wa = WA[:, :, :].rearrange("p b (h c) -> p (b h) c", c=64)
        if kind != "k":
            par = slot % 8 // 4
            oh, ol = 64 * par, 64 * (1 - par)
            hi = SCA(lambda e: e.activation(st[:, :, oh:oh + 64], wa, ACT.Copy), rot, A.stk_free, sig=sg("act_qh"))
            yield
            lo = VEC(lambda e: e.tensor_tensor(st[:, :, ol:ol + 64], wa, f32(st[:, :, oh:oh + 64]), ALU.subtract),
                     hi, sig=sg("dve_q"))
        else:
            hi = SCA(lambda e: e.activation(st[:, :, 0:64], wa, ACT.Copy), rot, A.stk_free, sig=sg("act_qh"))
            hi2 = SCA(lambda e: e.activation(st[:, :, 64:128], wa, ACT.Copy), sig=sg("act_qh"))
            yield
            lo = VEC(lambda e: e.tensor_tensor(KLN[:, :, :].rearrange("p b (h c) -> p (b h) c", c=64), wa,
                                               f32(st[:, :, 0:64]), ALU.subtract), hi, rot, sig=sg("dve_q"))
            hi = hi2
        yield
        turns = [("s", b) for b in range(4)]
        if kind == "k":
            turns = [(w, b) for b in range(4) for w in ("s", "l")]
        done_t, evac = [], []
        for n, (w, b) in enumerate(turns):
            bk = turn_banks[n % 2]
            nh = 4 if w == "s" else 2
            for h in range(nh):
                src = f32(STK[:, b, h, :]) if w == "s" else f32(KLN[:, b, 128 * h:128 * h + 128])
                tr = transpose(B[bk][:, 128 * h:128 * h + 128], src, lo, hi, bank_free[bk],
                               sig=sg("pe_tq") if h == nh - 1 else None)
            cols = slice(128 * b, 128 * b + 128)
            dst = K2[:, 0:2, cols] if w == "l" else K1[:, 0:4, cols] if kind == "k" else QS[:, slot % 8:slot % 8 + 4, cols]
            qs_free = [A.qs_free.get(slot + i - 8) for i in range(4)] if kind != "k" else None
            yield
            ev = SCA(lambda e, bk=bk, dst=dst, nh=nh: e.activation(
                dst, B[bk][:, 0:128 * nh].rearrange("p (h c) -> p h c", h=nh), ACT.Copy), tr, qs_free, sig=sg("act_qs"))
            bank_free[bk] = [ev]
            done_t.append(ev)
        A.stk_free = tr
        if kind == "k":
            A.k_ready = done_t
        else:
            for i in range(4):
                A.q_ready[slot + i] = done_t

    def nat_proj(banks, hs, res):
        for kh in range(2):
            j, wh, wl, wt = W.take()
            n = wh.shape[2]
            for k in range(4):
                kt = 4 * kh + k
                for b in range(4):
                    bk, off = banks[b]
                    tok = slice(128 * b, 128 * b + 128)
                    t = mm3(B[bk][:, off:off + n], (HH[:, kt, tok], HL[:, kt, tok]), (wh[:, k, :], wl[:, k, :]),
                            kt == 0 and off == 0, kt == 7 and (off > 0 or n > 256), hs[kt], wt, bank_free[bk] if kt == 0 else None,
                            sig=sg("pe_proj") if (k == 3 and b == 3) else None)
                    if b % 2:
                        yield
            W.free[j] = t
        res.append(t)

    PJ = [(6, 0), (6, 256), (7, 0), (7, 256)]

    def q_group(kind, slot, turn_banks=(6, 7)):
        res = []
        yield from nat_proj(PJ, h_ready, res)
        yield from rope(kind, PJ, res[0], slot, turn_banks)

    def drain(gen):
        for _ in gen:
            pass

    KB = [(0, 0), (0, 256), (1, 0), (1, 256)]
    VB = [(2, 0), (2, 256), (3, 0), (3, 256)]
    A.v_ready = v_evac(VB, VS, RN, 0, 4, None, kv_done, rn)
    A.wb_free = A.stk_free = [rn, A.consts, A.tables]
    kgen = rope("k", KB, kv_done, 0, (3, 4))
    next(kgen)
    proj0 = q_group("qa", 0, (3, 4))
    for i in range(17):
        next(proj0)
        if i >= 5:
            next(kgen)
    proj1 = q_group("qa", 4)
    for i in range(17):
        next(proj1)
        if i % 2:
            next(proj0)
        if i > 3:
            next(kgen, None)
    drain(kgen)
    proj4 = q_group("qb", 8)
    proj5 = q_group("qb", 12)
    drain(proj0)

    class Attention:
        def __init__(self, units, P, OTs, vs):
            self.units, self.P, self.OTs, self.vs = units, P, OTs, vs
            self.npair = 0

        def scores(self, i):
            u = self.units[i]
            u.bank = i % 3
            n = u.n
            dst = B[u.bank]
            w = [bank_free[u.bank], u.ready()]
            PE(lambda e: e.matmul(dst[:, 0:n], u.q, u.k1, start=True, stop=False), w)
            last = not u.extra
            u.s = PE(lambda e: e.matmul(dst[:, 0:n], u.qh, u.k2, start=False, stop=last),
                     sig=sg("pe_s") if last else None)
            for n_x, (c0, cn, lhs, rhs, wt) in enumerate(u.extra):
                end = n_x == len(u.extra) - 1
                u.s = PE(lambda e, c0=c0, cn=cn, lhs=lhs, rhs=rhs, end=end: e.matmul(
                    dst[:, c0:c0 + cn], lhs, rhs, start=False, stop=end), wt, sig=sg("pe_s") if end else None)

        def maxes(self, i):
            u = self.units[i]
            c = i % 8
            u.max = VEC(lambda e: e.tensor_reduce(NM[:, c:c + 1], B[u.bank][:, 0:u.width], AX.X, ALU.max, negate=True),
                        u.s, self.units[i - 8].exp if i >= 8 else None, sig=sg("dve_max"))

        def exps(self, i):
            u = self.units[i]
            c = i % 8
            p = self.P[i % 4]
            u.exp = SCA(lambda e: e.activation(p[:, 0:u.width], B[u.bank][:, 0:u.width], ACT.Exp, bias=NM[:, c:c + 1],
                                               scale=1.0, accum_out=DEN[:, c:c + 1]),
                        u.max, self.units[i - 4].t if i >= 4 else u.p_free,
                        self.units[i - 8].rec if i >= 8 else None, sig=sg("act_exp"))
            bank_free[u.bank] = [u.exp]

        def norms(self, i):
            u = self.units[i]
            c = i % 8
            p = self.P[i % 4]
            u.rec = VEC(lambda e: e.reciprocal(RD[:, c:c + 1], DEN[:, c:c + 1]), u.exp,
                        self.units[i - 8].norm if i >= 8 else None, sig=sg("dve_rec"))
            u.norm = POOL(lambda e: e.tensor_scalar(p[:, 0:u.n], p[:, 0:u.n], RD[:, c:c + 1], 1.0, ALU.mult, ALU.mult),
                          u.rec, u.exp, sig=sg("pool_p"))

        def turns(self, i):
            u = self.units[i]
            p = self.P[i % 4]
            bk = t_bank()
            nb = u.n // 128
            for j in range(nb):
                u.t = transpose(B[bk][:, 128 * j:128 * j + 128], p[:, 128 * j:128 * j + 128], u.norm, bank_free[bk],
                                sig=sg("pe_t") if j == nb - 1 else None)
            s = u.pair % 2
            cols = slice(128 * (u.b % 2), 128 * (u.b % 2) + 128)
            u.src = B[bk][:, 0:u.n].rearrange("p (k c) -> p k c", c=128)
            u.t_bank = bk
            u.ph, u.pl = (t[s][:, u.kb:u.kb + nb, cols] for t in (PTH, PTL))
            u.pt_free = self.pv_tok.get(u.pair - 2, u.pt_free)
            u.hi = SCA(lambda e: e.activation(u.ph, u.src, ACT.Copy), u.t, u.pt_free, sig=sg("act_pt"))

        def lows(self, i):
            u = self.units[i]
            u.lo = VEC(lambda e: e.tensor_tensor(u.pl, u.src, f32(u.ph), ALU.subtract), u.hi, u.pt_free, sig=sg("dve_pt"))
            bank_free[u.t_bank] = [u.lo]

        def values(self, i):
            u1 = self.units[i]
            u0 = self.units[i - 1]
            assert u0.pair == u1.pair
            s = u1.pair % 2
            bk = 5
            dst = B[bk]
            kbs = sorted(set(range(u0.kb, u0.kb + u0.n // 128)) | set(range(u1.kb, u1.kb + u1.n // 128)))

            def cols(kb):
                has = [u.kb <= kb < u.kb + u.n // 128 for u in (u0, u1)]
                return (0 if has[0] else 128, 256 if has[1] else 128)

            kbs.sort(key=lambda kb: (cols(kb) != (0, 256), kb))
            assert cols(kbs[0]) == (0, 256)
            seq = [(kb, t) for kb in kbs for t in (PTH[s], PTL[s])]
            for n, (kb, t) in enumerate(seq):
                a, z = cols(kb)
                end = n == len(seq) - 1
                pv = PE(lambda e, kb=kb, t=t, a=a, z=z, n=n, end=end: e.matmul(
                    dst[:, a:z], self.vs[:, u1.v, kb, :], t[:, kb, a:z], start=n == 0, stop=end),
                    u0.lo, u1.lo, bank_free[bk], u1.v_ready, sig=sg("pe_pv") if end else None)
            self.pv_tok[u1.pair] = pv
            ot = self.OTs[u1.pair % 2]
            lowc = SCA(lambda e: e.activation(ot[0:64, :], dst[64:128, 0:256], ACT.Copy), pv,
                       self.ot_free.get(u1.pair - 2, u1.p_free), sig=sg("act_o"))

            def add():
                t = VEC(lambda e: e.tensor_tensor(u1.o, dst[0:64, 0:256], ot[0:64, :], ALU.add), lowc, u1.o_free,
                        sig=sg("dve_o"))
                self.ot_free[u1.pair] = t
                bank_free[bk] = [t]
                u1.done(t)
            self.add = add

        def run(self, fill):
            self.pv_tok, self.ot_free, self.add = {}, {}, None
            W.defer = True
            n = len(self.units)
            self.scores(0)
            self.scores(1)
            for i in range(n + 7):
                if self.add:
                    self.add()
                    self.add = None
                if i < n:
                    self.maxes(i)
                if 0 <= i - 4 < n:
                    self.lows(i - 4)
                if 0 <= i - 3 < n:
                    self.turns(i - 3)
                if i + 2 < n:
                    self.scores(i + 2)
                if i < n:
                    self.exps(i)
                if 1 <= i <= n:
                    self.norms(i - 1)
                k = i - 5
                if 0 <= k < n and k % 2 == 1:
                    self.values(k)
                W.flush()
                fill(i)
            W.defer = False

    class Unit:
        pass

    def filler(gens):
        live = list(gens)

        def go(n):
            while n > 0 and live:
                try:
                    next(live[0])
                    n -= 1
                except StopIteration:
                    live.pop(0)
        return go

    units = []
    o_done = {}
    for h in range(16):
        win = h >= 8
        kv = (h // 4)
        for b in range(4):
            u = Unit()
            u.h, u.b = h, b
            u.pair = 2 * h + b // 2
            s = kv % 2
            k0, k1 = (max(0, b - 1), min(4, b + 2)) if win else (0, 4)
            u.kb, u.n = k0, 128 * (k1 - k0)
            u.width = u.n + 1 if win else u.n
            slot = h % 8
            u.q = QS[:, slot, 128 * b:128 * b + 128]
            u.qh = QS[64 * s:64 * s + 64, slot, 128 * b:128 * b + 128]
            u.k1 = K1[:, kv, 128 * k0:128 * k1]
            u.k2 = K2[64 * s:64 * s + 64, kv // 2, 128 * k0:128 * k1]
            u.ready = lambda h=h: [A.q_ready[h], A.k_ready]
            u.v, u.v_ready = kv, A.v_ready
            u.p_free, u.pt_free, u.o_free = None, None, None
            u.extra = []
            if win:
                if b > 0:
                    u.extra.append((0, 128, IDB[:, :], MLB[:, :], [A.consts]))
                if b < 3:
                    u.extra.append((u.n - 128, 128, IDB[:, :], MRB[:, :], [A.consts]))
                u.extra.append((u.n, 1, ONB[0:65, :], SKB[0:65, h - 8:h - 7], [A.sink_ready, onb_ready]))
            u.o = OR[64 * (h % 2):64 * (h % 2) + 64, h // 2, 256 * (b // 2):256 * (b // 2) + 256]
            u.done = lambda t, h=h: o_done.setdefault(h, []).append(t)
            units.append(u)

    hs_o = [None] * 8

    def group_norm(g, col, bank, h_free):
        src = OR[:, 4 * g:4 * g + 4, :]
        ow = [o_done[8 * g + i] for i in range(8)]
        assert all(len(t) == 2 for t in ow)
        sq = SCA(lambda e: e.activation(SQ4[:, :, :], src, ACT.Square), ow, A.stk_free, A.sq4_free, sig=sg("act_gn"))
        yield
        s = VEC(lambda e: e.tensor_tensor(SQ4[:, 0:2, :], SQ4[:, 0:2, :], SQ4[:, 2:4, :], ALU.add), sq, sig=sg("dve_gn"))
        yield
        s = VEC(lambda e: e.tensor_tensor(RW[0][:, :], SQ4[:, 0, :], SQ4[:, 1, :], ALU.add), s, A.rw_free, sig=sg("dve_gn"))
        A.sq4_free = s
        yield
        r, p = rstd_tokens(RW[0][:, :], 512, bank, s)
        yield
        p = rstd_rows(RW[1][:, :], r, p, bank, A.rw_free)
        yield
        for i in range(4):
            t = 4 * g + i
            n = VEC(lambda e, t=t: e.tensor_tensor(OR[:, t, :], OR[:, t, :], RW[1][:, :], ALU.mult), p, sig=sg("dve_gn"))
            hi = SCA(lambda e, t=t, i=i: e.activation(HH[:, t, :], OR[:, t, :], ACT.Copy, scale=gcol(col, i)), n, h_free,
                     sig=sg("act_gn"))
            hs_o[t] = VEC(lambda e, t=t, i=i: e.scalar_tensor_tensor(HL[:, t, :], OR[:, t, :], gcol(col, i),
                                                                     f32(HH[:, t, :]), ALU.mult, ALU.subtract),
                          hi, h_free, n, sig=sg("dve_gn"))
            yield
        A.rw_free = n

    A.sq4_free = A.rw_free = None

    def late_a():
        A.h_free = (signals["pe_proj"], signals["pe_proj"].value)
        yield from group_norm(0, G_A, 6, A.h_free)

    def spread(plan):
        given = [0] * len(plan)

        def go(i):
            for p, (gen, s0, s1, n) in enumerate(plan):
                if s0 <= i < s1:
                    want = -(-n * (i + 1 - s0) // (s1 - s0))
                    while given[p] < want:
                        given[p] += 1
                        next(gen, None)
                if i == s1 - 1:
                    drain(gen)
        return go

    att = Attention(units, PR, OT, VS)
    for i, u in enumerate(units):
        if u.b == 3:
            def done_q(i=i):
                A.qs_free[units[i].h] = units[i].s
            u.q_done = done_q
        else:
            u.q_done = None
    scores0 = att.scores

    def scores_and_release(i):
        scores0(i)
        if units[i].q_done:
            units[i].q_done()
    att.scores = scores_and_release
    att.run(spread([(proj1, 0, 9, 11), (proj4, 9, 28, 25), (proj5, 28, 46, 25), (late_a(), 46, 56, 10)]))
    p_end = units[-1].t
    pv_end = att.pv_tok[units[-1].pair]

    def tr_mm(dst, chunk, k, m, h, kt, cols, start, stop, *waits, sig=None):
        j, wh, wl, wt = chunk
        hh, hl = h
        return mm3(dst, (wh[:, k, 128 * m:128 * m + 128], wl[:, k, 128 * m:128 * m + 128]),
                   (hh[:, kt, cols], hl[:, kt, cols]), start, stop, wt, *waits, sig=sig)

    ALLC = slice(0, 512)
    HALVES = [slice(0, 256), slice(256, 512)]

    class PostNorm:

        def __init__(self, mix, g_post, g_next, mix_free, work_free, rp_bank, r_bank, nat, h_free):
            self.mix, self.gp, self.gn = mix, g_post, g_next
            self.mix_free, self.work_free = mix_free, work_free
            self.rp_bank, self.r_bank, self.nat, self.h_free = rp_bank, r_bank, nat, h_free
            self.nsq, self.sum_tok = [work_free, work_free], [None, None]
            self.count = 0
            self.mix_tok = {}
            self.h = [[None, None] for _ in range(8)]
            self.u_tok = [work_free, work_free]
            self.first = True
            self.sums2 = [None, None]

        def full(self, m, bank, done):
            c = SCA(lambda e: e.activation(self.mix[:, m, :], B[bank][:, :], ACT.Copy), done, self.mix_free,
                    sig=sg("act_mix"))
            bank_free[bank] = [c]
            self.mix_tok[m] = [c, c]
            i = self.count % 2
            self.count += 1
            if self.first:
                t = SCA(lambda e: e.activation(NSUM[:, :], self.mix[:, m, :], ACT.Square), c, self.work_free,
                        sig=sg("act_msq"))
                self.sum_tok = [t, t]
                self.first = False
                return
            q = SCA(lambda e: e.activation(NSQ[i][:, :], self.mix[:, m, :], ACT.Square), c, self.nsq[i],
                    sig=sg("act_msq"))
            t = VEC(lambda e: e.tensor_tensor(NSUM[:, :], NSUM[:, :], NSQ[i][:, :], ALU.add), q, self.sum_tok,
                    sig=sg("dve_msum"))
            self.nsq[i] = t
            self.sum_tok = [t, t]

        def half(self, hf, bank, done):
            cols = HALVES[hf]
            i = self.count % 2
            self.count += 1
            q = SCA(lambda e: e.activation(NSQ[i][:, :], B[bank][:, :], ACT.Square), done, self.nsq[i], sig=sg("act_msq"))
            t = VEC(lambda e: e.tensor_tensor(NSUM[:, cols], NSUM[:, cols], NSQ[i][:, 0:256], ALU.add), q,
                    self.sum_tok[hf], sig=sg("dve_msum"))
            t = VEC(lambda e: e.tensor_tensor(NSUM[:, cols], NSUM[:, cols], NSQ[i][:, 256:512], ALU.add), t,
                    sig=sg("dve_msum"))
            self.nsq[i] = t
            self.sum_tok[hf] = t
            c = SCA(lambda e: e.activation(self.mix[:, 6:8, cols], B[bank][:, :].rearrange("p (m c) -> p m c", m=2),
                                           ACT.Copy), q, sig=sg("act_mix"))
            bank_free[bank] = [c]
            for m in (6, 7):
                self.mix_tok.setdefault(m, [None, None])[hf] = c
            rb = self.rp_bank[hf]
            yield
            r, p = rstd_tokens(NSUM[:, cols], D, rb, t)
            yield
            p = rstd_rows(NRP[:, cols], r, p, rb, self.work_free)
            yield
            pend = None
            sums = None
            for kt in range(8):
                n = kt % 2
                u = VEC(lambda e, kt=kt, n=n: e.scalar_tensor_tensor(
                    NU[n][:, :], self.mix[:, kt, cols], gcol(self.gp, kt), NRP[:, cols], ALU.mult, ALU.mult),
                    p, self.mix_tok[kt][hf], self.u_tok[n], sig=sg("dve_x"))
                xx = VEC(lambda e, kt=kt, n=n: e.tensor_tensor(XT[:, kt, cols], XT[:, kt, cols], NU[n][:, :], ALU.add),
                         u, sig=sg("dve_x"))
                self.u_tok[n] = xx
                if pend:
                    pend()
                hi = SCA(lambda e, kt=kt: e.activation(HH[:, kt, cols], XT[:, kt, cols], ACT.Copy,
                                                       scale=gcol(self.gn, kt)), xx, self.h_free[hf], sig=sg("act_h"))

                def lo(kt=kt, hi=hi, xx=xx):
                    self.h[kt][hf] = VEC(lambda e: e.scalar_tensor_tensor(
                        HL[:, kt, cols], XT[:, kt, cols], gcol(self.gn, kt), f32(HH[:, kt, cols]), ALU.mult,
                        ALU.subtract), hi, xx, self.h_free[hf], sig=sg("dve_h"))
                pend = lo
                if kt == 0:
                    sums = SCA(lambda e: e.activation(NSUM2[:, cols], XT[:, 0, cols], ACT.Square), xx, self.work_free,
                               sig=sg("act_xsq"))
                else:
                    z = kt % 2
                    q = SCA(lambda e, kt=kt, z=z: e.activation(NSQ[z][:, 0:256], XT[:, kt, cols], ACT.Square), xx,
                            self.nsq[z], sig=sg("act_xsq"))
                    sums = POOL(lambda e, z=z: e.tensor_tensor(NSUM2[:, cols], NSUM2[:, cols], NSQ[z][:, 0:256], ALU.add),
                                q, sums, sig=sg("pool_xsum"))
                    self.nsq[z] = sums
                self.sums2[hf] = sums
                yield
            pend()
            yield

    def barrier(pn, groups, src, ready, banks, fresh, take_next, mm_next):
        last = {}

        def tail(hf):
            tot, n = sum(nk for _, _, nk in groups), 0
            for ch, k0, nk in groups:
                for k in range(nk):
                    for m in range(2):
                        t = tr_mm(B[banks[hf]][:, 256 * m:256 * m + 256], ch, k, m, src, k0 + k, HALVES[hf],
                                  fresh and n == 0 and m == 0, n == tot - 1 and m == 1, ready[k0 + k],
                                  bank_free[banks[hf]] if n == 0 and fresh else None,
                                  sig=sg("pe_tail") if (k == nk - 1 and m == 1) else None)
                    n += 1
                    if k == nk - 1 and hf == 1:
                        W.free[ch[0]] = t
                    last[hf] = t
                    yield
            pn.h_free[hf] = t

        drain(tail(0))
        c0 = pn.half(0, banks[0], last[0])
        next(c0)
        for i, _ in enumerate(tail(1)):
            if i in (1, 5):
                W.ahead(W.next + 2)
            if i in (3, 6):
                next(c0)
        c1 = pn.half(1, banks[1], last[1])
        next(c0)
        next(c0)
        pairs = [take_next(VEC), None]
        next(c1)
        for kt in range(8):
            while pn.h[kt][0] is None:
                next(c0)
            if kt == 1:
                pairs[1] = take_next(POOL)
            if kt in (3, 5):
                next(c1)
            mm_next(0, kt, pairs[kt // 4])
        for kt in range(8):
            while pn.h[kt][1] is None:
                next(c1)
            mm_next(1, kt, pairs[kt // 4])

    def take2(queue):
        W.lo_queue = queue
        r = [W.take(0), W.take(0)]
        W.lo_queue = VEC
        return r

    OH = (HH, HL)
    mpb = {0: (6, 7), 1: (0, 1), 2: (2, 3)}
    gb = group_norm(1, G_B, 4, A.h_free)
    drain(gb)
    bank_w = {}
    for kh in range(2):
        for mp in range(3):
            ch = W.take()
            for k in range(4):
                kt = 4 * kh + k
                for m in range(2):
                    bk = mpb[mp][m]
                    t = tr_mm(B[bk][:, :], ch, k, m, OH, kt, ALLC, kt == 0, kt == 7, hs_o[kt],
                              bank_free[bk] if kt == 0 else None, sig=sg("pe_wo") if k == 3 else None)
            W.free[ch[0]] = t
            bank_w[mp] = t
    wo_b = None
    post1 = PostNorm(MIX1, G_POST, G_FPRE, [pv_end], [signals["dve_gn"].value and (signals["dve_gn"], signals["dve_gn"].value),
                     A.stk_free], (6, 7), None, False, [None, None])

    for mp in range(3):
        for m in range(2):
            post1.full(2 * mp + m, mpb[mp][m], bank_w[mp])
    ch_a, ch_b = W.take(), W.take(0)
    pair0 = {}

    def ffn_half(hf, kt, chs):
        for c in range(2):
            bk = 2 * hf + c
            for m in range(2):
                t = tr_mm(B[bk][:, 256 * m:256 * m + 256], chs[c], kt % 4, m, OH, kt, HALVES[hf], kt == 0 and m == 0,
                          kt == 7 and m == 1, post1.h[kt][hf], bank_free[bk] if kt == 0 else None,
                          sig=sg("pe_ff") if (kt % 4 == 3 and m == 1) else None)
            if hf == 1 and kt % 4 == 3:
                W.free[chs[c][0]] = t
        pair0[hf] = t

    barrier(post1, [(ch_a, 0, 4), (ch_b, 4, 4)], OH, hs_o, (4, 5), True, take2, ffn_half)

    def glu(fi, n, cols, pg, pu, r, done, free, it):
        ts, tu = TS[it % 2], TU[it % 2]
        width = cols.stop - cols.start
        view = (lambda t: t[:, :].rearrange("p (m c) -> p m c", m=n)) if n > 1 else (lambda t: t[:, :])
        rv = r[:, cols].unsqueeze(1).to_broadcast([128, n, width]) if n > 1 else r[:, cols]
        hv = FFH[:, fi:fi + n, cols] if n > 1 else FFH[:, fi, cols]
        lv = FFL[:, fi:fi + n, cols] if n > 1 else FFL[:, fi, cols]
        t = VEC(lambda e: e.tensor_tensor(view(ts), view(pg), rv, ALU.mult), done, free, F.ts_free[it % 2], sig=sg("dve_ff"))
        u = VEC(lambda e: e.tensor_tensor(view(tu), view(pu), rv, ALU.mult), F.tu_free[it % 2], sig=sg("dve_ff"))
        s = SCA(lambda e: e.activation(ts[:, :], ts[:, :], ACT.Silu), t, sig=sg("act_ff"))
        f = VEC(lambda e: e.tensor_tensor(tu[:, :], ts[:, :], tu[:, :], ALU.mult), s, u, sig=sg("dve_ff"))
        F.ts_free[it % 2] = f
        hi = SCA(lambda e: e.activation(hv, view(tu), ACT.Copy), f, free, sig=sg("act_ff"))
        lo = VEC(lambda e: e.tensor_tensor(lv, view(tu), f32(hv), ALU.subtract), hi, f, sig=sg("dve_ff"))
        F.tu_free[it % 2] = lo
        return t, u, lo

    F = Bag()

    def ffn_pair(p, h_tok, bset, between):
        for gu in range(2):
            for kh in range(2):
                ch = W.take()
                for k in range(4):
                    kt = 4 * kh + k
                    for m in range(2):
                        bk = bset[2 * gu + m]
                        t = tr_mm(B[bk][:, :], ch, k, m, (HH, HL), kt, ALLC, kt == 0, kt == 7, h_tok(kt),
                                  bank_free[bk] if kt == 0 else None, sig=sg("pe_ff") if (k == 3 and m == 1) else None)
                W.free[ch[0]] = t
                between(2 * gu + kh)
        return t

    def ffn(h_tok, sums, first, f_free, sets):
        F.ts_free, F.tu_free = [f_free, f_free], [f_free, f_free]
        f_ready = [None] * NF
        it = 0
        st = {}

        def between1(i):
            if i == 0:
                st["r"] = rstd_tokens(NSUM2[:, :], D, sets[1][3], sums())
            if i == 1:
                st["r2"] = rstd_rows(R2[:, :], *st["r"], sets[1][3], None)
                first(f_ready, st["r2"])

        for p in range(1, NF // 2):
            bset = sets[p % 2]
            t = ffn_pair(p, h_tok, bset, between1 if p == 1 else lambda i: None)
            for m in range(2):
                a, b_, lo = glu(2 * p + m, 1, ALLC, B[bset[m]], B[bset[2 + m]], R2, [t, st["r2"]], f_free, m)
                bank_free[bset[m]], bank_free[bset[2 + m]] = [a], [b_]
                f_ready[2 * p + m] = lo
        return f_ready, t, st["r"][0]

    mix1_read = [(signals["dve_x"], signals["dve_x"].value), (signals["act_mix"], signals["act_mix"].value)]
    f_free1 = mix1_read + [p_end]

    def first1(f_ready, r2):
        for hf in range(2):
            bg, bu = 2 * hf, 2 * hf + 1
            a, b_, lo = glu(0, 2, HALVES[hf], B[bg], B[bu], R2, [pair0[0], pair0[1], r2], f_free1, hf)
            bank_free[bg], bank_free[bu] = [a], [b_]
            f_ready[0] = f_ready[1] = lo

    f_ready, ff_end, _ = ffn(lambda kt: post1.h[kt], lambda: post1.sums2, first1, f_free1, [(0, 1, 2, 3), (4, 5, 6, 7)])

    FS = (FFH, FFL)
    nsum_free = [(signals["pool_xsum"], signals["pool_xsum"].value), (signals["pe_misc"], signals["pe_misc"].value),
                 (signals["dve_row"], signals["dve_row"].value), (signals["pool_row"], signals["pool_row"].value),
                 (signals["dve_x"], signals["dve_x"].value), (signals["dve_ff"], signals["dve_ff"].value)]
    post2 = PostNorm(MIX2, G_FPOST, G_N1, [ff_end], nsum_free, (0, 1), None, True, [ff_end, ff_end])
    dpb = {0: (4, 5), 1: (6, 7), 2: (0, 1)}
    for mp in range(3):
        for k0, nk in KD:
            ch = W.take()
            for k in range(nk):
                kt = k0 + k
                for m in range(2):
                    bk = dpb[mp][m]
                    t = tr_mm(B[bk][:, :], ch, k, m, FS, kt, ALLC, kt == 0, kt == NF - 1, f_ready[kt],
                              bank_free[bk] if kt == 0 else None, sig=sg("pe_dn") if k == nk - 1 else None)
            W.free[ch[0]] = t
        for m in range(2):
            post2.full(2 * mp + m, dpb[mp][m], t)
    for k0, nk in KD[:3]:
        ch = W.take()
        for k in range(nk):
            kt = k0 + k
            for hf in range(2):
                for m in range(2):
                    bk = 2 + hf
                    t = tr_mm(B[bk][:, 256 * m:256 * m + 256], ch, k, m, FS, kt, HALVES[hf], kt == 0 and m == 0, False,
                              f_ready[kt], bank_free[bk] if kt == 0 else None,
                              sig=sg("pe_dn") if (k == nk - 1 and m == 1) else None)
        W.free[ch[0]] = t
    tail_ch = [(W.take(2 if i == 0 else 0), k0, nk) for i, (k0, nk) in enumerate(KD[3:])]
    qk_t = {}

    def qk_half(hf, kt, chs):
        for which in range(2):
            j, wh, wl, wt = chs[which]
            bk = (4 + which) if hf == 0 else (6 + which)
            for bb in range(2):
                b = 2 * hf + bb
                tok = slice(128 * b, 128 * b + 128)
                t = mm3(B[bk][:, 256 * bb:256 * bb + 256], (HH[:, kt, tok], HL[:, kt, tok]),
                        (wh[:, kt % 4, :], wl[:, kt % 4, :]), kt == 0 and bb == 0, kt == 7 and bb == 1, wt,
                        post2.h[kt][hf], bank_free[bk] if kt == 0 else None,
                        sig=sg("pe_proj") if (kt % 4 == 3 and bb == 1) else None)
            if hf == 1 and kt % 4 == 3:
                W.free[j] = t
            qk_t[hf, which] = t

    barrier(post2, tail_ch, FS, f_ready, (2, 3), False, take2, qk_half)
    f_end = post2.h_free[1]

    r_nat, r_tok = rstd_tokens(NSUM2[:, :], D, 2, post2.sums2)
    rn2 = nat_rstd(r_nat, [r_tok, rn])
    r2 = rstd_rows(R2[:, :], r_nat, r_tok, 3, None)
    chain_end = [r2, (signals["dve_x"], signals["dve_x"].value), (signals["dve_h"], signals["dve_h"].value)]

    A2 = Bag()
    A2.q_ready, A2.k_ready, A2.v_ready = {}, {}, {}
    A2.stk_free = chain_end
    A2.kln_free = chain_end

    def stack2(plan, lo, turn_banks, ready):
        evs = []
        for n, (srcs, dst) in enumerate(plan):
            bk = turn_banks[n % 2]
            for h, src in enumerate(srcs):
                tr = transpose(B[bk][:, 128 * h:128 * h + 128], src, lo, bank_free[bk],
                               sig=sg("pe_tq") if h == len(srcs) - 1 else None)
            yield
            ev = SCA(lambda e, bk=bk, dst=dst, nh=len(srcs): e.activation(
                dst, B[bk][:, 0:128 * nh].rearrange("p (h c) -> p h c", h=nh), ACT.Copy), tr, f_end, sig=sg("act_qs"))
            bank_free[bk] = [ev]
            evs.append(ev)
        A2.stk_free = tr
        ready(evs)

    def q2_evac(banks, done, h0, turn_banks):
        st = STK2[:, :, :, :].rearrange("p b (h s) c -> p b h s c", s=2)
        for bk in sorted({bk for bk, _ in banks}):
            mine = [(b, s, B[bk][:, off:off + 256].rearrange("p (h s c) -> p h s c", s=2, c=64)[:, :, s, :])
                    for b, (bank, off) in enumerate(banks) if bank == bk for s in range(2)]
            for b, s, src in mine:
                hi = SCA(lambda e, b=b, s=s, src=src: e.activation(
                    st[:, b, :, s, 64 * s:64 * s + 64], src, ACT.Copy, scale=RN8[:, b:b + 1]),
                    done, rn2, A2.stk_free, sig=sg("act_q"))
            yield
            for b, s, src in mine:
                lo = VEC(lambda e, b=b, s=s, src=src: e.scalar_tensor_tensor(
                    st[:, b, :, s, 64 - 64 * s:128 - 64 * s], src, RN8[:, b:b + 1],
                    f32(st[:, b, :, s, 64 * s:64 * s + 64]), ALU.mult, ALU.subtract), hi, A2.stk_free, rn2,
                    sig=sg("dve_q"))
            bank_free[bk] = [lo]
            yield
        def ready(evs):
            for h in range(4):
                A2.q_ready[h0 + h] = evs
        yield from stack2([([f32(STK2[:, b, h, :]) for h in range(4)], QS2[:, h0:h0 + 4, 128 * b:128 * b + 128])
                           for b in range(4)], lo, turn_banks, ready)

    def k2_evac(banks, done, h0, turn_banks):
        for bk in sorted({bk for bk, _ in banks}):
            mine = [(b, B[bk][:, off:off + 256].rearrange("p (h c) -> p h c", c=64))
                    for b, (bank, off) in enumerate(banks) if bank == bk]
            for b, src in mine:
                for s in range(2):
                    hi = SCA(lambda e, b=b, s=s, src=src: e.activation(
                        STK2[:, b, :, 64 * s:64 * s + 64], src, ACT.Copy, scale=RN[:, b:b + 1]),
                        done, rn2, A2.stk_free, sig=sg("act_q"))
            yield
            for b, src in mine:
                lo = VEC(lambda e, b=b, src=src: e.scalar_tensor_tensor(
                    KLN2[:, b, :].rearrange("p (h c) -> p h c", c=64), src, RN[:, b:b + 1], f32(STK2[:, b, :, 0:64]),
                    ALU.mult, ALU.subtract), hi, A2.kln_free, rn2, sig=sg("dve_q"))
            bank_free[bk] = [lo]
            yield
        def ready(evs):
            A2.kln_free = A2.stk_free
            for h in range(4):
                A2.k_ready[h0 + h] = evs
        plan = []
        for b in range(4):
            cols = slice(128 * b, 128 * b + 128)
            plan.append(([f32(STK2[:, b, h, :]) for h in range(4)], K1B[:, h0:h0 + 4, cols]))
            plan.append(([f32(KLN2[:, b, 128 * h:128 * h + 128]) for h in range(2)], K2B[:, h0 // 2:h0 // 2 + 2, cols]))
        yield from stack2(plan, lo, turn_banks, ready)

    h2r = post2.h
    QB0 = [(4, 0), (4, 256), (6, 0), (6, 256)]
    KB0 = [(5, 0), (5, 256), (7, 0), (7, 256)]
    gq = q2_evac(QB0, [qk_t[0, 0], qk_t[1, 0]], 0, (3, 2))
    gk = k2_evac(KB0, [qk_t[0, 1], qk_t[1, 1]], 0, (3, 2))
    VA = [(0, 0), (0, 256), (1, 0), (1, 256)]
    VBK = [(4, 0), (5, 0), (6, 0), (7, 0)]
    res = []
    pv_gen = nat_proj(VA, h2r, res)
    both = filler([gq, gk])
    for _ in range(4):
        both(1)
    for _ in pv_gen:
        both(2)
    both(100)
    A2.v_ready[0] = v_evac(VA, VSB, RN, 0, 4, None, res, [rn2, f_end])
    res = []
    drain(nat_proj(VBK, h2r, res))
    A2.v_ready[1] = v_evac(VBK, VSB, RN, 4, 4, None, res, [rn2, f_end])

    fl = None
    for b in range(4):
        bk = VBK[b][0]
        fl = VEC(lambda e, b=b, bk=bk: e.scalar_tensor_tensor(FLG[:, b, :], B[bk][:, 256:264], RN[:, b:b + 1], BF[:, :],
                                                             ALU.mult, ALU.add), ld_bf, res, rn2, A2.v_ready[1],
                 sig=sg("dve_f"))
        bank_free[bk] = [fl]

    def v(fn, *w):
        return VEC(fn, *w, sig=sg("dve_f"))

    t1 = v(lambda e: e.scalar_tensor_tensor(FL1[:, :, :], FLG[:, :, :], -1.0, FLG[:, :, :], ALU.mult, ALU.max), fl)
    ex = SCA(lambda e: e.activation(FL1[:, :, :], FL1[:, :, :], ACT.Exp, scale=-1.0), t1, sig=sg("act_f"))
    w1 = v(lambda e: e.tensor_scalar(FL2[:, :, :], FL1[:, :, :], 1.0, None, ALU.add), ex)
    ln = SCA(lambda e: e.activation(FL3[:, :, :], FL2[:, :, :], ACT.Ln), w1, sig=sg("act_f"))
    d1 = v(lambda e: e.scalar_tensor_tensor(FL1[:, :, :], FL2[:, :, :], -1.0, FL1[:, :, :], ALU.add, ALU.subtract), w1)
    rc = v(lambda e: e.reciprocal(FL2[:, :, :], FL2[:, :, :]), d1, ln)
    d2 = v(lambda e: e.tensor_tensor(FL1[:, :, :], FL1[:, :, :], FL2[:, :, :], ALU.mult), rc)
    l1 = v(lambda e: e.tensor_tensor(FL3[:, :, :], FL3[:, :, :], FL1[:, :, :], ALU.subtract), d2, ln)
    lf = v(lambda e: e.scalar_tensor_tensor(FLG[:, :, :], FLG[:, :, :], 0.0, FL3[:, :, :], ALU.min, ALU.subtract), l1)
    for b in range(4):
        for a in range(b + 1):
            cs = PE(lambda e, a=a, b=b: e.matmul(B[0][:, 8 * b:8 * b + 8], (UPPER if a == b else ONES)[:, :],
                                                 FLG[:, a, :], start=a == 0, stop=a == b), lf, A.consts, bank_free[0],
                    sig=sg("pe_misc") if a == b else None)
    cps = B[0][:, 0:32].rearrange("p (b h) -> p b h", b=4)
    ch_ = v(lambda e: e.tensor_scalar(CN[:, :, 0:8], cps, -1.0, None, ALU.mult), cs)
    cl_ = v(lambda e: e.scalar_tensor_tensor(CN[:, :, 8:16], cps, -1.0, f32(CN[:, :, 0:8]), ALU.mult, ALU.subtract), ch_)
    for b in range(4):
        ctt = transpose(B[0][0:16, 128 * b:128 * b + 128], f32(CN[:, b, :]), cl_, sig=sg("pe_misc"))
    ct = SCA(lambda e: e.activation(CT[:, :], B[0][0:16, :], ACT.Copy), ctt, f_end, sig=sg("act_f"))
    bank_free[0] = [ct]

    def qk1():
        res = []
        yield from nat_proj(PJ, h2r, res)
        yield from q2_evac(PJ, res, 4, (6, 7))
        res = []
        yield from nat_proj(PJ, h2r, res)
        yield from k2_evac(PJ, res, 4, (6, 7))

    o2_done = {}
    units2 = []
    for h in range(8):
        for b in range(4):
            u = Unit()
            u.h, u.b, u.pair = h, b, 2 * h + b // 2
            s = h % 2
            u.kb, u.n = 0, 128 * (b + 1)
            u.width = u.n
            u.q = QS2[:, h, 128 * b:128 * b + 128]
            u.qh = QS2[64 * s:64 * s + 64, h, 128 * b:128 * b + 128]
            u.k1 = K1B[:, h, 0:u.n]
            u.k2 = K2B[64 * s:64 * s + 64, h // 2, 0:u.n]
            u.ready = lambda h=h: [A2.q_ready[h], A2.k_ready[h], ct]
            u.v, u.v_ready = h, A2.v_ready[h // 4]
            u.p_free, u.pt_free, u.o_free = [f_end], [f_end], [f_end]
            u.extra = [(0, u.n, SEL[0:16, h:h + 1].to_broadcast([16, 128]), CT[0:16, 0:u.n], [ct]),
                       (128 * b, 128, IDB[:, :], MRB[:, :], None)]
            u.o = ORB[64 * s:64 * s + 64, h // 2, 256 * (b // 2):256 * (b // 2) + 256]
            u.done = lambda t, h=h: o2_done.setdefault(h, []).append(t)
            units2.append(u)

    att2 = Attention(units2, PRB, OTB, VSB)
    mix_ready = [None] * 8

    def o_split(i):
        src = ORB[:, i, :]
        assert len(o2_done[2 * i]) == len(o2_done[2 * i + 1]) == 2
        w = [o2_done[2 * i], o2_done[2 * i + 1], A2.stk_free, A2.kln_free]
        if i == 3:
            w.append(units2[-1].t)
        hi = SCA(lambda e: e.activation(AH[i][:, :], src, ACT.Copy), w, sig=sg("act_os"))
        mix_ready[i] = VEC(lambda e: e.tensor_tensor(AL[i][:, :], src, f32(AH[i][:, :]), ALU.subtract), hi, w,
                           sig=sg("dve_os"))

    def pool_path():
        ur = []
        g0 = units2[15]
        dead = [g0.s, att2.pv_tok[g0.pair]]
        for c in range(2):
            for kh in range(2):
                ch = W.take()
                for k in range(4):
                    kt = 4 * kh + k
                    for m in range(2):
                        bk = 6 + m
                        t = tr_mm(B[bk][:, :], ch, k, m, (HH, HL), kt, ALLC, kt == 0, kt == 7, h2r[kt],
                                  bank_free[bk] if kt == 0 else None, sig=sg("pe_u") if k == 3 else None)
                        yield
                W.free[ch[0]] = t
            for m in range(2):
                g = 2 * c + m
                ev = VEC(lambda e, g=g, m=m: e.tensor_tensor(UR[:, g, :], B[6 + m][:, :], R2[:, :], ALU.mult), t, r2, dead,
                         sig=sg("dve_u"))
                bank_free[6 + m] = [ev]
                ur.append(ev)
                yield
        ch = W.take()
        j, wh, wl, wt = ch
        ps_free, pd_free = [dead, dead], [dead]
        for g in range(4):
            src, last = UR[:, g, :], ur[g]
            cur_t = src
            n = 0
            for lvl in range(g + 1):
                sh = 1 << lvl
                dst = (PS1, PS2)[lvl % 2]
                cp = VEC(lambda e, dst=dst, cur_t=cur_t, sh=sh: e.tensor_copy(dst[:, 0:sh], cur_t[:, 0:sh]), last,
                         ps_free, sig=sg("dve_u"))
                last = VEC(lambda e, dst=dst, cur_t=cur_t, sh=sh: e.tensor_tensor(
                    dst[:, sh:512], cur_t[:, sh:512], cur_t[:, 0:512 - sh], ALU.add), last, ps_free, sig=sg("dve_u"))
                cur_t = dst[:, :]
                yield
            other = (PS1, PS2)[(g + 1) % 2]
            w = 1 << (g + 1)
            a = VEC(lambda e, cur_t=cur_t, other=other, g=g: e.tensor_tensor(
                other[:, 0:16], cur_t[:, 0:16], ICNT[:, g, :], ALU.mult), last, sig=sg("dve_u"))
            a = VEC(lambda e, other=other, src=src: e.tensor_tensor(other[:, 0:16], other[:, 0:16], src[:, 0:16],
                                                                   ALU.subtract), a, sig=sg("dve_u"))
            a2 = VEC(lambda e, cur_t=cur_t, other=other, src=src, w=w: e.scalar_tensor_tensor(
                other[:, 16:512], cur_t[:, 16:512], 1.0 / w, src[:, 16:512], ALU.mult, ALU.subtract), last, a,
                sig=sg("dve_u"))
            yield
            hi = SCA(lambda e, other=other: e.activation(PDH[:, :], other[:, :], ACT.Copy), a2, pd_free, sig=sg("act_u"))
            lo = VEC(lambda e, other=other: e.tensor_tensor(PDL[:, :], other[:, :], f32(PDH[:, :]), ALU.subtract), hi,
                     pd_free, sig=sg("dve_u"))
            ps_free = [lo]
            bk = 6 + g % 2
            yield
            t = mm3(B[bk][:, :], (wh[:, g, :], wl[:, g, :]), (PDH[:, :], PDL[:, :]), True, True, wt, lo, bank_free[bk],
                    sig=sg("pe_u"))
            pd_free = [t]
            yield
            pw = [dead] if g < 3 else [mix_ready[0], mix_ready[1]]
            hi = SCA(lambda e, g=g, bk=bk: e.activation(PLH[g][:, :], B[bk][:, :], ACT.Copy, scale=gcol(G_PS, g)), t, pw,
                     sig=sg("act_u"))
            mix_ready[4 + g] = VEC(lambda e, g=g, bk=bk: e.scalar_tensor_tensor(
                PLL[g][:, :], B[bk][:, :], gcol(G_PS, g), f32(PLH[g][:, :]), ALU.mult, ALU.subtract), hi, pw,
                sig=sg("dve_u"))
            bank_free[bk] = [mix_ready[4 + g]]
            yield
        W.free[j] = t

    fill_a = filler([qk1()])
    state = {"b": None}

    def fill2(i):
        if i < 15:
            fill_a(4)
        elif i == 15:
            fill_a(1000)
        if i == 22:
            o_split(0)
            o_split(1)
            state["b"] = filler([pool_path()])
        if i == 30:
            o_split(2)
        if i >= 22:
            state["b"](5)
    att2.run(fill2)
    state["b"](1000)
    o_split(3)

    mh = [AH[i] for i in range(4)] + [PLH[i] for i in range(4)]
    ml = [AL[i] for i in range(4)] + [PLL[i] for i in range(4)]
    mpb2 = {0: (6, 7), 1: (0, 1), 2: (2, 3), 3: (4, 5)}
    h3 = [None] * 8
    x3 = [None] * 8
    s3 = [None]
    nsq_free = [chain_end, chain_end]

    def wo2(mp, kh, first):
        ch = W.take()
        j, wh, wl, wt = ch
        for k in range(4):
            kt = 4 * kh + k
            for m in range(2):
                bk = mpb2[mp][m]
                t = mm3(B[bk][:, :], (wh[:, k, 128 * m:128 * m + 128], wl[:, k, 128 * m:128 * m + 128]),
                        (mh[kt][:, :], ml[kt][:, :]), first and k == 0, (not first) and k == 3, wt, mix_ready[kt],
                        bank_free[bk] if first and k == 0 else None, sig=sg("pe_wo") if k == 3 else None)
        W.free[j] = t
        return t

    def res2(m, bank, done):
        x3[m] = VEC(lambda e: e.tensor_tensor(XT[:, m, :], B[bank][:, :], XT[:, m, :], ALU.add), done, sig=sg("dve_x3"))
        bank_free[bank] = [x3[m]]
        hi = SCA(lambda e: e.activation(HH[:, m, :], XT[:, m, :], ACT.Copy, scale=gcol(G_N2, m)), x3[m], sig=sg("act_h"))
        h3[m] = VEC(lambda e: e.scalar_tensor_tensor(HL[:, m, :], XT[:, m, :], gcol(G_N2, m), f32(HH[:, m, :]),
                                                     ALU.mult, ALU.subtract), hi, x3[m], sig=sg("dve_h"))
        if m == 0:
            s3[0] = SCA(lambda e: e.activation(NSUM2[:, :], XT[:, 0, :], ACT.Square), x3[0], ur_done, sig=sg("act_xsq"))
        else:
            i = m % 2
            q = SCA(lambda e: e.activation(NSQ[i][:, :], XT[:, m, :], ACT.Square), x3[m], nsq_free[i], a_free,
                    sig=sg("act_xsq"))
            s3[0] = POOL(lambda e: e.tensor_tensor(NSUM2[:, :], NSUM2[:, :], NSQ[i][:, :], ALU.add), q, s3[0],
                         sig=sg("pool_xsum"))
            nsq_free[i] = s3[0]

    ur_done = [(signals["dve_u"], signals["dve_u"].value)]
    a_free = []
    for mp in range(3):
        wo2(mp, 1, True)
    done_mp = [wo2(mp, 0, False) for mp in range(3)]
    wo2(3, 1, True)
    done_mp.append(wo2(3, 0, False))
    a_free.append(done_mp[3])
    for mp in range(4):
        for m in range(2):
            res2(2 * mp + m, mpb2[mp][m], done_mp[mp])

    first_t = []
    chs = [W.take() for _ in range(4)]
    for c, ch in enumerate(chs):
        kh, gu = c // 2, c % 2
        for k in range(4):
            kt = 4 * kh + k
            for m in range(2):
                bk = 2 * gu + m
                t = tr_mm(B[bk][:, :], ch, k, m, (HH, HL), kt, ALLC, kt == 0, kt == 7, h3[kt],
                          bank_free[bk] if kt == 0 else None, sig=sg("pe_ff") if (k == 3 and m == 1) else None)
        W.free[ch[0]] = t

    def first2(f_ready, r2):
        for m in range(2):
            a, b_, lo = glu(m, 1, ALLC, B[m], B[2 + m], R2, [t, r2], f_free2, m)
            bank_free[m], bank_free[2 + m] = [a], [b_]
            f_ready[m] = lo

    f_free2 = [done_mp[3], s3[0]]
    f_ready2, ff_end2, _ = ffn(lambda kt: h3[kt], lambda: s3[0], first2, f_free2, [(0, 1, 2, 3), (4, 5, 6, 7)])

    ld_fg = SP(lambda e: e.dma_start(FG[:, :], final_g_2.unsqueeze(0).broadcast_to([128, 1024])),
               [(signals["pe_misc"], signals["pe_misc"].value), (signals["pool_xsum"], signals["pool_xsum"].value)],
               sig=sg("dma_fg"), by=16)
    x3n = None
    x3n_t = []
    for b in range(4):
        for q in range(2):
            bk = 6 + (2 * b + q) % 2
            for i in range(4):
                kt = 4 * q + i
                tr = transpose(B[bk][:, 128 * i:128 * i + 128], XT[:, kt, 128 * b:128 * b + 128], x3[kt], bank_free[bk],
                               sig=sg("pe_x3") if i == 3 else None)
            x3n = SCA(lambda e, b=b, q=q, bk=bk: e.activation(X3N[:, b, 512 * q:512 * q + 512], B[bk][:, :], ACT.Copy),
                      tr, ff_end2, sig=sg("act_x3"))
            bank_free[bk] = [x3n]
    x4 = {}
    sqf = {}

    def finish(b, q, bank, done):
        cols = slice(512 * q, 512 * q + 512)
        x4[b, q] = VEC(lambda e: e.tensor_tensor(X3N[:, b, cols], B[bank][:, :], X3N[:, b, cols], ALU.add), done, x3n,
                       sig=sg("dve_x4"))
        bank_free[bank] = [x4[b, q]]
        sqf[b, q] = SCA(lambda e: e.activation(JNK[:, :], X3N[:, b, cols], ACT.Square,
                                               accum_out=SSF[:, 2 * b + q:2 * b + q + 1]), x4[b, q], sqf.get("last"),
                        ld_fg, sig=sg("act_sf"))
        sqf["last"] = sqf[b, q]

    dsets = [(0, 1, 2, 3), (4, 5, 6, 7)]
    nchunk = NF // 2
    HOLD = 4
    for q in range(2):
        head = nchunk if q == 0 else nchunk - HOLD
        for c in range(head):
            j, wh, wl, wt = W.take()
            for k in range(2):
                kt = 2 * c + k
                for b in range(4):
                    tok = slice(128 * b, 128 * b + 128)
                    bk = dsets[q][b]
                    t = mm3(B[bk][:, :], (FFH[:, kt, tok], FFL[:, kt, tok]), (wh[:, k, :], wl[:, k, :]), kt == 0,
                            kt == NF - 1, wt, f_ready2[kt], bank_free[bk] if kt == 0 else None,
                            sig=sg("pe_dn") if (k == 1 and b == 3) else None)
            W.free[j] = t
        if q == 0:
            for b in range(4):
                finish(b, 0, dsets[0][b], t)
    hold = [W.take() for _ in range(HOLD)]
    ld_out = []
    for b in range(4):
        tok = slice(128 * b, 128 * b + 128)
        bk = dsets[1][b]
        for i, (j, wh, wl, wt) in enumerate(hold):
            for k in range(2):
                kt = 2 * (nchunk - HOLD + i) + k
                t = mm3(B[bk][:, :], (FFH[:, kt, tok], FFL[:, kt, tok]), (wh[:, k, :], wl[:, k, :]), False,
                        kt == NF - 1, wt, f_ready2[kt], sig=sg("pe_dn") if (i == HOLD - 1 and k == 1) else None)
        finish(b, 1, bk, t)
        s = VEC(lambda e, b=b: e.tensor_tensor(SSG[:, b:b + 1], SSF[:, 2 * b:2 * b + 1], SSF[:, 2 * b + 1:2 * b + 2], ALU.add),
                sqf[b, 1], sqf[b, 0], sig=sg("dve_fin"))
        s = VEC(lambda e, b=b: e.tensor_scalar(SSG[:, b:b + 1], SSG[:, b:b + 1], 1.0 / D, EPS, ALU.mult, ALU.add), s,
                sig=sg("dve_fin"))
        p = POOL(lambda e, b=b: e.tensor_tensor(RFN[:, b:b + 1], SSG[:, b:b + 1], HALF[:, :], ALU.pow), s, sig=sg("pool_fin"))
        y = VEC(lambda e, b=b: e.scalar_tensor_tensor(YO[:, b, :], X3N[:, b, :], RFN[:, b:b + 1], FG[:, :], ALU.mult,
                                                      ALU.mult), p, ld_fg, ff_end2, x4[b, 0], x4[b, 1], sig=sg("dve_fin"))
        st = SP(lambda e, b=b: e.dma_start(out[0, 128 * b:128 * b + 128, :], YO[:, b, :]), y, sig=sg("dma_out"), by=16)
    for c in hold:
        W.free[c[0]] = t
    SP(lambda e: e.wait_ge(signals["dma_out"].handle, 64))
    assert W.next == len(chunks)

    with nc.Block() as block:
        @block.sync
        def _(e):
            SP.play(e)

        @block.scalar
        def _(e):
            SCA.play(e)

        @block.vector
        def _(e):
            VEC.play(e)

        @block.gpsimd
        def _(e):
            POOL.play(e)

        @block.tensor
        def _(e):
            PE.play(e)


_INS = ["w_in", "q_norm_a", "k_norm_a", "sink_b", "w_out", "w_gate", "w_up", "w_down", "w_in_2", "b_forget_2",
        "w_pool_2", "w_out_2", "w_gate_2", "w_up_2", "w_down_2", "final_g_2"]
_GAINS = ["norm_mix_pre", "norm_mix_post", "norm_ffn_pre", "norm_ffn_post", "norm1_g_2", "norm2_g_2", "group_norm_a",
          "group_norm_b", "pool_scale_2"]


def kernel(**inputs):
    import concourse.bacc as _bacc
    from concourse.bass_utils import run_bass_kernel_spmd as _run

    nc = _bacc.Bacc("TRN2", target_bir_lowering=False, num_devices=1)
    arrays, args = {}, []
    laid = {"x_t": np.ascontiguousarray(np.asarray(inputs["x"])[0].T.reshape(8, 128, 512).transpose(1, 0, 2)),
            "gain_cols": np.ascontiguousarray(np.concatenate(
                [np.asarray(inputs[n])[0].reshape(-1, 128) for n in _GAINS], axis=0).T)}
    laid.update({n: np.ascontiguousarray(inputs[n]) for n in _INS})
    laid.update(zip(("c_ident", "c_small", "c_rope"), rope_and_masks()))
    for name, a in laid.items():
        arrays[f"in_{name}_dram"] = a
        args.append(nc.dram_tensor(f"in_{name}_dram", a.shape, mybir.dt.from_np(a.dtype), kind="ExternalInput").ap())
    args.append(nc.dram_tensor("out_0_dram", (1, 512, 1024), F32, kind="ExternalOutput").ap())
    program(nc, *args)
    r = _run(nc, [arrays], core_ids=[0])
    return r.results[0]["out_0_dram"]
```

```python
from contextlib import ExitStack

import numpy as np
import concourse.bass as bass
from concourse import mybir

ACT = mybir.ActivationFunctionType
ALU = mybir.AluOpType
AX = mybir.AxisListType
F32 = mybir.dt.float32
F32R = mybir.dt.float32r
BF16 = mybir.dt.bfloat16

EPS = 1e-6
NEG = -3.0e38
D = 1024
FF = 2816
NF = FF // 128
BASE = 16640
NRAW = 3
NSPLIT = 4
WCOLS = 1056

G_PRE, G_POST, G_FPRE, G_FPOST, G_N1, G_N2, G_A, G_B, G_PS = 0, 8, 16, 24, 32, 40, 48, 52, 56
NG = 60


class Signal:

    def __init__(self, handle):
        self.handle, self.value, self.owner = handle, 0, None

    def up(self, owner, by):
        assert self.owner in (None, owner)
        self.owner = owner
        self.value += by
        return (self, self.value)


class Queue:

    def __init__(self, name):
        self.name, self.ops, self.seen = name, [], {}

    def __call__(self, fn, *waits, sig=None, by=1):
        need = []
        todo = list(waits)
        while todo:
            w = todo.pop()
            if w is None:
                continue
            if isinstance(w, list):
                todo += w
                continue
            s, v = w
            if self.seen.get(s, 0) < v:
                self.seen[s] = v
                need.append(w)
        self.ops.append((need, fn, sig, by))
        return sig.up(self.name, by) if sig is not None else None

    def play(self, engine):
        for need, fn, sig, by in self.ops:
            best = {}
            for s, v in need:
                best[s] = max(best.get(s, 0), v)
            for s, v in best.items():
                engine.wait_ge(s.handle, v)
            ins = fn(engine)
            if sig is not None:
                ins.then_inc(sig.handle, by)


def rope_and_masks():
    r = np.arange(128)[:, None]
    c = np.arange(128)[None, :]
    ident = np.eye(128, dtype=np.float32)
    left = np.where(c >= r, 0.0, NEG).astype(np.float32)
    right = np.where(c <= r, 0.0, NEG).astype(np.float32)
    upper = (r <= c).astype(np.float32)
    count = np.zeros((128, 4, 16), np.float32)
    for g in range(4):
        count[:, g, :] = 1.0 / np.minimum(np.arange(16) + 1, 2 ** (g + 1))
    sel = np.zeros((128, 8), np.float32)
    for h in range(8):
        sel[[h, 32 + h, 64 + h, 96 + h], h] = 1.0
    t = np.arange(512, dtype=np.float32)
    theta = np.float64(10000.0)
    fa = (theta ** (-np.arange(16, dtype=np.float64) / 16)).astype(np.float32)
    f1 = (theta ** (-np.arange(32, dtype=np.float64) / 32)).astype(np.float32)
    row, col = np.floor(t / 64).astype(np.float32), (t % 64).astype(np.float32)
    ax = np.concatenate([row[:, None] * fa[None], col[:, None] * fa[None]], axis=1)
    a1 = t[:, None] * f1[None]
    tabs = []
    for ang in (ax, a1):
        cs, sn = np.cos(ang.astype(np.float64)), np.sin(ang.astype(np.float64))
        for full in (np.concatenate([cs, cs], 1), np.concatenate([-sn, sn], 1)):
            tabs.append(full.astype(np.float32).reshape(4, 128, 64).transpose(1, 0, 2).reshape(128, 256))
    small = np.concatenate([left, right, upper, count.reshape(128, 64), sel], axis=1)
    return ident, np.ascontiguousarray(small), np.ascontiguousarray(np.concatenate(tabs, axis=1))


def program(nc, x_t, gain_cols, w_in, q_norm_a, k_norm_a, sink_b, w_out, w_gate, w_up, w_down, w_in_2, b_forget_2,
            w_pool_2, w_out_2, w_gate_2, w_up_2, w_down_2, final_g_2, c_ident, c_small, c_rope, out):
    ctx = ExitStack()
    signals = {}

    def sg(name):
        if name not in signals:
            signals[name] = Signal(ctx.enter_context(nc.semaphore(name)))
        return signals[name]

    PE, SCA, VEC, POOL, SP = (Queue(n) for n in ("pe", "act", "dve", "pool", "sp"))

    def sb(name, shape, dt, off):
        return nc.alloc_sbuf_tensor_at(name, shape, dt, offset=BASE + off)

    o_xt, o_hh, o_hl = 0, 16384, 32768
    XT = sb("XT", [128, 8, 512], F32, o_xt)
    HH = sb("HH", [128, 8, 512], F32R, o_hh)
    HL = sb("HL", [128, 8, 512], F32R, o_hl)
    o_raw = 49152
    RAW = [sb(f"RAW{i}", [128, WCOLS], F32, o_raw + 4224 * i) for i in range(NRAW)]
    o_w = o_raw + 4224 * NRAW
    WH = [sb(f"WH{i}", [128, WCOLS], F32R, o_w + 8448 * i) for i in range(NSPLIT)]
    WL = [sb(f"WL{i}", [128, WCOLS], F32R, o_w + 8448 * i + 4224) for i in range(NSPLIT)]
    o_c = o_w + 8448 * NSPLIT
    cur = [o_c]

    def const(name, shape, dt, nbytes):
        t = sb(name, shape, dt, cur[0])
        cur[0] += (nbytes + 31) // 32 * 32
        return t

    IDENT = const("IDENT", [128, 128], F32, 512)
    ONES = const("ONES", [128, 128], F32, 512)
    UPPER = const("UPPER", [128, 128], F32, 512)
    IDB = const("IDB", [128, 128], BF16, 256)
    MLB = const("MLB", [128, 128], BF16, 256)
    MRB = const("MRB", [128, 128], BF16, 256)
    ONB = const("ONB", [128, 128], BF16, 256)
    GC = const("GC", [128, NG], F32, 240)
    ICNT = const("ICNT", [128, 4, 16], F32, 256)
    SEL = const("SEL", [128, 8], F32R, 32)
    SKB = const("SKB", [128, 8], BF16, 16)
    BF = const("BF", [128, 8], F32, 32)
    HALF = const("HALF", [128, 1], F32, 4)
    RN = const("RN", [128, 4], F32, 16)
    RN8 = const("RN8", [128, 4], F32, 16)
    SSH = const("SSH", [128, 16], F32, 64)
    FH16 = const("FH16", [128, 16], F32, 64)
    NM = const("NM", [128, 8], F32, 32)
    DEN = const("DEN", [128, 8], F32, 32)
    RD = const("RD", [128, 8], F32, 32)
    RSC = const("RSC", [128, 12, 8], F32, 384)
    SKF = const("SKF", [128, 8], F32, 32)
    SKT = const("SKT", [128, 8], F32, 32)
    SKT2 = const("SKT2", [128, 8], BF16, 16)
    o_r = cur[0]
    REG = 229368 - BASE - o_r

    def rg(name, shape, dt, off):
        t = sb(name, shape, dt, o_r + off)
        n = 4 if dt != BF16 else 2
        for s in shape[1:]:
            n *= s
        assert off + n <= REG, (name, off + n, REG)
        return t

    PTH = [rg(f"PTH{i}", [128, 4, 256], F32R, 8192 * i) for i in range(2)]
    PTL = [rg(f"PTL{i}", [128, 4, 256], F32R, 8192 * i + 4096) for i in range(2)]
    MIX1 = rg("MIX1", [128, 8, 512], F32, 0)
    OR = rg("OR", [128, 8, 512], F32, 16384)
    QS = rg("QS", [128, 8, 512], F32R, 32768)
    K1 = rg("K1", [128, 4, 512], F32R, 49152)
    K2 = rg("K2", [128, 2, 512], F32R, 57344)
    VS = rg("VS", [128, 4, 4, 128], F32R, 61440)
    PR = [rg(f"PR{i}", [128, 516], F32, 69632 + 2080 * i) for i in range(4)]
    OT = [rg(f"OT{i}", [128, 256], F32, 77952 + 1024 * i) for i in range(2)]
    TQ1 = rg("TQ1", [128, 4, 64], F32, 80000)
    TQ2 = rg("TQ2", [128, 4, 64], F32, 81024)
    TAB = rg("TAB", [128, 4, 4, 64], F32, 82048)
    RW = [rg(f"RW{i}", [128, 512], F32, 86144 + 2048 * i) for i in range(2)]
    QRAW = rg("QRAW", [128, 4, 256], F32, 90240)
    WA = rg("WA", [128, 4, 256], F32, 94336)
    WB = rg("WB", [128, 4, 256], F32, 98432)
    KLN = rg("KLN", [128, 4, 256], F32R, 28672)
    STK = rg("STK", [128, 4, 4, 128], F32R, 102528)
    SQ4 = rg("SQ4", [128, 4, 512], F32, 102528)
    CSM = rg("CSM", [128, 456], F32, 104576)
    QKG = rg("QKG", [128, 2, 64], F32, 106496)

    TS = [rg(f"TS{i}", [128, 512], F32, 2048 * i) for i in range(2)]
    TU = [rg(f"TU{i}", [128, 512], F32, 4096 + 2048 * i) for i in range(2)]
    FFH = rg("FFH", [128, NF, 512], F32R, 8192)
    FFL = rg("FFL", [128, NF, 512], F32R, 8192 + 2048 * NF)
    o_n = 8192 + 4096 * NF
    NSQ = [rg(f"NSQ{i}", [128, 512], F32, o_n + 2048 * i) for i in range(2)]
    NSUM = rg("NSUM", [128, 512], F32, o_n + 4096)
    NRP = rg("NRP", [128, 512], F32, o_n + 6144)
    NU = [rg(f"NU{i}", [128, 256], F32, o_n + 8192 + 1024 * i) for i in range(2)]
    NSUM2 = rg("NSUM2", [128, 512], F32, o_n + 10240)
    R2 = rg("R2", [128, 512], F32, o_n + 12288)
    XSQ1 = [rg(f"XSQA{i}", [128, 256], F32, 16384 + 1024 * i)[:, :] for i in range(4)]
    XSQ2 = [rg(f"XSQB{i}", [128, 256], F32, 1024 * i)[:, :] for i in range(4)]
    MIX2 = sb("MIX2", [128, 8, 512], F32, o_hl)

    QS2 = rg("QS2", [128, 8, 512], F32R, 16384)
    K1B = rg("K1B", [128, 8, 512], F32R, 32768)
    K2B = rg("K2B", [128, 4, 512], F32R, 49152)
    VSB = rg("VSB", [128, 8, 4, 128], F32R, 57344)
    PRB = [rg(f"PRB{i}", [128, 512], F32, 73728 + 2048 * i) for i in range(4)]
    OTB = [rg(f"OTB{i}", [128, 256], F32, 81920 + 1024 * i) for i in range(2)]
    FLG, FL1, FL2, FL3 = (rg(f"FLG{i}", [128, 4, 8], F32, 81920 + 128 * i) for i in range(4))
    ORB = rg("ORB", [128, 4, 512], F32, 83968)
    CT = rg("CT", [104, 512], F32R, 92160)
    STK2 = rg("STK2", [128, 4, 4, 128], F32R, 94208)
    STK3 = rg("STK3", [128, 4, 4, 128], F32R, 73728)
    KLN2 = rg("KLN2", [128, 4, 256], F32R, 102400)
    UR = rg("UR", [128, 4, 512], F32, 94208)
    _at, _pl = [49152, 102400, 40960, 24576], [32768, 36864, 16384, 20480]
    AH = [rg(f"AH{i}", [128, 512], F32R, _at[i]) for i in range(4)]
    AL = [rg(f"AL{i}", [128, 512], F32R, _at[i] + 2048) for i in range(4)]
    PLH = [rg(f"PLH{i}", [128, 512], F32R, _pl[i]) for i in range(4)]
    PLL = [rg(f"PLL{i}", [128, 512], F32R, _pl[i] + 2048) for i in range(4)]
    PS1, PS2 = rg("PS1", [128, 512], F32, _pl[0]), rg("PS2", [128, 512], F32, _pl[0] + 2048)
    PD = rg("PD", [128, 512], F32, 106496)

    X3N = sb("X3N", [128, 4, 1024], F32, o_hh)
    YO = sb("YO", [128, 4, 1024], F32, o_hl)
    FG = rg("FG", [128, 1024], F32, o_n)
    JNK = rg("JNK", [128, 512], F32, o_n + 4096)
    SSF = rg("SSF", [128, 8], F32, o_n + 6144)
    SSG = rg("SSG", [128, 4], F32, o_n + 6176)
    RFN = rg("RFN", [128, 4], F32, o_n + 6208)

    B = [ctx.enter_context(nc.psum_tensor(f"B{i}", [128, 512], F32)) for i in range(8)]
    bank_free = [[] for _ in range(8)]

    def f32(ap):
        return ap.bitcast(F32)

    chunks = []

    def wchunk(w, k0, nk, c0, nc_):
        chunks.append(([(w[0, 128 * k0:128 * (k0 + nk), c0:c0 + nc_].rearrange("(k p) c -> p k c", p=128), 0, nc_)],
                       nk, nc_))

    def wchunk2(w, k0, nk, ca, cb):
        chunks.append(([(w[0, 128 * k0:128 * (k0 + nk), c:c + 128].rearrange("(k p) c -> p k c", p=128), 128 * i, 128)
                        for i, c in enumerate((ca, cb))], nk, 256))

    for kh in range(2):
        wchunk2(w_in, 4 * kh, 4, 512, 1280)
        wchunk2(w_in, 4 * kh, 4, 640, 1408)
    for c0 in (0, 256, 768, 1024):
        for kh in range(2):
            wchunk(w_in, 4 * kh, 4, c0, 256)
    for kh, mps in ((0, (0, 1, 2)), (1, (0, 1, 2))):
        for mp in mps:
            wchunk(w_out, 4 * kh, 4, 256 * mp, 256)
    for kh in range(2):
        wchunk(w_out, 4 * kh, 4, 768, 256)

    def ffn_chunks(wg, wu, interleave):
        for p in range(NF // 2):
            order = [(w, kh) for kh in range(2) for w in (wg, wu)] if p == 0 and interleave else \
                [(w, kh) for w in (wg, wu) for kh in range(2)]
            for w, kh in order:
                wchunk(w, 4 * kh, 4, 256 * p, 256)

    ffn_chunks(w_gate, w_up, True)
    KD = [(k, min(4, NF - k)) for k in range(0, NF, 4)]
    for mp in range(4):
        for k0, nk in KD:
            wchunk(w_down, k0, nk, 256 * mp, 256)
    for kh in range(2):
        for c0 in (0, 512):
            wchunk(w_in_2, 4 * kh, 4, c0, 256)
    for c0, n in ((1280, 264), (1024, 256), (256, 256), (768, 256), (1800, 256), (1544, 256)):
        for kh in range(2):
            wchunk(w_in_2, 4 * kh, 4, c0, n)
    chunks.append(([(w_pool_2[0].rearrange("g p c -> p g c"), 0, 128)], 4, 128))
    for kh, mps in ((1, (0, 1, 2)), (0, (0, 1, 2))):
        for mp in mps:
            wchunk(w_out_2, 4 * kh, 4, 256 * mp, 256)
    for kh in (1, 0):
        wchunk(w_out_2, 4 * kh, 4, 768, 256)
    ffn_chunks(w_gate_2, w_up_2, True)
    for fh in range(2):
        for k0 in range(0, NF, 2):
            wchunk(w_down_2, k0, 2, 512 * fh, 512)

    class Weights:
        def __init__(self):
            self.loaded, self.split_n, self.next = 0, 0, 0
            self.lo_queue, self.low, self.defer = VEC, [], False
            self.dma, self.hi, self.lo, self.free = {}, {}, {}, {}

        def view(self, t, j):
            _, nk, n = chunks[j]
            return t[:, :nk * n].rearrange("p (k c) -> p k c", k=nk)

        def load(self):
            j = self.loaded
            if j >= len(chunks) or (j >= NRAW and (j - NRAW) not in self.lo):
                return False
            pieces, nk, n = chunks[j]
            dst = self.view(RAW[j % NRAW], j)
            raw_free = [self.hi[j - NRAW], self.lo[j - NRAW]] if j >= NRAW else None
            for ap, c0, cn in pieces:
                self.dma[j] = SP(lambda e, ap=ap, c0=c0, cn=cn: e.dma_start(dst[:, :, c0:c0 + cn], ap),
                                 raw_free, sig=sg(f"dma_w{j % NRAW}"), by=16)
            self.loaded += 1
            return True

        def split(self):
            j = self.split_n
            if j >= self.loaded or (j >= NSPLIT and (j - NSPLIT) not in self.free):
                return False
            _, nk, n = chunks[j]
            raw, hi, lo = (t[:, :nk * n] for t in (RAW[j % NRAW], WH[j % NSPLIT], WL[j % NSPLIT]))
            slot_free = self.free.get(j - NSPLIT)
            self.hi[j] = SCA(lambda e: e.activation(hi, raw, ACT.Copy), self.dma[j], slot_free, sig=sg("act_w"))
            q = self.lo_queue

            def low(c0, c1):
                t = q(lambda e: e.tensor_tensor(lo[:, c0:c1], raw[:, c0:c1], f32(hi[:, c0:c1]), ALU.subtract), self.hi[j],
                      slot_free, sig=sg(q.name + "_w"))
                if c1 == nk * n:
                    self.lo[j] = t
            mid = [0, nk * n // 2, nk * n] if q is POOL else [0, nk * n]
            self.low += [lambda c0=c0, c1=c1: low(c0, c1) for c0, c1 in zip(mid, mid[1:])]
            self.split_n += 1
            return True

        def begin(self, n, queue):
            if self.split_n < self.next + n:
                self.lo_queue = queue
                assert self.split()
                self.lo_queue = VEC

        def drip(self):
            if self.low:
                self.low.pop(0)()
            while self.load():
                pass

        def flush(self):
            while self.low:
                self.low.pop(0)()

        def ahead(self, n):
            if not self.defer:
                self.flush()
            while self.loaded < min(n, len(chunks)) and self.load():
                pass
            while self.split_n < min(n, len(chunks)):
                if not self.split():
                    break
                if not self.defer:
                    self.flush()
                self.load()
            while self.load():
                pass

        def take(self, more=2):
            j = self.next
            self.next += 1
            while self.split_n <= j:
                if not self.split():
                    self.flush()
                    if self.split_n <= j and not self.split():
                        assert self.load()
            if j not in self.lo or not more:
                self.flush()
            while self.load():
                pass
            if more:
                self.ahead(j + 1 + more)
            assert self.split_n > j
            return j, self.view(WH[j % NSPLIT], j), self.view(WL[j % NSPLIT], j), [self.hi[j], self.lo[j]]

    W = Weights()

    def mm3(dst, sta, mov, start, stop, *waits, sig=None):
        (sh, sl), (mh, ml) = sta, mov
        PE(lambda e: e.matmul(dst, sh, mh, start=start, stop=False), *waits)
        PE(lambda e: e.matmul(dst, sh, ml, start=False, stop=False))
        return PE(lambda e: e.matmul(dst, sl, mh, start=False, stop=stop), sig=sig)

    def transpose(dst, src, *waits, sig=None):
        n = src.shape[0]
        return PE(lambda e: e.transpose(dst, src, IDENT[0:n, 0:n]), *waits, sig=sig)

    ld_gains = SP(lambda e: e.dma_start(GC[:, :], gain_cols), sig=sg("dma_gains"), by=16)
    ld_x = {}

    def load_x(k0, n):
        t = SP(lambda e: e.dma_start(XT[:, k0:k0 + n, :], x_t[:, k0:k0 + n, :]), sig=sg(f"dma_x{k0}"), by=16)
        for k in range(k0, k0 + n):
            ld_x[k] = t

    load_x(0, 1)
    W.load()
    load_x(1, 1)
    W.load()
    load_x(2, 2)
    W.load()
    load_x(4, 2)
    load_x(6, 2)
    ld_ident = SCA(lambda e: e.dma_start(IDENT[:, :], c_ident), sig=sg("dma_ident"), by=16)
    ld_csm = SCA(lambda e: e.dma_start(CSM[:, :], c_small), ld_x[2], sig=sg("dma_csm"), by=16)
    cst = sg("pool_const")
    POOL(lambda e: e.memset(HALF[:, :], -0.5), sig=cst)
    onb_ready = POOL(lambda e: e.memset(ONB[:, :], 1.0), sig=cst)
    POOL(lambda e: e.memset(SKB[:, :], 0.0), sig=cst)
    ones_ready = POOL(lambda e: e.memset(ONES[:, :], 1.0), sig=cst)
    ld_tab = POOL(lambda e: e.dma_start(TAB[:, :, :, :].rearrange("p a b c -> p (a b c)"), c_rope), ld_x[2],
                  sig=sg("dma_tab"), by=16)
    ld_qkg = None
    for i, g in enumerate((q_norm_a, k_norm_a)):
        ld_qkg = POOL(lambda e, i=i, g=g: e.dma_start(QKG[:, i, :], g[0:1, :].broadcast_to([128, 64])),
                      sig=sg("dma_qkg"), by=16)
    ld_sink = POOL(lambda e: e.dma_start(SKF[:, :], sink_b[0:1, :].broadcast_to([128, 8])), sig=sg("dma_sink"), by=16)
    ld_bf = POOL(lambda e: e.dma_start(BF[:, :], b_forget_2[0:1, :].broadcast_to([128, 8])), sig=sg("dma_bf"), by=16)
    gains = ld_gains

    def half_col(shape):
        return HALF[:, 0:1].to_broadcast(shape)

    def gcol(g, k):
        return GC[:, g + k:g + k + 1]

    h_ready = [None] * 8
    xs = {"sum": None, "sq": [None, None]}
    XSUM, XSQ = WA[:, 0:2, :].rearrange("p a c -> p (a c)"), [WB[:, 0:2, :].rearrange("p a c -> p (a c)"),
                                                             WB[:, 2:4, :].rearrange("p a c -> p (a c)")]

    def prep(kt):
        hi = SCA(lambda e: e.activation(HH[:, kt, :], XT[:, kt, :], ACT.Copy, scale=gcol(G_PRE, kt)),
                 ld_x[kt], gains, sig=sg("act_h"))
        h_ready[kt] = VEC(lambda e: e.scalar_tensor_tensor(HL[:, kt, :], XT[:, kt, :], gcol(G_PRE, kt),
                                                           f32(HH[:, kt, :]), ALU.mult, ALU.subtract),
                          hi, ld_x[kt], gains, sig=sg("dve_h"))

    def square(kt):
        if kt == 0:
            xs["sum"] = SCA(lambda e: e.activation(XSUM, XT[:, 0, :], ACT.Square), ld_x[0], sig=sg("act_xsq"))
            return
        i = kt % 2
        q = SCA(lambda e: e.activation(XSQ[i], XT[:, kt, :], ACT.Square), ld_x[kt], xs["sq"][i], sig=sg("act_xsq"))
        xs["sum"] = xs["sq"][i] = VEC(lambda e: e.tensor_tensor(XSUM, XSUM, XSQ[i], ALU.add), q, xs["sum"],
                                      sig=sg("dve_xsum"))

    kv_chunk = {}
    kv_done = [None]

    def kv_mm(kt):
        for g in range(2):
            j, wh, wl, wt = kv_chunk[g]
            for b in range(4):
                tok = slice(128 * b, 128 * b + 128)
                dst = B[2 * g + b // 2][:, 256 * (b % 2):256 * (b % 2) + 256]
                end = kt % 4 == 3 and b == 3
                t = mm3(dst, (HH[:, kt, tok], HL[:, kt, tok]), (wh[:, kt % 4, :], wl[:, kt % 4, :]),
                        kt == 0 and b % 2 == 0, kt == 7 and b % 2 == 1, h_ready[kt], wt, sig=sg("pe_kv") if end else None)
                if end:
                    W.free[j] = kv_done[0] = t

    def other_constants():
        VEC(lambda e: e.tensor_copy(IDB[:, :], IDENT[:, :]), ld_ident, sig=sg("dve_c"))
        VEC(lambda e: e.tensor_copy(MLB[:, :], CSM[:, 0:128]), ld_csm, sig=sg("dve_c"))
        VEC(lambda e: e.tensor_copy(MRB[:, :], CSM[:, 128:256]), sig=sg("dve_c"))
        VEC(lambda e: e.tensor_copy(UPPER[:, :], CSM[:, 256:384]), sig=sg("dve_c"))
        VEC(lambda e: e.tensor_copy(ICNT[:, :, :].rearrange("p g t -> p (g t)"), CSM[:, 384:448]), sig=sg("dve_c"))
        A.consts = VEC(lambda e: e.tensor_copy(SEL[:, :], CSM[:, 448:456]), sig=sg("dve_c"))
        s0 = VEC(lambda e: e.tensor_copy(SKB[0:1, :], SKF[0:1, :]), ld_sink, ones_ready, sig=sg("dve_sk"))
        s1 = VEC(lambda e: e.tensor_tensor(SKT[0:1, :], SKF[0:1, :], SKB[0:1, :], ALU.subtract), s0, sig=sg("dve_sk"))
        s2 = VEC(lambda e: e.tensor_copy(SKB[32:33, :], SKT[0:1, :]), s1, sig=sg("dve_sk"))
        s2b = VEC(lambda e: e.tensor_copy(SKT2[0:1, :], SKT[0:1, :]), s1, sig=sg("dve_sk"))
        s3 = VEC(lambda e: e.tensor_tensor(SKT[0:1, :], SKT[0:1, :], SKT2[0:1, :], ALU.subtract), s2, s2b,
                 sig=sg("dve_sk"))
        A.sink_ready = VEC(lambda e: e.tensor_copy(SKB[64:65, :], SKT[0:1, :]), s3, sig=sg("dve_sk"))
        tq = VEC(lambda e: e.tensor_tensor(TQ1[:, :, :], TAB[:, 0, :, :], QKG[:, 0:1, :].to_broadcast([128, 4, 64]),
                                           ALU.mult), ld_tab, ld_qkg, sig=sg("dve_tab"))
        for s in range(2):
            a, z = 32 * s, 32 * (1 - s)
            tq = VEC(lambda e, a=a, z=z: e.tensor_tensor(
                TQ2[:, :, a:a + 32], TAB[:, 1, :, a:a + 32],
                QKG[:, 0:1, z:z + 32].to_broadcast([128, 4, 32]), ALU.mult), sig=sg("dve_tab"))
        tk = VEC(lambda e: e.tensor_tensor(TAB[:, 0, :, :], TAB[:, 0, :, :],
                                           QKG[:, 1:2, :].to_broadcast([128, 4, 64]), ALU.mult), tq, sig=sg("dve_tab"))
        for s in range(2):
            a, z = 32 * s, 32 * (1 - s)
            tk = VEC(lambda e, a=a, z=z: e.tensor_tensor(
                TAB[:, 1, :, a:a + 32], TAB[:, 1, :, a:a + 32],
                QKG[:, 1:2, z:z + 32].to_broadcast([128, 4, 32]), ALU.mult), tq, sig=sg("dve_tab"))
        A.tables = tk

    class Bag:
        pass

    A = Bag()
    prep(0)
    kv_chunk[0] = W.take(0)
    prep(1)
    kv_chunk[1] = W.take(0)
    kv_mm(0)
    prep(2)
    kv_mm(1)
    prep(3)
    kv_mm(2)
    prep(4)
    kv_mm(3)
    kv_chunk[0] = W.take(0)
    prep(5)
    kv_chunk[1] = W.take(0)
    prep(6)
    prep(7)
    W.ahead(5)
    kv_mm(4)
    for kt in range(4):
        square(kt)
    W.ahead(6)
    kv_mm(5)
    for kt in range(4, 8):
        square(kt)
    kv_mm(6)

    rstd_use = [0]

    def rstd_tokens(sums, n, bank, done):
        nb = sums.shape[1] // 128
        i = rstd_use[0]
        rstd_use[0] += 1
        v, r = RSC[:, i, 0:nb], RSC[:, i, 4:4 + nb]
        for b in range(nb):
            m = PE(lambda e, b=b: e.matmul(B[bank][:, b:b + 1], sums[:, 128 * b:128 * b + 128], ONES[:, 0:1],
                                           start=True, stop=True), done, ones_ready, bank_free[bank],
                   sig=sg("pe_misc") if b == nb - 1 else None)
        a = VEC(lambda e: e.tensor_scalar(v, B[bank][:, 0:nb], 1.0 / n, EPS, ALU.mult, ALU.add), m, sig=sg("dve_row"))
        bank_free[bank] = [a]
        return r, POOL(lambda e: e.tensor_tensor(r, v, half_col([128, nb]), ALU.pow), a, sig=sg("pool_row"))

    def rstd_rows(dst, r, done, bank, dst_free):
        nb = r.shape[1]
        for b in range(nb):
            m = PE(lambda e, b=b: e.matmul(B[bank][:, 128 * b:128 * b + 128], r[:, b:b + 1].to_broadcast([128, 128]),
                                           IDENT[:, :], start=True, stop=True), done, ld_ident, bank_free[bank],
                   sig=sg("pe_misc") if b == nb - 1 else None)
        c = VEC(lambda e: e.tensor_copy(dst, B[bank][:, 0:128 * nb]), m, dst_free, sig=sg("dve_row"))
        bank_free[bank] = [c]
        return c

    def nat_rstd(r, done):
        a = VEC(lambda e: e.tensor_copy(RN[:, :], r), done, sig=sg("dve_rn"))
        return VEC(lambda e: e.tensor_scalar(RN8[:, :], RN[:, :], 0.125, None, ALU.mult), a, sig=sg("dve_rn"))

    r_nat = rstd_tokens(XSUM, D, 5, xs["sum"])
    other_constants()
    kv_mm(7)
    rn = nat_rstd(*r_nat)

    t_ring = [3, 4]
    t_count = [0]

    def t_bank():
        bk = t_ring[t_count[0] % 2]
        t_count[0] += 1
        return bk

    A.q_ready, A.k_ready, A.v_ready = {}, None, None
    A.qraw_free = A.wb_free = A.stk_free = None
    A.qs_free = {}

    def v_evac(banks, vs, r, h0, nh, step, done, waits):
        for bk in sorted({bk for bk, _ in banks}):
            mine = [(b, B[bk][:, off:off + 64 * nh].rearrange("p (h c) -> p h c", c=64))
                    for b, (bank, off) in enumerate(banks) if bank == bk]
            for b, src in mine:
                hi = SCA(lambda e, src=src, b=b: e.activation(vs[:, h0:h0 + nh, b, 0:64], src, ACT.Copy,
                                                              scale=r[:, b:b + 1]), done, waits, sig=sg("act_v"))
            for b, src in mine:
                tok = VEC(lambda e, src=src, b=b: e.scalar_tensor_tensor(
                    vs[:, h0:h0 + nh, b, 64:128], src, r[:, b:b + 1], f32(vs[:, h0:h0 + nh, b, 0:64]),
                    ALU.mult, ALU.subtract), hi, waits, sig=sg("dve_v"))
            bank_free[bk] = [tok]
        return tok

    def rope(kind, banks, done, slot, turn_banks):
        n_a = {"qa": 4, "qb": 0, "k": 2}[kind]
        scale = RN8 if kind == "qb" else RN
        ev = []
        for b in range(4):
            bk, off = banks[b]
            ev.append(SCA(lambda e, bk=bk, off=off, b=b: e.activation(
                QRAW[:, b, :], B[bk][:, off:off + 256], ACT.Copy, scale=scale[:, b:b + 1]),
                done, rn, A.qraw_free, sig=sg("act_q")))
        for b in range(4):
            bank_free[banks[b][0]] = [ev[b]]
        src_t = ev[3]
        yield
        q4 = QRAW[:, :, :].rearrange("p b (h c) -> p b h c", c=64)
        a4 = WA[:, :, :].rearrange("p b (h c) -> p b h c", c=64)
        b4 = WB[:, :, :].rearrange("p b (h c) -> p b h c", c=64)
        if n_a:
            ncol = 4 * n_a
            ssh = SSH[:, 0:ncol].rearrange("p (b h) -> p b h", b=4)
            f16 = FH16[:, 0:ncol].rearrange("p (b h) -> p b h", b=4)
            sq = SCA(lambda e: e.activation(b4[:, :, 0:n_a, :], q4[:, :, 0:n_a, :], ACT.Square), src_t, A.wb_free,
                     sig=sg("act_qsq"))
            yield
            s = VEC(lambda e: e.tensor_reduce(ssh, b4[:, :, 0:n_a, :], AX.X, ALU.add), sq, sig=sg("dve_q"))
            if kind == "qa":
                s = VEC(lambda e: e.tensor_scalar(ssh, ssh, 1.0, 64 * EPS, ALU.mult, ALU.add), s, sig=sg("dve_q"))
            else:
                s = VEC(lambda e: e.tensor_scalar(ssh, ssh, 1.0 / 64, EPS, ALU.mult, ALU.add), s, sig=sg("dve_q"))
            yield
            for c in range(0, ncol, 8):
                f = POOL(lambda e, c=c: e.tensor_tensor(FH16[:, c:c + 8], SSH[:, c:c + 8], half_col([128, 8]), ALU.pow),
                         s, sig=sg("pool_q"))
                yield
            fb = f16.unsqueeze(3).to_broadcast([128, 4, n_a, 64])
            src_t = VEC(lambda e: e.tensor_tensor(q4[:, :, 0:n_a, :], q4[:, :, 0:n_a, :], fb, ALU.mult), f, src_t,
                        sig=sg("dve_q"))
            yield
        parts = {"qa": [(0, 4, TQ1[:, :, :], TQ2[:, :, :])],
                 "qb": [(0, 4, TAB[:, 2, :, :], TAB[:, 3, :, :])],
                 "k": [(0, 2, TAB[:, 0, :, :], TAB[:, 1, :, :]), (2, 2, TAB[:, 2, :, :], TAB[:, 3, :, :])]}[kind]
        ta = []
        for h0, nh, t1, t2 in parts:
            for b0 in (0, 2):
                c1 = t1[:, b0:b0 + 2, :].unsqueeze(2).to_broadcast([128, 2, nh, 64])
                ta.append(POOL(lambda e, h0=h0, nh=nh, c1=c1, b0=b0: e.tensor_tensor(
                    a4[:, b0:b0 + 2, h0:h0 + nh, :], q4[:, b0:b0 + 2, h0:h0 + nh, :], c1, ALU.mult), src_t, A.tables,
                    A.stk_free, sig=sg("pool_q")))
            for s in range(2):
                a, z = 32 * s, 32 * (1 - s)
                c2 = t2[:, :, a:a + 32].unsqueeze(2).to_broadcast([128, 4, nh, 32])
                ta.append(VEC(lambda e, h0=h0, nh=nh, a=a, z=z, c2=c2: e.tensor_tensor(
                    b4[:, :, h0:h0 + nh, a:a + 32], q4[:, :, h0:h0 + nh, z:z + 32], c2, ALU.mult),
                    src_t, A.tables, A.wb_free, sig=sg("dve_q")))
                yield
        A.qraw_free = ta
        yield
        rot = VEC(lambda e: e.tensor_tensor(WA[:, :, :], WA[:, :, :], WB[:, :, :], ALU.add), ta, sig=sg("dve_q"))
        A.wb_free = rot
        yield
        st = STK[:, :, :, :].rearrange("p b h c -> p (b h) c")
        wa = WA[:, :, :].rearrange("p b (h c) -> p (b h) c", c=64)
        if kind != "k":
            par = slot % 8 // 4
            oh, ol = 64 * par, 64 * (1 - par)
            hi = SCA(lambda e: e.activation(st[:, :, oh:oh + 64], wa, ACT.Copy), rot, A.stk_free, sig=sg("act_qh"))
            yield
            lo = VEC(lambda e: e.tensor_tensor(st[:, :, ol:ol + 64], wa, f32(st[:, :, oh:oh + 64]), ALU.subtract),
                     hi, sig=sg("dve_q"))
        else:
            hi = SCA(lambda e: e.activation(st[:, :, 0:64], wa, ACT.Copy), rot, A.stk_free, sig=sg("act_qh"))
            hi2 = SCA(lambda e: e.activation(st[:, :, 64:128], wa, ACT.Copy), sig=sg("act_qh"))
            yield
            lo = VEC(lambda e: e.tensor_tensor(KLN[:, :, :].rearrange("p b (h c) -> p (b h) c", c=64), wa,
                                               f32(st[:, :, 0:64]), ALU.subtract), hi, rot, sig=sg("dve_q"))
            hi = hi2
        yield
        turns = [("s", b) for b in range(4)]
        if kind == "k":
            turns = [(w, b) for b in range(4) for w in ("s", "l")]
        done_t, evac = [], []
        for n, (w, b) in enumerate(turns):
            bk = turn_banks[n % 2]
            nh = 4 if w == "s" else 2
            for h in range(nh):
                src = f32(STK[:, b, h, :]) if w == "s" else f32(KLN[:, b, 128 * h:128 * h + 128])
                tr = transpose(B[bk][:, 128 * h:128 * h + 128], src, lo, hi, bank_free[bk],
                               sig=sg("pe_tq") if h == nh - 1 else None)
            cols = slice(128 * b, 128 * b + 128)
            dst = K2[:, 0:2, cols] if w == "l" else K1[:, 0:4, cols] if kind == "k" else QS[:, slot % 8:slot % 8 + 4, cols]
            qs_free = [A.qs_free.get(slot + i - 8) for i in range(4)] if kind != "k" else None
            yield
            ev = SCA(lambda e, bk=bk, dst=dst, nh=nh: e.activation(
                dst, B[bk][:, 0:128 * nh].rearrange("p (h c) -> p h c", h=nh), ACT.Copy), tr, qs_free, sig=sg("act_qs"))
            bank_free[bk] = [ev]
            done_t.append(ev)
        A.stk_free = tr
        if kind == "k":
            A.k_ready = done_t
        else:
            for i in range(4):
                A.q_ready[slot + i] = done_t

    def nat_proj(banks, hs, res):
        for kh in range(2):
            j, wh, wl, wt = W.take()
            n = wh.shape[2]
            for k in range(4):
                kt = 4 * kh + k
                for b in range(4):
                    bk, off = banks[b]
                    tok = slice(128 * b, 128 * b + 128)
                    t = mm3(B[bk][:, off:off + n], (HH[:, kt, tok], HL[:, kt, tok]), (wh[:, k, :], wl[:, k, :]),
                            kt == 0 and off == 0, kt == 7 and (off > 0 or n > 256), hs[kt], wt, bank_free[bk] if kt == 0 else None,
                            sig=sg("pe_proj") if (k == 3 and b == 3) else None)
                    if b % 2:
                        yield
            W.free[j] = t
        res.append(t)

    PJ = [(6, 0), (6, 256), (7, 0), (7, 256)]

    def q_group(kind, slot, turn_banks=(6, 7)):
        res = []
        yield from nat_proj(PJ, h_ready, res)
        yield from rope(kind, PJ, res[0], slot, turn_banks)

    def drain(gen):
        for _ in gen:
            pass

    KB = [(0, 0), (0, 256), (1, 0), (1, 256)]
    VB = [(2, 0), (2, 256), (3, 0), (3, 256)]
    A.v_ready = v_evac(VB, VS, RN, 0, 4, None, kv_done, rn)
    A.wb_free = A.stk_free = [rn, A.consts, A.tables]
    kgen = rope("k", KB, kv_done, 0, (3, 4))
    next(kgen)
    proj0 = q_group("qa", 0, (3, 4))
    for i in range(17):
        next(proj0)
        if i >= 5:
            next(kgen)
    proj1 = q_group("qa", 4)
    for i in range(17):
        next(proj1)
        if i % 2:
            next(proj0)
        if i > 3:
            next(kgen, None)
    drain(kgen)
    proj4 = q_group("qb", 8)
    proj5 = q_group("qb", 12)
    drain(proj0)

    class Attention:
        def __init__(self, units, P, OTs, vs):
            self.units, self.P, self.OTs, self.vs = units, P, OTs, vs
            self.npair = 0

        def scores(self, i):
            u = self.units[i]
            u.bank = i % 3
            n = u.n
            dst = B[u.bank]
            w = [bank_free[u.bank], u.ready()]
            PE(lambda e: e.matmul(dst[:, 0:n], u.q, u.k1, start=True, stop=False), w)
            last = not u.extra
            u.s = PE(lambda e: e.matmul(dst[:, 0:n], u.qh, u.k2, start=False, stop=last),
                     sig=sg("pe_s") if last else None)
            for n_x, (c0, cn, lhs, rhs, wt) in enumerate(u.extra):
                end = n_x == len(u.extra) - 1
                u.s = PE(lambda e, c0=c0, cn=cn, lhs=lhs, rhs=rhs, end=end: e.matmul(
                    dst[:, c0:c0 + cn], lhs, rhs, start=False, stop=end), wt, sig=sg("pe_s") if end else None)

        def maxes(self, i):
            u = self.units[i]
            c = i % 8
            u.max = VEC(lambda e: e.tensor_reduce(NM[:, c:c + 1], B[u.bank][:, 0:u.width], AX.X, ALU.max, negate=True),
                        u.s, self.units[i - 8].exp if i >= 8 else None, sig=sg("dve_max"))

        def exps(self, i):
            u = self.units[i]
            c = i % 8
            p = self.P[i % 4]
            u.exp = SCA(lambda e: e.activation(p[:, 0:u.width], B[u.bank][:, 0:u.width], ACT.Exp, bias=NM[:, c:c + 1],
                                               scale=1.0, accum_out=DEN[:, c:c + 1]),
                        u.max, self.units[i - 4].t if i >= 4 else u.p_free,
                        self.units[i - 8].rec if i >= 8 else None, sig=sg("act_exp"))
            bank_free[u.bank] = [u.exp]

        def norms(self, i):
            u = self.units[i]
            c = i % 8
            p = self.P[i % 4]
            u.rec = VEC(lambda e: e.reciprocal(RD[:, c:c + 1], DEN[:, c:c + 1]), u.exp,
                        self.units[i - 8].norm if i >= 8 else None, sig=sg("dve_rec"))
            u.norm = POOL(lambda e: e.tensor_scalar(p[:, 0:u.n], p[:, 0:u.n], RD[:, c:c + 1], 1.0, ALU.mult, ALU.mult),
                          u.rec, u.exp, sig=sg("pool_p"))

        def turns(self, i):
            u = self.units[i]
            p = self.P[i % 4]
            bk = t_bank()
            nb = u.n // 128
            for j in range(nb):
                u.t = transpose(B[bk][:, 128 * j:128 * j + 128], p[:, 128 * j:128 * j + 128], u.norm, bank_free[bk],
                                sig=sg("pe_t") if j == nb - 1 else None)
            s = u.pair % 2
            cols = slice(128 * (u.b % 2), 128 * (u.b % 2) + 128)
            u.src = B[bk][:, 0:u.n].rearrange("p (k c) -> p k c", c=128)
            u.t_bank = bk
            u.ph, u.pl = (t[s][:, u.kb:u.kb + nb, cols] for t in (PTH, PTL))
            u.pt_free = self.pv_tok.get(u.pair - 2, u.pt_free)
            u.hi = SCA(lambda e: e.activation(u.ph, u.src, ACT.Copy), u.t, u.pt_free, sig=sg("act_pt"))

        def lows(self, i):
            u = self.units[i]
            u.lo = VEC(lambda e: e.tensor_tensor(u.pl, u.src, f32(u.ph), ALU.subtract), u.hi, u.pt_free, sig=sg("dve_pt"))
            bank_free[u.t_bank] = [u.lo]

        def values(self, i):
            u1 = self.units[i]
            u0 = self.units[i - 1]
            assert u0.pair == u1.pair
            s = u1.pair % 2
            bk = 5
            dst = B[bk]
            kbs = sorted(set(range(u0.kb, u0.kb + u0.n // 128)) | set(range(u1.kb, u1.kb + u1.n // 128)))

            def cols(kb):
                has = [u.kb <= kb < u.kb + u.n // 128 for u in (u0, u1)]
                return (0 if has[0] else 128, 256 if has[1] else 128)

            kbs.sort(key=lambda kb: (cols(kb) != (0, 256), kb))
            assert cols(kbs[0]) == (0, 256)
            seq = [(kb, t) for kb in kbs for t in (PTH[s], PTL[s])]
            for n, (kb, t) in enumerate(seq):
                a, z = cols(kb)
                end = n == len(seq) - 1
                pv = PE(lambda e, kb=kb, t=t, a=a, z=z, n=n, end=end: e.matmul(
                    dst[:, a:z], self.vs[:, u1.v, kb, :], t[:, kb, a:z], start=n == 0, stop=end),
                    u0.lo, u1.lo, bank_free[bk], u1.v_ready, sig=sg("pe_pv") if end else None)
            self.pv_tok[u1.pair] = pv
            ot = self.OTs[u1.pair % 2]
            lowc = []

            def low():
                lowc.append(SCA(lambda e: e.activation(ot[0:64, :], dst[64:128, 0:256], ACT.Copy), pv,
                                self.ot_free.get(u1.pair - 2, u1.p_free), sig=sg("act_o")))

            def add():
                t = VEC(lambda e: e.tensor_tensor(u1.o, dst[0:64, 0:256], ot[0:64, :], ALU.add), lowc, u1.o_free,
                        sig=sg("dve_o"))
                self.ot_free[u1.pair] = t
                bank_free[bk] = [t]
                u1.done(t)
            self.low, self.add = low, add

        def run(self, fill, lo_queue):
            self.pv_tok, self.ot_free, self.low, self.add = {}, {}, None, None
            W.defer, W.lo_queue = True, lo_queue
            n = len(self.units)
            self.scores(0)
            self.scores(1)
            for i in range(n + 7):
                low, add, self.low, self.add = self.low, self.add, None, None
                if i < n:
                    self.maxes(i)
                if 0 <= i - 4 < n:
                    self.lows(i - 4)
                if 0 <= i - 3 < n:
                    self.turns(i - 3)
                if i + 2 < n:
                    self.scores(i + 2)
                if i < n:
                    self.exps(i)
                if low:
                    low()
                if 1 <= i <= n:
                    self.norms(i - 1)
                if add:
                    add()
                k = i - 5
                if 0 <= k < n and k % 2 == 1:
                    self.values(k)
                W.drip()
                fill(i)
            W.defer, W.lo_queue = False, VEC

    class Unit:
        pass

    def filler(gens):
        live = list(gens)

        def go(n):
            while n > 0 and live:
                try:
                    next(live[0])
                    n -= 1
                except StopIteration:
                    live.pop(0)
        return go

    units = []
    o_done = {}
    for h in range(16):
        win = h >= 8
        kv = (h // 4)
        for b in range(4):
            u = Unit()
            u.h, u.b = h, b
            u.pair = 2 * h + b // 2
            s = kv % 2
            k0, k1 = (max(0, b - 1), min(4, b + 2)) if win else (0, 4)
            u.kb, u.n = k0, 128 * (k1 - k0)
            u.width = u.n + 1 if win else u.n
            slot = h % 8
            u.q = QS[:, slot, 128 * b:128 * b + 128]
            u.qh = QS[64 * s:64 * s + 64, slot, 128 * b:128 * b + 128]
            u.k1 = K1[:, kv, 128 * k0:128 * k1]
            u.k2 = K2[64 * s:64 * s + 64, kv // 2, 128 * k0:128 * k1]
            u.ready = lambda h=h: [A.q_ready[h], A.k_ready]
            u.v, u.v_ready = kv, A.v_ready
            u.p_free, u.pt_free, u.o_free = None, None, None
            u.extra = []
            if win:
                if b > 0:
                    u.extra.append((0, 128, IDB[:, :], MLB[:, :], [A.consts]))
                if b < 3:
                    u.extra.append((u.n - 128, 128, IDB[:, :], MRB[:, :], [A.consts]))
                u.extra.append((u.n, 1, ONB[0:65, :], SKB[0:65, h - 8:h - 7], [A.sink_ready, onb_ready]))
            u.o = OR[64 * (h % 2):64 * (h % 2) + 64, h // 2, 256 * (b // 2):256 * (b // 2) + 256]
            u.done = lambda t, h=h: o_done.setdefault(h, []).append(t)
            units.append(u)

    hs_o = [None] * 8

    def group_norm(g, col, bank, h_free):
        src = OR[:, 4 * g:4 * g + 4, :]
        ow = [o_done[8 * g + i] for i in range(8)]
        assert all(len(t) == 2 for t in ow)
        sq = SCA(lambda e: e.activation(SQ4[:, :, :], src, ACT.Square), ow, A.stk_free, A.sq4_free, sig=sg("act_gn"))
        yield
        s = VEC(lambda e: e.tensor_tensor(SQ4[:, 0:2, :], SQ4[:, 0:2, :], SQ4[:, 2:4, :], ALU.add), sq, sig=sg("dve_gn"))
        yield
        s = VEC(lambda e: e.tensor_tensor(RW[0][:, :], SQ4[:, 0, :], SQ4[:, 1, :], ALU.add), s, A.rw_free, sig=sg("dve_gn"))
        A.sq4_free = s
        yield
        r, p = rstd_tokens(RW[0][:, :], 512, bank, s)
        yield
        p = rstd_rows(RW[1][:, :], r, p, bank, A.rw_free)
        yield
        for i in range(4):
            t = 4 * g + i
            n = VEC(lambda e, t=t: e.tensor_tensor(OR[:, t, :], OR[:, t, :], RW[1][:, :], ALU.mult), p, sig=sg("dve_gn"))
            hi = SCA(lambda e, t=t, i=i: e.activation(HH[:, t, :], OR[:, t, :], ACT.Copy, scale=gcol(col, i)), n, h_free,
                     sig=sg("act_gn"))
            hs_o[t] = VEC(lambda e, t=t, i=i: e.scalar_tensor_tensor(HL[:, t, :], OR[:, t, :], gcol(col, i),
                                                                     f32(HH[:, t, :]), ALU.mult, ALU.subtract),
                          hi, h_free, n, sig=sg("dve_gn"))
            yield
        A.rw_free = n

    A.sq4_free = A.rw_free = None

    def late_a():
        A.h_free = (signals["pe_proj"], signals["pe_proj"].value)
        yield from group_norm(0, G_A, 6, A.h_free)

    def spread(plan):
        given = [0] * len(plan)

        def go(i):
            for p, (gen, s0, s1, n) in enumerate(plan):
                if s0 <= i < s1:
                    want = -(-n * (i + 1 - s0) // (s1 - s0))
                    while given[p] < want:
                        given[p] += 1
                        next(gen, None)
                if i == s1 - 1 and all(g is not gen for g, *_ in plan[p + 1:]):
                    drain(gen)
        return go

    att = Attention(units, PR, OT, VS)
    for i, u in enumerate(units):
        if u.b == 3:
            def done_q(i=i):
                A.qs_free[units[i].h] = units[i].s
            u.q_done = done_q
        else:
            u.q_done = None
    scores0 = att.scores

    def scores_and_release(i):
        scores0(i)
        if units[i].q_done:
            units[i].q_done()
    att.scores = scores_and_release
    att.run(spread([(proj1, 0, 9, 11), (proj4, 9, 28, 25), (proj5, 28, 46, 25), (late_a(), 46, 56, 10)]), VEC)
    p_end = units[-1].t
    pv_end = att.pv_tok[units[-1].pair]

    def tr_mm(dst, chunk, k, m, h, kt, cols, start, stop, *waits, sig=None):
        j, wh, wl, wt = chunk
        hh, hl = h
        return mm3(dst, (wh[:, k, 128 * m:128 * m + 128], wl[:, k, 128 * m:128 * m + 128]),
                   (hh[:, kt, cols], hl[:, kt, cols]), start, stop, wt, *waits, sig=sig)

    ALLC = slice(0, 512)
    HALVES = [slice(0, 256), slice(256, 512)]

    class PostNorm:

        def __init__(self, mix, g_post, g_next, mix_free, work_free, rp_bank, h_free, xsq):
            self.mix, self.gp, self.gn = mix, g_post, g_next
            self.mix_free, self.work_free = mix_free, work_free
            self.rp_bank, self.h_free, self.xsq = rp_bank, h_free, xsq
            self.xsq_free = [work_free] * len(xsq)
            self.nsq, self.sum_tok = [work_free, work_free], [None, None]
            self.count = 0
            self.mix_tok = {}
            self.h = [[None, None] for _ in range(8)]
            self.u_tok = [work_free, work_free]
            self.first = True
            self.sums2 = [None, None]

        def full(self, m, bank, done):
            c = SCA(lambda e: e.activation(self.mix[:, m, :], B[bank][:, :], ACT.Copy), done, self.mix_free,
                    sig=sg("act_mix"))
            bank_free[bank] = [c]
            self.mix_tok[m] = [c, c]
            i = self.count % 2
            self.count += 1
            if self.first:
                t = SCA(lambda e: e.activation(NSUM[:, :], self.mix[:, m, :], ACT.Square), c, self.work_free,
                        sig=sg("act_msq"))
                self.sum_tok = [t, t]
                self.first = False
                return
            q = SCA(lambda e: e.activation(NSQ[i][:, :], self.mix[:, m, :], ACT.Square), c, self.nsq[i],
                    sig=sg("act_msq"))
            t = VEC(lambda e: e.tensor_tensor(NSUM[:, :], NSUM[:, :], NSQ[i][:, :], ALU.add), q, self.sum_tok,
                    sig=sg("dve_msum"))
            self.nsq[i] = t
            self.sum_tok = [t, t]

        def half(self, hf, bank, done):
            cols = HALVES[hf]
            i = self.count % 2
            self.count += 1
            q = SCA(lambda e: e.activation(NSQ[i][:, :], B[bank][:, :], ACT.Square), done, self.nsq[i], sig=sg("act_msq"))
            c = SCA(lambda e: e.activation(self.mix[:, 6:8, cols], B[bank][:, :].rearrange("p (m c) -> p m c", m=2),
                                           ACT.Copy), q, sig=sg("act_mix"))
            bank_free[bank] = [c]
            for m in (6, 7):
                self.mix_tok.setdefault(m, [None, None])[hf] = c
            yield
            t = VEC(lambda e: e.tensor_tensor(NSUM[:, cols], NSUM[:, cols], NSQ[i][:, 0:256], ALU.add), q,
                    self.sum_tok[hf], sig=sg("dve_msum"))
            t = VEC(lambda e: e.tensor_tensor(NSUM[:, cols], NSUM[:, cols], NSQ[i][:, 256:512], ALU.add), t,
                    sig=sg("dve_msum"))
            self.nsq[i] = t
            self.sum_tok[hf] = t
            rb = self.rp_bank[hf]
            yield
            r, p = rstd_tokens(NSUM[:, cols], D, rb, t)
            yield
            p = rstd_rows(NRP[:, cols], r, p, rb, self.work_free)
            yield
            us = {}

            def post(kt):
                n = kt % 2
                us[kt] = VEC(lambda e: e.scalar_tensor_tensor(
                    NU[n][:, :], self.mix[:, kt, cols], gcol(self.gp, kt), NRP[:, cols], ALU.mult, ALU.mult),
                    p, self.mix_tok[kt][hf], self.u_tok[n], sig=sg("dve_x"))

            pend = None
            post(0)
            for kt in range(8):
                n = kt % 2
                if kt < 7:
                    post(kt + 1)
                xx = VEC(lambda e, kt=kt, n=n: e.tensor_tensor(XT[:, kt, cols], XT[:, kt, cols], NU[n][:, :], ALU.add),
                         us[kt], sig=sg("dve_x"))
                self.u_tok[n] = xx
                if pend:
                    pend()
                hi = SCA(lambda e, kt=kt: e.activation(HH[:, kt, cols], XT[:, kt, cols], ACT.Copy,
                                                       scale=gcol(self.gn, kt)), xx, self.h_free[hf], sig=sg("act_h"))

                def lo(kt=kt, hi=hi, xx=xx):
                    self.h[kt][hf] = VEC(lambda e: e.scalar_tensor_tensor(
                        HL[:, kt, cols], XT[:, kt, cols], gcol(self.gn, kt), f32(HH[:, kt, cols]), ALU.mult,
                        ALU.subtract), hi, xx, self.h_free[hf], sig=sg("dve_h"))
                pend = lo
                if kt == 0:
                    sums = SCA(lambda e: e.activation(NSUM2[:, cols], XT[:, 0, cols], ACT.Square), xx, self.work_free,
                               sig=sg("act_xsq"))
                else:
                    z = kt % len(self.xsq)
                    q = SCA(lambda e, kt=kt, z=z: e.activation(self.xsq[z], XT[:, kt, cols], ACT.Square), xx,
                            self.xsq_free[z], sig=sg("act_xsq"))
                    sums = POOL(lambda e, z=z: e.tensor_tensor(NSUM2[:, cols], NSUM2[:, cols], self.xsq[z], ALU.add),
                                q, sums, sig=sg("pool_xsum"))
                    self.xsq_free[z] = sums
                self.sums2[hf] = sums
                yield
            pend()
            yield

    def barrier(pn, groups, src, ready, banks, fresh, mm_next):
        last = {}

        def tail(hf):
            tot, n = sum(nk for _, _, nk in groups), 0
            for ch, k0, nk in groups:
                for k in range(nk):
                    for m in range(2):
                        t = tr_mm(B[banks[hf]][:, 256 * m:256 * m + 256], ch, k, m, src, k0 + k, HALVES[hf],
                                  fresh and n == 0 and m == 0, n == tot - 1 and m == 1, ready[k0 + k],
                                  bank_free[banks[hf]] if n == 0 and fresh else None,
                                  sig=sg("pe_tail") if (k == nk - 1 and m == 1) else None)
                    n += 1
                    if k == nk - 1 and hf == 1:
                        W.free[ch[0]] = t
                    last[hf] = t
                    yield
            pn.h_free[hf] = t

        drain(tail(0))
        c0 = pn.half(0, banks[0], last[0])
        next(c0)
        next(c0)
        for i, _ in enumerate(tail(1)):
            if i in (0, 3):
                W.begin(1 + i // 3, (VEC, POOL)[i // 3])
            if i in (2, 5):
                next(c0)
            if i in (2, 4, 5):
                W.drip()
        c1 = pn.half(1, banks[1], last[1])
        next(c0)
        next(c0)
        pairs = [[W.take(0), W.take(0)], None]
        for kt in range(8):
            while pn.h[kt][0] is None:
                next(c0)
            for _ in range((0, 0, 1, 2, 0, 0, 0, 0)[kt]):
                W.drip()
            if kt in (0, 1, 3, 5):
                next(c1)
            if kt in (1, 2):
                W.begin(kt, (VEC, POOL)[kt - 1])
            if kt == 4:
                pairs[1] = [W.take(0), W.take(0)]
            mm_next(0, kt, pairs[kt // 4])
        for kt in range(8):
            while pn.h[kt][1] is None:
                next(c1)
            if kt in (5, 7):
                W.drip()
            if kt in (4, 6):
                W.begin(kt // 2 - 1, VEC)
            mm_next(1, kt, pairs[kt // 4])
        drain(c1)

    OH = (HH, HL)
    mpb = {0: (6, 7), 1: (0, 1), 2: (2, 3)}
    gb = group_norm(1, G_B, 4, A.h_free)
    drain(gb)
    bank_w = {}
    for kh in range(2):
        for mp in range(3):
            ch = W.take()
            for k in range(4):
                kt = 4 * kh + k
                for m in range(2):
                    bk = mpb[mp][m]
                    t = tr_mm(B[bk][:, :], ch, k, m, OH, kt, ALLC, kt == 0, kt == 7, hs_o[kt],
                              bank_free[bk] if kt == 0 else None, sig=sg("pe_wo") if k == 3 else None)
            W.free[ch[0]] = t
            bank_w[mp] = t
    wo_b = None
    post1 = PostNorm(MIX1, G_POST, G_FPRE, [pv_end], [signals["dve_gn"].value and (signals["dve_gn"], signals["dve_gn"].value),
                     A.stk_free], (6, 7), [None, None], XSQ1)

    for mp in range(3):
        for m in range(2):
            post1.full(2 * mp + m, mpb[mp][m], bank_w[mp])
    ch_a, ch_b = W.take(), W.take(0)
    pair0 = {}

    def ffn_half(hf, kt, chs):
        for c in range(2):
            bk = 2 * hf + c
            for m in range(2):
                t = tr_mm(B[bk][:, 256 * m:256 * m + 256], chs[c], kt % 4, m, OH, kt, HALVES[hf], kt == 0 and m == 0,
                          kt == 7 and m == 1, post1.h[kt][hf], bank_free[bk] if kt == 0 else None,
                          sig=sg("pe_ff") if (kt % 4 == 3 and m == 1) else None)
            if hf == 1 and kt % 4 == 3:
                W.free[chs[c][0]] = t
        pair0[hf] = t

    barrier(post1, [(ch_a, 0, 4), (ch_b, 4, 4)], OH, hs_o, (4, 5), True, ffn_half)

    def glu(fi, n, cols, pg, pu, r, done, free, it):
        ts, tu = TS[it % 2], TU[it % 2]
        width = cols.stop - cols.start
        view = (lambda t: t[:, :].rearrange("p (m c) -> p m c", m=n)) if n > 1 else (lambda t: t[:, :])
        rv = r[:, cols].unsqueeze(1).to_broadcast([128, n, width]) if n > 1 else r[:, cols]
        hv = FFH[:, fi:fi + n, cols] if n > 1 else FFH[:, fi, cols]
        lv = FFL[:, fi:fi + n, cols] if n > 1 else FFL[:, fi, cols]
        t = VEC(lambda e: e.tensor_tensor(view(ts), view(pg), rv, ALU.mult), done, free, F.ts_free[it % 2], sig=sg("dve_ff"))
        u = VEC(lambda e: e.tensor_tensor(view(tu), view(pu), rv, ALU.mult), F.tu_free[it % 2], sig=sg("dve_ff"))
        s = SCA(lambda e: e.activation(ts[:, :], ts[:, :], ACT.Silu), t, sig=sg("act_ff"))
        f = VEC(lambda e: e.tensor_tensor(tu[:, :], ts[:, :], tu[:, :], ALU.mult), s, u, sig=sg("dve_ff"))
        F.ts_free[it % 2] = f
        hi = SCA(lambda e: e.activation(hv, view(tu), ACT.Copy), f, free, sig=sg("act_ff"))
        lo = VEC(lambda e: e.tensor_tensor(lv, view(tu), f32(hv), ALU.subtract), hi, f, sig=sg("dve_ff"))
        F.tu_free[it % 2] = lo
        return t, u, lo

    F = Bag()

    def ffn_pair(p, h_tok, bset, between):
        for gu in range(2):
            for kh in range(2):
                ch = W.take()
                for k in range(4):
                    kt = 4 * kh + k
                    for m in range(2):
                        bk = bset[2 * gu + m]
                        t = tr_mm(B[bk][:, :], ch, k, m, (HH, HL), kt, ALLC, kt == 0, kt == 7, h_tok(kt),
                                  bank_free[bk] if kt == 0 else None, sig=sg("pe_ff") if (k == 3 and m == 1) else None)
                W.free[ch[0]] = t
                between(2 * gu + kh)
        return t

    def ffn(h_tok, sums, first, f_free, sets):
        F.ts_free, F.tu_free = [f_free, f_free], [f_free, f_free]
        f_ready = [None] * NF
        it = 0
        st = {}

        def between1(i):
            if i == 0:
                st["r"] = rstd_tokens(NSUM2[:, :], D, sets[1][3], sums())
            if i == 1:
                st["r2"] = rstd_rows(R2[:, :], *st["r"], sets[1][3], None)
                first(f_ready, st["r2"])

        for p in range(1, NF // 2):
            bset = sets[p % 2]
            t = ffn_pair(p, h_tok, bset, between1 if p == 1 else lambda i: None)
            for m in range(2):
                a, b_, lo = glu(2 * p + m, 1, ALLC, B[bset[m]], B[bset[2 + m]], R2, [t, st["r2"]], f_free, m)
                bank_free[bset[m]], bank_free[bset[2 + m]] = [a], [b_]
                f_ready[2 * p + m] = lo
        return f_ready, t, st["r"][0]

    mix1_read = [(signals["dve_x"], signals["dve_x"].value), (signals["act_mix"], signals["act_mix"].value)]
    f_free1 = mix1_read + [p_end]

    def first1(f_ready, r2):
        for hf in range(2):
            bg, bu = 2 * hf, 2 * hf + 1
            a, b_, lo = glu(0, 2, HALVES[hf], B[bg], B[bu], R2, [pair0[0], pair0[1], r2], f_free1, hf)
            bank_free[bg], bank_free[bu] = [a], [b_]
            f_ready[0] = f_ready[1] = lo

    f_ready, ff_end, _ = ffn(lambda kt: post1.h[kt], lambda: post1.sums2, first1, f_free1, [(0, 1, 2, 3), (4, 5, 6, 7)])

    FS = (FFH, FFL)
    nsum_free = [(signals["pool_xsum"], signals["pool_xsum"].value), (signals["pe_misc"], signals["pe_misc"].value),
                 (signals["dve_row"], signals["dve_row"].value), (signals["pool_row"], signals["pool_row"].value),
                 (signals["dve_x"], signals["dve_x"].value), (signals["dve_ff"], signals["dve_ff"].value)]
    post2 = PostNorm(MIX2, G_FPOST, G_N1, [ff_end], nsum_free, (0, 1), [ff_end, ff_end], XSQ2)
    dpb = {0: (4, 5), 1: (6, 7), 2: (0, 1)}
    for mp in range(3):
        for k0, nk in KD:
            ch = W.take()
            for k in range(nk):
                kt = k0 + k
                for m in range(2):
                    bk = dpb[mp][m]
                    t = tr_mm(B[bk][:, :], ch, k, m, FS, kt, ALLC, kt == 0, kt == NF - 1, f_ready[kt],
                              bank_free[bk] if kt == 0 else None, sig=sg("pe_dn") if k == nk - 1 else None)
            W.free[ch[0]] = t
        for m in range(2):
            post2.full(2 * mp + m, dpb[mp][m], t)
    for k0, nk in KD[:3]:
        ch = W.take()
        for k in range(nk):
            kt = k0 + k
            for hf in range(2):
                for m in range(2):
                    bk = 2 + hf
                    t = tr_mm(B[bk][:, 256 * m:256 * m + 256], ch, k, m, FS, kt, HALVES[hf], kt == 0 and m == 0, False,
                              f_ready[kt], bank_free[bk] if kt == 0 else None,
                              sig=sg("pe_dn") if (k == nk - 1 and m == 1) else None)
        W.free[ch[0]] = t
    tail_ch = [(W.take(2 if i == 0 else 0), k0, nk) for i, (k0, nk) in enumerate(KD[3:])]
    qk_t = {}

    def qk_half(hf, kt, chs):
        for which in range(2):
            j, wh, wl, wt = chs[which]
            bk = (4 + which) if hf == 0 else (6 + which)
            for bb in range(2):
                b = 2 * hf + bb
                tok = slice(128 * b, 128 * b + 128)
                t = mm3(B[bk][:, 256 * bb:256 * bb + 256], (HH[:, kt, tok], HL[:, kt, tok]),
                        (wh[:, kt % 4, :], wl[:, kt % 4, :]), kt == 0 and bb == 0, kt == 7 and bb == 1, wt,
                        post2.h[kt][hf], bank_free[bk] if kt == 0 else None,
                        sig=sg("pe_proj") if (kt % 4 == 3 and bb == 1) else None)
            if hf == 1 and kt % 4 == 3:
                W.free[j] = t
            qk_t[hf, which] = t

    barrier(post2, tail_ch, FS, f_ready, (2, 3), False, qk_half)
    f_end = post2.h_free[1]

    r_nat, r_tok = rstd_tokens(NSUM2[:, :], D, 2, post2.sums2)
    rn2 = nat_rstd(r_nat, [r_tok, rn])
    chain_end = [r_tok, (signals["dve_x"], signals["dve_x"].value), (signals["dve_h"], signals["dve_h"].value)]

    A2 = Bag()
    A2.v_ready = {}
    A2.q_ready, A2.k_ready = {}, {}
    st_free, kl_free = [chain_end, chain_end], [chain_end, chain_end]

    def turn2(bk, srcs, dst, lo):
        n = len(srcs)
        for h, src in enumerate(srcs):
            tr = transpose(B[bk][:, 128 * h:128 * h + 128], src, lo, bank_free[bk], sig=sg("pe_tq") if h == n - 1 else None)
        ev = SCA(lambda e: e.activation(dst, B[bk][:, 0:128 * n].rearrange("p (h c) -> p h c", h=n), ACT.Copy), tr, f_end,
                 sig=sg("act_qs"))
        bank_free[bk] = [ev]
        return tr, ev

    def q2_half(hf, bank, done, h0, turn):
        st = STK2[:, :, :, :].rearrange("p b (h s) c -> p b h s c", s=2)
        mine = [(2 * hf + i, s, B[bank][:, 256 * i:256 * i + 256].rearrange("p (h s c) -> p h s c", s=2, c=64)[:, :, s, :])
                for i in range(2) for s in range(2)]
        free = st_free[hf]
        for b, s, src in mine:
            hi = SCA(lambda e, b=b, s=s, src=src: e.activation(
                st[:, b, :, s, 64 * s:64 * s + 64], src, ACT.Copy, scale=RN8[:, b:b + 1]), done, rn2, free, sig=sg("act_q"))
        yield
        for b, s, src in mine:
            lo = VEC(lambda e, b=b, s=s, src=src: e.scalar_tensor_tensor(
                st[:, b, :, s, 64 - 64 * s:128 - 64 * s], src, RN8[:, b:b + 1],
                f32(st[:, b, :, s, 64 * s:64 * s + 64]), ALU.mult, ALU.subtract), hi, free, rn2, sig=sg("dve_q"))
        bank_free[bank] = [lo]
        yield
        for b in (2 * hf, 2 * hf + 1):
            yield
            st_free[hf], ev = turn2(turn(), [f32(STK2[:, b, h, :]) for h in range(4)],
                                    QS2[:, h0:h0 + 4, 128 * b:128 * b + 128], lo)
            for h in range(4):
                A2.q_ready.setdefault(h0 + h, []).append(ev)

    def k2_half(hf, bank, done, h0, turn, stk):
        mine = [(2 * hf + i, B[bank][:, 256 * i:256 * i + 256].rearrange("p (h c) -> p h c", c=64)) for i in range(2)]
        free = st_free[hf] if stk is STK2 else f_end
        for b, src in mine:
            hi = SCA(lambda e, b=b, src=src: e.activation(
                stk[:, b, :, :].rearrange("p h (s c) -> p h s c", s=2), src.unsqueeze(2).to_broadcast([128, 4, 2, 64]),
                ACT.Copy, scale=RN[:, b:b + 1]), done, rn2, free, sig=sg("act_q"))
        yield
        for b, src in mine:
            lo = VEC(lambda e, b=b, src=src: e.scalar_tensor_tensor(
                KLN2[:, b, :].rearrange("p (h c) -> p h c", c=64), src, RN[:, b:b + 1], f32(stk[:, b, :, 0:64]),
                ALU.mult, ALU.subtract), hi, kl_free[hf], rn2, sig=sg("dve_q"))
        bank_free[bank] = [lo]
        yield
        for b in (2 * hf, 2 * hf + 1):
            cols = slice(128 * b, 128 * b + 128)
            yield
            tr, e1 = turn2(turn(), [f32(stk[:, b, h, :]) for h in range(4)], K1B[:, h0:h0 + 4, cols], lo)
            if stk is STK2:
                st_free[hf] = tr
            else:
                A2.p_free = tr
            yield
            kl_free[hf], e2 = turn2(turn(), [f32(KLN2[:, b, 128 * h:128 * h + 128]) for h in range(2)],
                                    K2B[:, h0 // 2:h0 // 2 + 2, cols], lo)
            for h in range(4):
                A2.k_ready.setdefault(h0 + h, []).extend([e1, e2])

    class Side:

        def __init__(self):
            self.live = []

        def add(self, gen):
            self.live.append(gen)

        def step(self):
            while self.live:
                try:
                    return next(self.live[0])
                except StopIteration:
                    self.live.pop(0)

        def end(self):
            while self.live:
                self.step()

    h2r = post2.h
    VBK = [(0, 0), (1, 0), (3, 0), (2, 0)]
    VA = [(5, 0), (5, 256), (7, 0), (7, 256)]
    turn_n = [0]

    def turn46():
        turn_n[0] += 1
        return (4, 6)[turn_n[0] % 2]

    side = Side()
    early = [q2_half(0, 4, [qk_t[0, 0]], 0, turn46), q2_half(1, 6, [qk_t[1, 0]], 0, turn46),
             k2_half(0, 5, [qk_t[0, 1]], 0, turn46, STK3), k2_half(1, 7, [qk_t[1, 1]], 0, turn46, STK3)]
    for gen in early:
        next(gen)
        next(gen)
        side.add(gen)
    res = []
    for i, _ in enumerate(nat_proj(VBK, h2r, res)):
        if i >= 5:
            side.step()

    fl = None
    for b in range(4):
        bk = VBK[b][0]
        fl = VEC(lambda e, b=b, bk=bk: e.scalar_tensor_tensor(FLG[:, b, :], B[bk][:, 256:264], RN[:, b:b + 1], BF[:, :],
                                                             ALU.mult, ALU.add), ld_bf, res, rn2, f_end,
                 sig=sg("dve_f"))
    ct0 = POOL(lambda e: e.memset(f32(CT[:, :]), 0.0), f_end, sig=sg("pool_f"))

    def v(fn, *w):
        return VEC(fn, *w, sig=sg("dve_f"))

    t1 = v(lambda e: e.scalar_tensor_tensor(FL1[:, :, :], FLG[:, :, :], -1.0, FLG[:, :, :], ALU.mult, ALU.max), fl)
    ex = SCA(lambda e: e.activation(FL1[:, :, :], FL1[:, :, :], ACT.Exp, scale=-1.0), t1, sig=sg("act_f"))
    w1 = v(lambda e: e.tensor_scalar(FL2[:, :, :], FL1[:, :, :], 1.0, None, ALU.add), ex)
    ln = SCA(lambda e: e.activation(FL3[:, :, :], FL2[:, :, :], ACT.Ln), w1, sig=sg("act_f"))
    d1 = v(lambda e: e.scalar_tensor_tensor(FL1[:, :, :], FL2[:, :, :], -1.0, FL1[:, :, :], ALU.add, ALU.subtract), w1)
    rc = v(lambda e: e.reciprocal(FL2[:, :, :], FL2[:, :, :]), d1, ln)
    d2 = v(lambda e: e.tensor_tensor(FL1[:, :, :], FL1[:, :, :], FL2[:, :, :], ALU.mult), rc)
    l1 = v(lambda e: e.tensor_tensor(FL3[:, :, :], FL3[:, :, :], FL1[:, :, :], ALU.subtract), d2, ln)
    lf = v(lambda e: e.scalar_tensor_tensor(FLG[:, :, :], FLG[:, :, :], 0.0, FL3[:, :, :], ALU.min, ALU.subtract), l1)
    A2.v_ready[1] = v_evac(VBK, VSB, RN, 4, 4, None, res, [rn2, f_end, fl])

    def running_sums():
        for a in range(4):
            cols = slice(128 * a, 128 * a + 128)
            cs = PE(lambda e, a=a, cols=cols: e.matmul(B[0][0:8, cols], FLG[:, a, :], UPPER[:, :], start=a == 0,
                                                       stop=a == 3), lf, A.consts, bank_free[0], sig=sg("pe_misc"))
            if a < 3:
                PE(lambda e, a=a: e.matmul(B[0][0:8, 128 * a + 128:512], FLG[:, a, :],
                                           ONES[:, 0:1].to_broadcast([128, 384 - 128 * a]), start=False, stop=False))
        ch = VEC(lambda e: e.tensor_scalar(CT[0:8, :], B[0][0:8, :], -1.0, None, ALU.mult), cs, ct0, sig=sg("dve_f"))
        ct = VEC(lambda e: e.scalar_tensor_tensor(CT[32:40, :], B[0][0:8, :], -1.0, f32(CT[0:8, :]), ALU.mult,
                                                  ALU.subtract), ch, f_end, sig=sg("dve_f"))
        bank_free[0] = [ct]
        SCA(lambda e: e.activation(CT[64:72, :], f32(CT[0:8, :]), ACT.Copy), ch, sig=sg("act_f"))
        return [ct, SCA(lambda e: e.activation(CT[96:104, :], f32(CT[32:40, :]), ACT.Copy), ct, sig=sg("act_f"))]

    res = []
    for i, _ in enumerate(nat_proj(VA, h2r, res)):
        side.step()
        if i == 11:
            side.end()
            ct = running_sums()
            r2 = rstd_rows(R2[:, :], r_nat, r_tok, 3, None)
    A2.v_ready[0] = v_evac(VA, VSB, RN, 0, 4, None, res, [rn2, f_end])

    o2_done = {}
    units2 = []
    for h in range(8):
        for b in range(4):
            u = Unit()
            u.h, u.b, u.pair = h, b, 2 * h + b // 2
            s = h % 2
            u.kb, u.n = 0, 128 * (b + 1)
            u.width = u.n
            u.q = QS2[:, h, 128 * b:128 * b + 128]
            u.qh = QS2[64 * s:64 * s + 64, h, 128 * b:128 * b + 128]
            u.k1 = K1B[:, h, 0:u.n]
            u.k2 = K2B[64 * s:64 * s + 64, h // 2, 0:u.n]
            u.ready = lambda h=h: [A2.q_ready[h][:4], A2.k_ready[h][:8], ct]
            u.v, u.v_ready = h, A2.v_ready[h // 4]
            u.p_free, u.pt_free, u.o_free = [f_end, A2.p_free], [f_end], [f_end]
            u.extra = [(0, u.n, SEL[64 * s:64 * s + 40, h:h + 1].to_broadcast([40, 128]),
                        CT[64 * s:64 * s + 40, 0:u.n], [ct]),
                       (128 * b, 128, IDB[:, :], MRB[:, :], None)]
            u.o = ORB[64 * s:64 * s + 64, h // 2, 256 * (b // 2):256 * (b // 2) + 256]
            u.done = lambda t, h=h: o2_done.setdefault(h, []).append(t)
            units2.append(u)

    att2 = Attention(units2, PRB, OTB, VSB)
    mix_ready = [None] * 8

    def o_split(i):
        src = ORB[:, i, :]
        assert len(o2_done[2 * i]) == len(o2_done[2 * i + 1]) == 2
        w = [o2_done[2 * i], o2_done[2 * i + 1], kl_free, units2[15 if i < 2 else 23].s]
        hi = SCA(lambda e: e.activation(AH[i][:, :], src, ACT.Copy), w, sig=sg("act_os"))

        def low():
            mix_ready[i] = VEC(lambda e: e.tensor_tensor(AL[i][:, :], src, f32(AH[i][:, :]), ALU.subtract), hi, w,
                               sig=sg("dve_os"))
        o_low.append(low)

    o_low = []

    mh = [AH[i] for i in range(4)] + [PLH[i] for i in range(4)]
    ml = [AL[i] for i in range(4)] + [PLL[i] for i in range(4)]
    mpb2 = {0: (6, 7), 1: (0, 1), 2: (2, 3), 3: (4, 5)}

    def wo2(mp, kh, first):
        ch = W.take()
        j, wh, wl, wt = ch
        for n, k in enumerate((3, 2, 1, 0) if kh else range(4)):
            kt = 4 * kh + k
            for m in range(2):
                bk = mpb2[mp][m]
                t = mm3(B[bk][:, :], (wh[:, k, 128 * m:128 * m + 128], wl[:, k, 128 * m:128 * m + 128]),
                        (mh[kt][:, :], ml[kt][:, :]), first and n == 0, (not first) and n == 3, wt, mix_ready[kt],
                        bank_free[bk] if first and n == 0 else None, sig=sg("pe_wo") if n == 3 else None)
                yield
        W.free[j] = t
        wo_tok[mp] = t

    wo_tok = {}

    def proj_half(chs, bank, hf, done):
        for kt in range(8):
            j, wh, wl, wt = chs[kt // 4]
            for i in range(2):
                tok = slice(256 * hf + 128 * i, 256 * hf + 128 * i + 128)
                t = mm3(B[bank][:, 256 * i:256 * i + 256], (HH[:, kt, tok], HL[:, kt, tok]),
                        (wh[:, kt % 4, :], wl[:, kt % 4, :]), kt == 0 and i == 0, kt == 7 and i == 1, h2r[kt], wt,
                        bank_free[bank] if kt == 0 else None, sig=sg("pe_proj") if kt % 4 == 3 and i == 1 else None)
            if hf and kt % 4 == 3:
                W.free[j] = t
            yield
        done.append(t)

    def u_tile(chs, m, done):
        bank = 7 - m
        for kt in range(8):
            t = tr_mm(B[bank][:, :], chs[kt // 4], kt % 4, m, (HH, HL), kt, ALLC, kt == 0, kt == 7, h2r[kt],
                      bank_free[bank] if kt == 0 else None, sig=sg("pe_u") if kt % 4 == 3 else None)
            if m == 0 and kt % 4 == 3:
                W.free[chs[kt // 4][0]] = t
            yield
        done.append(t)

    pool_in = [None] * 4
    last_pd = [None]

    def means(g, bank, done):
        w = [units2[15].s, last_pd[0], chain_end]
        src = UR[:, g, :]
        ur = VEC(lambda e: e.tensor_tensor(src, B[bank][:, :], R2[:, :], ALU.mult), done, r2, st_free, sig=sg("dve_u"))
        bank_free[bank] = [ur]
        yield
        last, cur_t = ur, src
        for lvl in range(g + 1):
            sh = 1 << lvl
            dst = (PS1, PS2)[lvl % 2]
            VEC(lambda e, dst=dst, cur_t=cur_t, sh=sh: e.tensor_copy(dst[:, 0:sh], cur_t[:, 0:sh]), last, w, sig=sg("dve_u"))
            last = VEC(lambda e, dst=dst, cur_t=cur_t, sh=sh: e.tensor_tensor(
                dst[:, sh:512], cur_t[:, sh:512], cur_t[:, 0:512 - sh], ALU.add), last, w, sig=sg("dve_u"))
            cur_t = dst[:, :]
            yield
        wide = 1 << (g + 1)
        a = VEC(lambda e: e.tensor_tensor(PD[:, 0:16], cur_t[:, 0:16], ICNT[:, g, :], ALU.mult), last, w, sig=sg("dve_u"))
        b = VEC(lambda e: e.scalar_tensor_tensor(PD[:, 16:512], cur_t[:, 16:512], 1.0 / wide, src[:, 16:512], ALU.mult,
                                                 ALU.subtract), last, w, sig=sg("dve_u"))
        a = VEC(lambda e: e.tensor_tensor(PD[:, 0:16], PD[:, 0:16], src[:, 0:16], ALU.subtract), a, sig=sg("dve_u"))
        yield
        hi = SCA(lambda e: e.activation(PLH[g][:, :], PD[:, :], ACT.Copy), a, b, w, sig=sg("act_u"))
        yield
        pool_in[g] = last_pd[0] = VEC(lambda e: e.tensor_tensor(PLL[g][:, :], PD[:, :], f32(PLH[g][:, :]), ALU.subtract),
                                      hi, w, sig=sg("dve_u"))
        yield

    def pooled(g, bank, t):
        hi = SCA(lambda e: e.activation(PLH[g][:, :], B[bank][:, :], ACT.Copy, scale=gcol(G_PS, g)), t, sig=sg("act_u"))
        yield
        mix_ready[4 + g] = VEC(lambda e: e.scalar_tensor_tensor(
            PLL[g][:, :], B[bank][:, :], gcol(G_PS, g), f32(PLH[g][:, :]), ALU.mult, ALU.subtract), hi, t, sig=sg("dve_u"))
        bank_free[bank] = [mix_ready[4 + g]]
        yield

    def peek():
        return t_ring[t_count[0] % 2]

    def under2():
        for which in ("q", "k"):
            chs = [W.take(), W.take()]
            for hf in range(2):
                done = []
                for _ in proj_half(chs, 6 + hf, hf, done):
                    side.step()
                    yield
                side.add(q2_half(hf, 6 + hf, done, 4, peek) if which == "q" else
                         k2_half(hf, 6 + hf, done, 4, peek, STK2))
        for c in (1, 0):
            chs = [W.take(), W.take()]
            for m in (1, 0):
                done = []
                for _ in u_tile(chs, m, done):
                    side.step()
                    yield
                gen = means(2 * c + m, 7 - m, done)
                next(gen)
                side.add(gen)
        ch = W.take()
        outs = Side()
        for g in (3, 2, 1, 0):
            while pool_in[g] is None:
                outs.step()
                side.step()
                yield
            outs.end()
            bk = 7 - g % 2
            t = mm3(B[bk][:, :], (ch[1][:, g, :], ch[2][:, g, :]), (PLH[g][:, :], PLL[g][:, :]), True, True, ch[3],
                    pool_in[g], bank_free[bk], sig=sg("pe_u"))
            outs.add(pooled(g, bk, t))
            yield
        W.free[ch[0]] = t
        outs.end()
        for _ in wo2(0, 1, True):
            yield

    gen2 = under2()
    plan2 = spread([(gen2, 0, 12, 34), (gen2, 12, 39, 54)])

    def fill2(i):
        while o_low:
            o_low.pop()()
        if i in (22, 24, 30, 38):
            o_split((22, 24, 30, 38).index(i))
        plan2(i)

    att2.run(fill2, POOL)
    o_low.pop()()

    h3 = [None] * 8
    x3 = [None] * 8
    s3 = [None]
    nsq_free = [chain_end, chain_end]

    def res2(m, bank, done):
        x3[m] = VEC(lambda e: e.tensor_tensor(XT[:, m, :], B[bank][:, :], XT[:, m, :], ALU.add), done, sig=sg("dve_x3"))
        bank_free[bank] = [x3[m]]
        hi = SCA(lambda e: e.activation(HH[:, m, :], XT[:, m, :], ACT.Copy, scale=gcol(G_N2, m)), x3[m], sig=sg("act_h"))
        h3[m] = VEC(lambda e: e.scalar_tensor_tensor(HL[:, m, :], XT[:, m, :], gcol(G_N2, m), f32(HH[:, m, :]),
                                                     ALU.mult, ALU.subtract), hi, x3[m], sig=sg("dve_h"))
        if m == 0:
            s3[0] = SCA(lambda e: e.activation(NSUM2[:, :], XT[:, 0, :], ACT.Square), x3[0], ur_done, sig=sg("act_xsq"))
        else:
            i = m % 2
            q = SCA(lambda e: e.activation(NSQ[i][:, :], XT[:, m, :], ACT.Square), x3[m], nsq_free[i], a_free,
                    sig=sg("act_xsq"))
            s3[0] = POOL(lambda e: e.tensor_tensor(NSUM2[:, :], NSUM2[:, :], NSQ[i][:, :], ALU.add), q, s3[0],
                         sig=sg("pool_xsum"))
            nsq_free[i] = s3[0]

    ur_done = [(signals["dve_u"], signals["dve_u"].value)]
    a_free = []
    drain(wo2(1, 1, True))
    drain(wo2(2, 1, True))
    for mp in range(3):
        drain(wo2(mp, 0, False))
    drain(wo2(3, 1, True))
    drain(wo2(3, 0, False))
    a_free.append(wo_tok[3])
    for mp in range(4):
        for m in range(2):
            res2(2 * mp + m, mpb2[mp][m], wo_tok[mp])

    first_t = []
    chs = [W.take() for _ in range(4)]
    for c, ch in enumerate(chs):
        kh, gu = c // 2, c % 2
        for k in range(4):
            kt = 4 * kh + k
            for m in range(2):
                bk = 2 * gu + m
                t = tr_mm(B[bk][:, :], ch, k, m, (HH, HL), kt, ALLC, kt == 0, kt == 7, h3[kt],
                          bank_free[bk] if kt == 0 else None, sig=sg("pe_ff") if (k == 3 and m == 1) else None)
        W.free[ch[0]] = t

    def first2(f_ready, r2):
        for m in range(2):
            a, b_, lo = glu(m, 1, ALLC, B[m], B[2 + m], R2, [t, r2], f_free2, m)
            bank_free[m], bank_free[2 + m] = [a], [b_]
            f_ready[m] = lo

    f_free2 = [wo_tok[3], s3[0]]
    f_ready2, ff_end2, _ = ffn(lambda kt: h3[kt], lambda: s3[0], first2, f_free2, [(0, 1, 2, 3), (4, 5, 6, 7)])

    ld_fg = SP(lambda e: e.dma_start(FG[:, :], final_g_2.unsqueeze(0).broadcast_to([128, 1024])),
               [(signals["pe_misc"], signals["pe_misc"].value), (signals["pool_xsum"], signals["pool_xsum"].value)],
               sig=sg("dma_fg"), by=16)
    x3n = None
    x3n_t = []
    for b in range(4):
        for q in range(2):
            bk = 6 + (2 * b + q) % 2
            for i in range(4):
                kt = 4 * q + i
                tr = transpose(B[bk][:, 128 * i:128 * i + 128], XT[:, kt, 128 * b:128 * b + 128], x3[kt], bank_free[bk],
                               sig=sg("pe_x3") if i == 3 else None)
            x3n = SCA(lambda e, b=b, q=q, bk=bk: e.activation(X3N[:, b, 512 * q:512 * q + 512], B[bk][:, :], ACT.Copy),
                      tr, ff_end2, sig=sg("act_x3"))
            bank_free[bk] = [x3n]
    x4 = {}
    sqf = {}

    def finish(b, q, bank, done):
        cols = slice(512 * q, 512 * q + 512)
        x4[b, q] = VEC(lambda e: e.tensor_tensor(X3N[:, b, cols], B[bank][:, :], X3N[:, b, cols], ALU.add), done, x3n,
                       sig=sg("dve_x4"))
        bank_free[bank] = [x4[b, q]]
        sqf[b, q] = SCA(lambda e: e.activation(JNK[:, :], X3N[:, b, cols], ACT.Square,
                                               accum_out=SSF[:, 2 * b + q:2 * b + q + 1]), x4[b, q], sqf.get("last"),
                        ld_fg, sig=sg("act_sf"))
        sqf["last"] = sqf[b, q]

    dsets = [(0, 1, 2, 3), (4, 5, 6, 7)]
    nchunk = NF // 2
    HOLD = 4
    for q in range(2):
        head = nchunk if q == 0 else nchunk - HOLD
        for c in range(head):
            j, wh, wl, wt = W.take()
            for k in range(2):
                kt = 2 * c + k
                for b in range(4):
                    tok = slice(128 * b, 128 * b + 128)
                    bk = dsets[q][b]
                    t = mm3(B[bk][:, :], (FFH[:, kt, tok], FFL[:, kt, tok]), (wh[:, k, :], wl[:, k, :]), kt == 0,
                            kt == NF - 1, wt, f_ready2[kt], bank_free[bk] if kt == 0 else None,
                            sig=sg("pe_dn") if (k == 1 and b == 3) else None)
            W.free[j] = t
        if q == 0:
            for b in range(4):
                finish(b, 0, dsets[0][b], t)
    hold = [W.take() for _ in range(HOLD)]
    ld_out = []
    for b in range(4):
        tok = slice(128 * b, 128 * b + 128)
        bk = dsets[1][b]
        for i, (j, wh, wl, wt) in enumerate(hold):
            for k in range(2):
                kt = 2 * (nchunk - HOLD + i) + k
                t = mm3(B[bk][:, :], (FFH[:, kt, tok], FFL[:, kt, tok]), (wh[:, k, :], wl[:, k, :]), False,
                        kt == NF - 1, wt, f_ready2[kt], sig=sg("pe_dn") if (i == HOLD - 1 and k == 1) else None)
        finish(b, 1, bk, t)
        s = VEC(lambda e, b=b: e.tensor_tensor(SSG[:, b:b + 1], SSF[:, 2 * b:2 * b + 1], SSF[:, 2 * b + 1:2 * b + 2], ALU.add),
                sqf[b, 1], sqf[b, 0], sig=sg("dve_fin"))
        s = VEC(lambda e, b=b: e.tensor_scalar(SSG[:, b:b + 1], SSG[:, b:b + 1], 1.0 / D, EPS, ALU.mult, ALU.add), s,
                sig=sg("dve_fin"))
        p = POOL(lambda e, b=b: e.tensor_tensor(RFN[:, b:b + 1], SSG[:, b:b + 1], HALF[:, :], ALU.pow), s, sig=sg("pool_fin"))
        y = VEC(lambda e, b=b: e.scalar_tensor_tensor(YO[:, b, :], X3N[:, b, :], RFN[:, b:b + 1], FG[:, :], ALU.mult,
                                                      ALU.mult), p, ld_fg, ff_end2, x4[b, 0], x4[b, 1], sig=sg("dve_fin"))
        st = SP(lambda e, b=b: e.dma_start(out[0, 128 * b:128 * b + 128, :], YO[:, b, :]), y, sig=sg("dma_out"), by=16)
    for c in hold:
        W.free[c[0]] = t
    SP(lambda e: e.wait_ge(signals["dma_out"].handle, 64))
    assert W.next == len(chunks)

    with nc.Block() as block:
        @block.sync
        def _(e):
            SP.play(e)

        @block.scalar
        def _(e):
            SCA.play(e)

        @block.vector
        def _(e):
            VEC.play(e)

        @block.gpsimd
        def _(e):
            POOL.play(e)

        @block.tensor
        def _(e):
            PE.play(e)


_INS = ["w_in", "q_norm_a", "k_norm_a", "sink_b", "w_out", "w_gate", "w_up", "w_down", "w_in_2", "b_forget_2",
        "w_pool_2", "w_out_2", "w_gate_2", "w_up_2", "w_down_2", "final_g_2"]
_GAINS = ["norm_mix_pre", "norm_mix_post", "norm_ffn_pre", "norm_ffn_post", "norm1_g_2", "norm2_g_2", "group_norm_a",
          "group_norm_b", "pool_scale_2"]


def kernel(**inputs):
    import concourse.bacc as _bacc
    from concourse.bass_utils import run_bass_kernel_spmd as _run

    nc = _bacc.Bacc("TRN2", target_bir_lowering=False, num_devices=1)
    arrays, args = {}, []
    laid = {"x_t": np.ascontiguousarray(np.asarray(inputs["x"])[0].T.reshape(8, 128, 512).transpose(1, 0, 2)),
            "gain_cols": np.ascontiguousarray(np.concatenate(
                [np.asarray(inputs[n])[0].reshape(-1, 128) for n in _GAINS], axis=0).T)}
    laid.update({n: np.ascontiguousarray(inputs[n]) for n in _INS})
    laid.update(zip(("c_ident", "c_small", "c_rope"), rope_and_masks()))
    for name, a in laid.items():
        arrays[f"in_{name}_dram"] = a
        args.append(nc.dram_tensor(f"in_{name}_dram", a.shape, mybir.dt.from_np(a.dtype), kind="ExternalInput").ap())
    args.append(nc.dram_tensor("out_0_dram", (1, 512, 1024), F32, kind="ExternalOutput").ap())
    program(nc, *args)
    r = _run(nc, [arrays], core_ids=[0])
    return r.results[0]["out_0_dram"]
```

```python
from contextlib import ExitStack

import numpy as np
import concourse.bass as bass
from concourse import mybir

ACT = mybir.ActivationFunctionType
ALU = mybir.AluOpType
AX = mybir.AxisListType
F32 = mybir.dt.float32
F32R = mybir.dt.float32r
BF16 = mybir.dt.bfloat16

EPS = 1e-6
NEG = -3.0e38
D = 1024
FF = 2816
NF = FF // 128
BASE = 16640
NRAW = 3
NSPLIT = 4
WCOLS = 1056

G_PRE, G_FPRE, G_N1, G_N2, G_A, G_B, G_PS = 0, 8, 16, 24, 32, 36, 40
NG = 44


class Signal:

    def __init__(self, handle):
        self.handle, self.value, self.owner = handle, 0, None

    def up(self, owner, by):
        assert self.owner in (None, owner)
        self.owner = owner
        self.value += by
        return (self, self.value)


class Queue:

    def __init__(self, name):
        self.name, self.ops, self.seen = name, [], {}

    def __call__(self, fn, *waits, sig=None, by=1):
        need = []
        todo = list(waits)
        while todo:
            w = todo.pop()
            if w is None:
                continue
            if isinstance(w, list):
                todo += w
                continue
            s, v = w
            if self.seen.get(s, 0) < v:
                self.seen[s] = v
                need.append(w)
        self.ops.append((need, fn, sig, by))
        return sig.up(self.name, by) if sig is not None else None

    def play(self, engine):
        for need, fn, sig, by in self.ops:
            best = {}
            for s, v in need:
                best[s] = max(best.get(s, 0), v)
            for s, v in best.items():
                engine.wait_ge(s.handle, v)
            ins = fn(engine)
            if sig is not None:
                ins.then_inc(sig.handle, by)


def rope_and_masks():
    r = np.arange(128)[:, None]
    c = np.arange(128)[None, :]
    ident = np.eye(128, dtype=np.float32)
    left = np.where(c >= r, 0.0, NEG).astype(np.float32)
    right = np.where(c <= r, 0.0, NEG).astype(np.float32)
    upper = (r <= c).astype(np.float32)
    count = np.zeros((128, 4, 16), np.float32)
    for g in range(4):
        count[:, g, :] = 1.0 / np.minimum(np.arange(16) + 1, 2 ** (g + 1))
    sel = np.zeros((128, 8), np.float32)
    for h in range(8):
        sel[[h, 32 + h, 64 + h, 96 + h], h] = 1.0
    t = np.arange(512, dtype=np.float32)
    theta = np.float64(10000.0)
    fa = (theta ** (-np.arange(16, dtype=np.float64) / 16)).astype(np.float32)
    f1 = (theta ** (-np.arange(32, dtype=np.float64) / 32)).astype(np.float32)
    row, col = np.floor(t / 64).astype(np.float32), (t % 64).astype(np.float32)
    ax = np.concatenate([row[:, None] * fa[None], col[:, None] * fa[None]], axis=1)
    a1 = t[:, None] * f1[None]
    tabs = []
    for ang in (ax, a1):
        cs, sn = np.cos(ang.astype(np.float64)), np.sin(ang.astype(np.float64))
        for full in (np.concatenate([cs, cs], 1), np.concatenate([-sn, sn], 1)):
            tabs.append(full.astype(np.float32).reshape(4, 128, 64).transpose(1, 0, 2).reshape(128, 256))
    small = np.concatenate([left, right, upper, count.reshape(128, 64), sel], axis=1)
    return ident, np.ascontiguousarray(small), np.ascontiguousarray(np.concatenate(tabs, axis=1))


def program(nc, x, x_t, gain_cols, norm_mix_post, norm_ffn_post, w_in, q_norm_a, k_norm_a, sink_b, w_out, w_gate, w_up, w_down, w_in_2, b_forget_2,
            w_pool_2, w_out_2, w_gate_2, w_up_2, w_down_2, final_g_2, c_ident, c_small, c_rope, out):
    ctx = ExitStack()
    signals = {}

    def sg(name):
        if name not in signals:
            signals[name] = Signal(ctx.enter_context(nc.semaphore(name)))
        return signals[name]

    PE, SCA, VEC, POOL, SP = (Queue(n) for n in ("pe", "act", "dve", "pool", "sp"))

    def f32(ap):
        return ap.bitcast(F32)

    def sb(name, shape, dt, off):
        return nc.alloc_sbuf_tensor_at(name, shape, dt, offset=BASE + off)

    o_xt, o_hh, o_hl = 0, 16384, 32768
    XT = sb("XT", [128, 8, 512], F32, o_xt)
    XN = sb("XN", [128, 4, 1024], F32, o_xt)
    HH = sb("HH", [128, 8, 512], F32R, o_hh)
    HL = sb("HL", [128, 8, 512], F32R, o_hl)
    o_raw = 49152
    RAW = [sb(f"RAW{i}", [128, WCOLS], F32, o_raw + 4224 * i) for i in range(NRAW)]
    o_w = o_raw + 4224 * NRAW
    WH = [sb(f"WH{i}", [128, WCOLS], F32R, o_w + 8448 * i) for i in range(NSPLIT)]
    WL = [sb(f"WL{i}", [128, WCOLS], F32R, o_w + 8448 * i + 4224) for i in range(NSPLIT)]
    o_c = o_w + 8448 * NSPLIT
    cur = [o_c]

    def const(name, shape, dt, nbytes):
        t = sb(name, shape, dt, cur[0])
        cur[0] += (nbytes + 31) // 32 * 32
        return t

    IDENT = const("IDENT", [128, 128], F32, 512)
    ONES = const("ONES", [128, 128], F32, 512)
    UPPER = const("UPPER", [128, 128], F32, 512)
    IDB = const("IDB", [128, 128], BF16, 256)
    MLB = const("MLB", [128, 128], BF16, 256)
    MRB = const("MRB", [128, 128], BF16, 256)
    ONB = const("ONB", [128, 128], BF16, 256)
    GC = const("GC", [128, NG], F32, 240)
    ICNT = const("ICNT", [128, 4, 16], F32, 256)
    SEL = const("SEL", [128, 8], F32R, 32)
    SKB = const("SKB", [128, 8], BF16, 16)
    BF = const("BF", [128, 8], F32, 32)
    HALF = const("HALF", [128, 1], F32, 4)
    RN = const("RN", [128, 4], F32, 16)
    RN8 = const("RN8", [128, 4], F32, 16)
    SSH = [const(f"SSH{i}", [128, 16], F32, 64) for i in range(3)]
    FH16 = [const(f"FH16{i}", [128, 16], F32, 64) for i in range(3)]
    NM = const("NM", [128, 8], F32, 32)
    DEN = const("DEN", [128, 8], F32, 32)
    RD = const("RD", [128, 8], F32, 32)
    RSC = const("RSC", [128, 3, 8], F32, 96)
    SSA, SSB = (const(f"SS{i}", [128, 2, 4], F32, 32) for i in range(2))
    VA4, RP4, VB4, RH4 = (const(f"RT{i}", [128, 4], F32, 16) for i in range(4))
    SKF = const("SKF", [128, 8], F32, 32)
    SKT = const("SKT", [128, 8], F32, 32)
    SKT2 = const("SKT2", [128, 8], BF16, 16)
    o_r = cur[0]
    REG = 229368 - BASE - o_r

    def rg(name, shape, dt, off):
        t = sb(name, shape, dt, o_r + off)
        n = 4 if dt != BF16 else 2
        for s in shape[1:]:
            n *= s
        assert off + n <= REG, (name, off + n, REG)
        return t

    PTH = [rg(f"PTH{i}", [128, 4, 256], F32R, 8192 * i) for i in range(2)]
    PTL = [rg(f"PTL{i}", [128, 4, 256], F32R, 8192 * i + 4096) for i in range(2)]
    OR = rg("OR", [128, 8, 512], F32, 16384)
    QS = rg("QS", [128, 8, 512], F32R, 32768)
    K1 = rg("K1", [128, 4, 512], F32R, 49152)
    K2 = rg("K2", [128, 2, 512], F32R, 57344)
    VS = rg("VS", [128, 4, 4, 128], F32R, 61440)
    PR = [rg(f"PR{i}", [128, 516], F32, 69632 + 2080 * i) for i in range(4)]
    OT = [rg(f"OT{i}", [128, 256], F32, 77952 + 1024 * i) for i in range(2)]
    TQ1 = rg("TQ1", [128, 4, 64], F32, 80000)
    TQ2 = rg("TQ2", [128, 4, 64], F32, 81024)
    TAB = rg("TAB", [128, 4, 4, 64], F32, 82048)
    SQS = rg("SQS", [128, 512], F32, 86144)
    QRAW = rg("QRAW", [128, 4, 256], F32, 90240)
    WA = rg("WA", [128, 4, 256], F32, 94336)
    WB = rg("WB", [128, 4, 256], F32, 98432)
    KLN = rg("KLN", [128, 4, 256], F32R, 61440)
    STK = rg("STK", [128, 4, 4, 128], F32R, 102528)
    KRAW, KWA, KWB = (rg(f"KRW{i}", [128, 4, 256], F32, 4096 * i) for i in range(3))
    KST = rg("KST", [128, 4, 4, 128], F32R, 12288)
    FRAW, FWA, FWB = (rg(f"FRW{i}", [128, 4, 256], F32, 20480 + 4096 * i) for i in range(3))
    FST = rg("FST", [128, 4, 4, 128], F32R, 69632)
    CSM = rg("CSM", [128, 456], F32, 104576)
    QKG = rg("QKG", [128, 2, 64], F32, 106496)

    TS = [rg(f"TS{i}", [128, 512], F32, 2048 * i) for i in range(2)]
    TU = [rg(f"TU{i}", [128, 512], F32, 4096 + 2048 * i) for i in range(2)]
    FFH = rg("FFH", [128, NF, 512], F32R, 8192)
    FFL = rg("FFL", [128, NF, 512], F32R, 8192 + 2048 * NF)
    o_n = 8192 + 4096 * NF
    GP2 = rg("GP2", [128, 1024], F32, o_n)
    GP1 = rg("GP1", [128, 1024], F32, 102528)
    JNK = [rg(f"JNK{i}", [128, 512], F32, 106624 + 2048 * i) for i in range(2)]
    R2 = rg("R2", [128, 512], F32, 110720)
    YB = [rg(f"YB{i}", [128, 512], F32, 2048 * i)[:, :] for i in range(4)]
    _mix = [49152, 51200, 61440, 63488, 82048, 84096, 90240, 92288]
    MIXA = [[rg(f"MIXA{b}{f}", [128, 512], F32, _mix[2 * b + f])[:, :] for f in range(2)] for b in range(4)]
    SQA = MIXA[0]
    SQB = [WB[:, 2 * i:2 * i + 2, :].rearrange("p b c -> p (b c)") for i in range(2)]

    QS2 = rg("QS2", [128, 8, 512], F32R, 16384)
    K1B = rg("K1B", [128, 8, 512], F32R, 32768)
    K2B = rg("K2B", [128, 4, 512], F32R, 49152)
    VSB = rg("VSB", [128, 8, 4, 128], F32R, 57344)
    PRB = [rg(f"PRB{i}", [128, 512], F32, 73728 + 2048 * i) for i in range(4)]
    OTB = [rg(f"OTB{i}", [128, 256], F32, 81920 + 1024 * i) for i in range(2)]
    FLG, FL1, FL2, FL3 = (rg(f"FLG{i}", [128, 4, 8], F32, 81920 + 128 * i) for i in range(4))
    ORB = rg("ORB", [128, 4, 512], F32, 83968)
    CT = rg("CT", [104, 512], F32R, 92160)
    STK2 = rg("STK2", [128, 4, 4, 128], F32R, 94208)
    STK3 = rg("STK3", [128, 4, 4, 128], F32R, 73728)
    KLN2 = rg("KLN2", [128, 4, 256], F32R, 102400)
    UR = rg("UR", [128, 4, 512], F32, 94208)
    _at, _pl = [49152, 102400, 40960, 24576], [32768, 36864, 16384, 20480]
    AH = [rg(f"AH{i}", [128, 512], F32R, _at[i]) for i in range(4)]
    AL = [rg(f"AL{i}", [128, 512], F32R, _at[i] + 2048) for i in range(4)]
    PLH = [rg(f"PLH{i}", [128, 512], F32R, _pl[i]) for i in range(4)]
    PLL = [rg(f"PLL{i}", [128, 512], F32R, _pl[i] + 2048) for i in range(4)]
    PS1, PS2 = rg("PS1", [128, 512], F32, _pl[0]), rg("PS2", [128, 512], F32, _pl[0] + 2048)
    PD = rg("PD", [128, 512], F32, 106496)

    YO = sb("YO", [128, 4, 1024], F32, o_hl)
    FG = rg("FG", [128, 1024], F32, o_n)
    SSF = rg("SSF", [128, 8], F32, o_n + 4096)
    SSG = rg("SSG", [128, 4], F32, o_n + 4128)
    RFN = rg("RFN", [128, 4], F32, o_n + 4160)

    B = [ctx.enter_context(nc.psum_tensor(f"B{i}", [128, 512], F32)) for i in range(8)]
    bank_free = [[] for _ in range(8)]

    chunks = []

    def wchunk(w, k0, nk, c0, nc_):
        chunks.append(([(w[0, 128 * k0:128 * (k0 + nk), c0:c0 + nc_].rearrange("(k p) c -> p k c", p=128), 0, nc_)],
                       nk, nc_))

    def wchunk2(w, k0, nk, ca, cb):
        chunks.append(([(w[0, 128 * k0:128 * (k0 + nk), c:c + 128].rearrange("(k p) c -> p k c", p=128), 128 * i, 128)
                        for i, c in enumerate((ca, cb))], nk, 256))

    KCH = [(0, 2), (2, 2), (4, 4)]
    for k0, nk in KCH:
        wchunk2(w_in, k0, nk, 512, 1280)
    for c0 in (0, 256):
        for kh in range(2):
            wchunk(w_in, 4 * kh, 4, c0, 256)
    for kh in range(2):
        wchunk2(w_in, 4 * kh, 4, 640, 1408)
    for c0 in (768, 1024):
        for kh in range(2):
            wchunk(w_in, 4 * kh, 4, c0, 256)
    for kh in range(2):
        for f in range(2):
            for k0 in (0, 2):
                wchunk(w_out, 4 * kh + k0, 2, 512 * f, 512)

    def ffn_chunks(wg, wu, interleave):
        for p in range(NF // 2):
            order = [(w, kh) for kh in range(2) for w in (wg, wu)] if p == 0 and interleave else \
                [(w, kh) for w in (wg, wu) for kh in range(2)]
            for w, kh in order:
                wchunk(w, 4 * kh, 4, 256 * p, 256)

    ffn_chunks(w_gate, w_up, True)
    for f in range(2):
        for k0 in range(0, NF, 2):
            wchunk(w_down, k0, 2, 512 * f, 512)
    for kh in range(2):
        for c0 in (0, 512):
            wchunk(w_in_2, 4 * kh, 4, c0, 256)
    for c0, n in ((1280, 264), (1024, 256), (256, 256), (768, 256), (1800, 256), (1544, 256)):
        for kh in range(2):
            wchunk(w_in_2, 4 * kh, 4, c0, n)
    chunks.append(([(w_pool_2[0].rearrange("g p c -> p g c"), 0, 128)], 4, 128))
    for f in range(2):
        for k0 in (6, 4, 0, 2):
            wchunk(w_out_2, k0, 2, 512 * f, 512)
    ffn_chunks(w_gate_2, w_up_2, True)
    for fh in range(2):
        for k0 in range(0, NF, 2):
            wchunk(w_down_2, k0, 2, 512 * fh, 512)

    LO_POOL = (9, 12, 13, 14, 15, 16, 17, 20, 91, 93, 95, 96, 97, 98, 99, 109, 110, 112)

    class Weights:
        def __init__(self):
            self.loaded, self.split_n, self.next = 0, 0, 0
            self.lo_queue, self.low, self.defer = VEC, [], False
            self.dma, self.hi, self.lo, self.free = {}, {}, {}, {}

        def view(self, t, j):
            _, nk, n = chunks[j]
            return t[:, :nk * n].rearrange("p (k c) -> p k c", k=nk)

        def load(self):
            j = self.loaded
            if j >= len(chunks) or (j >= NRAW and (j - NRAW) not in self.lo):
                return False
            pieces, nk, n = chunks[j]
            dst = self.view(RAW[j % NRAW], j)
            raw_free = [self.hi[j - NRAW], self.lo[j - NRAW]] if j >= NRAW else None
            for ap, c0, cn in pieces:
                self.dma[j] = SP(lambda e, ap=ap, c0=c0, cn=cn: e.dma_start(dst[:, :, c0:c0 + cn], ap),
                                 raw_free, sig=sg(f"dma_w{j % NRAW}"), by=16)
            self.loaded += 1
            return True

        def split(self):
            j = self.split_n
            if j >= self.loaded or (j >= NSPLIT and (j - NSPLIT) not in self.free):
                return False
            _, nk, n = chunks[j]
            raw, hi, lo = (t[:, :nk * n] for t in (RAW[j % NRAW], WH[j % NSPLIT], WL[j % NSPLIT]))
            slot_free = self.free.get(j - NSPLIT)
            self.hi[j] = SCA(lambda e: e.activation(hi, raw, ACT.Copy), self.dma[j], slot_free, sig=sg("act_w"))
            q = POOL if j in LO_POOL else self.lo_queue

            def low(c0, c1):
                t = q(lambda e: e.tensor_tensor(lo[:, c0:c1], raw[:, c0:c1], f32(hi[:, c0:c1]), ALU.subtract), self.hi[j],
                      slot_free, sig=sg(q.name + "_w"))
                if c1 == nk * n:
                    self.lo[j] = t
            mid = [0, nk * n // 2, nk * n] if q is POOL else [0, nk * n]
            self.low += [lambda c0=c0, c1=c1: low(c0, c1) for c0, c1 in zip(mid, mid[1:])]
            self.split_n += 1
            return True

        def begin(self, n, queue):
            if self.split_n < self.next + n:
                self.lo_queue = queue
                assert self.split()
                self.lo_queue = VEC

        def drip(self):
            if self.low:
                self.low.pop(0)()
            while self.load():
                pass

        def flush(self):
            while self.low:
                self.low.pop(0)()

        def ahead(self, n):
            if not self.defer:
                self.flush()
            while self.loaded < min(n, len(chunks)) and self.load():
                pass
            while self.split_n < min(n, len(chunks)):
                if not self.split():
                    break
                if not self.defer:
                    self.flush()
                self.load()
            while self.load():
                pass

        def take(self, more=2):
            j = self.next
            self.next += 1
            while self.split_n <= j:
                if not self.split():
                    self.flush()
                    if self.split_n <= j and not self.split():
                        assert self.load()
            if j not in self.lo or not more:
                self.flush()
            while self.load():
                pass
            if more:
                self.ahead(j + 1 + more)
            assert self.split_n > j
            return j, self.view(WH[j % NSPLIT], j), self.view(WL[j % NSPLIT], j), [self.hi[j], self.lo[j]]

    W = Weights()

    def mm3(dst, sta, mov, start, stop, *waits, sig=None):
        (sh, sl), (mh, ml) = sta, mov
        PE(lambda e: e.matmul(dst, sh, mh, start=start, stop=False), *waits)
        PE(lambda e: e.matmul(dst, sh, ml, start=False, stop=False))
        return PE(lambda e: e.matmul(dst, sl, mh, start=False, stop=stop), sig=sig)

    def transpose(dst, src, *waits, sig=None):
        n = src.shape[0]
        return PE(lambda e: e.transpose(dst, src, IDENT[0:n, 0:n]), *waits, sig=sig)

    ld_gains = SP(lambda e: e.dma_start(GC[:, :], gain_cols), sig=sg("dma_gains"), by=16)
    ld_x = {}

    def load_x(k0, n):
        t = SP(lambda e: e.dma_start(XT[:, k0:k0 + n, :], x_t[:, k0:k0 + n, :]), sig=sg(f"dma_x{k0}"), by=16)
        for k in range(k0, k0 + n):
            ld_x[k] = t

    load_x(0, 1)
    W.load()
    load_x(1, 1)
    W.load()
    load_x(2, 2)
    W.load()
    load_x(4, 2)
    load_x(6, 2)
    cst = sg("pool_const")
    half_ready = POOL(lambda e: e.memset(HALF[:, :], -0.5), sig=cst)
    onb_ready = POOL(lambda e: e.memset(ONB[:, :], 1.0), sig=cst)
    POOL(lambda e: e.memset(SKB[:, :], 0.0), sig=cst)
    ones_ready = POOL(lambda e: e.memset(ONES[:, :], 1.0), sig=cst)
    ld_qkg = None
    for i, g in enumerate((q_norm_a, k_norm_a)):
        ld_qkg = POOL(lambda e, i=i, g=g: e.dma_start(QKG[:, i, :], g[0:1, :].broadcast_to([128, 64])),
                      sig=sg("dma_qkg"), by=16)
    ld_sink = POOL(lambda e: e.dma_start(SKF[:, :], sink_b[0:1, :].broadcast_to([128, 8])), sig=sg("dma_sink"), by=16)
    ld_bf = POOL(lambda e: e.dma_start(BF[:, :], b_forget_2[0:1, :].broadcast_to([128, 8])), sig=sg("dma_bf"), by=16)
    ld_ident = POOL(lambda e: e.dma_start(IDENT[:, :], c_ident), ld_x[4], sig=sg("dma_ident"), by=16)
    ld_csm = POOL(lambda e: e.dma_start(CSM[:, :], c_small), ld_x[6], sig=sg("dma_csm"), by=16)
    ld_tab = POOL(lambda e: e.dma_start(TAB[:, :, :, :].rearrange("p a b c -> p (a b c)"), c_rope), sig=sg("dma_tab"), by=16)
    gains = ld_gains

    def half_col(shape):
        return HALF[:, 0:1].to_broadcast(shape)

    def gcol(g, k):
        return GC[:, g + k:g + k + 1]

    h_ready = [None] * 8
    xs = {"sum": None, "sq": [None, None]}
    XSUM, XSQ = WA[:, 0:2, :].rearrange("p a c -> p (a c)"), [WB[:, 0:2, :].rearrange("p a c -> p (a c)"),
                                                             WB[:, 2:4, :].rearrange("p a c -> p (a c)")]

    def prep(kt):
        hi = SCA(lambda e: e.activation(HH[:, kt, :], XT[:, kt, :], ACT.Copy, scale=gcol(G_PRE, kt)),
                 ld_x[kt], gains, sig=sg("act_h"))
        h_ready[kt] = VEC(lambda e: e.scalar_tensor_tensor(HL[:, kt, :], XT[:, kt, :], gcol(G_PRE, kt),
                                                           f32(HH[:, kt, :]), ALU.mult, ALU.subtract),
                          hi, ld_x[kt], gains, sig=sg("dve_h"))

    def square(kt):
        if kt == 0:
            xs["sum"] = SCA(lambda e: e.activation(XSUM, XT[:, 0, :], ACT.Square), ld_x[0], sig=sg("act_xsq"))
            return
        i = kt % 2
        q = SCA(lambda e: e.activation(XSQ[i], XT[:, kt, :], ACT.Square), ld_x[kt], xs["sq"][i], sig=sg("act_xsq"))
        xs["sum"] = xs["sq"][i] = VEC(lambda e: e.tensor_tensor(XSUM, XSUM, XSQ[i], ALU.add), q, xs["sum"],
                                      sig=sg("dve_xsum"))

    k_chunk = {}
    k_done = [None]

    def k_mm(kt):
        n = max(i for i, (k0, _) in enumerate(KCH) if k0 <= kt)
        k0, nk = KCH[n]
        if n not in k_chunk:
            k_chunk[n] = W.take(0)
        j, wh, wl, wt = k_chunk[n]
        for b in range(4):
            tok = slice(128 * b, 128 * b + 128)
            end = kt == k0 + nk - 1 and b == 3
            t = mm3(B[b // 2][:, 256 * (b % 2):256 * (b % 2) + 256], (HH[:, kt, tok], HL[:, kt, tok]),
                    (wh[:, kt - k0, :], wl[:, kt - k0, :]), kt == 0 and b % 2 == 0, kt == 7 and b % 2 == 1, h_ready[kt], wt,
                    sig=sg("pe_kv") if end else None)
            if end:
                W.free[j] = k_done[0] = t

    def tables(part):
        t1, t2 = (TQ1[:, :, :], TQ2[:, :, :]) if part == 0 else (TAB[:, 0, :, :], TAB[:, 1, :, :])
        before = [ld_tab, ld_qkg, A.tables]
        A.tables = [POOL(lambda e: e.tensor_tensor(t1, TAB[:, 0, :, :], QKG[:, part:part + 1, :].to_broadcast([128, 4, 64]),
                                                   ALU.mult), before, sig=sg("pool_tab"))]
        for s in range(2):
            a, z = 32 * s, 32 * (1 - s)
            A.tables = [POOL(lambda e, a=a, z=z: e.tensor_tensor(
                t2[:, :, a:a + 32], TAB[:, 1, :, a:a + 32],
                QKG[:, part:part + 1, z:z + 32].to_broadcast([128, 4, 32]), ALU.mult), before, sig=sg("pool_tab"))]

    def other_constants():
        c = sg("pool_c")
        POOL(lambda e: e.tensor_copy(IDB[:, :], IDENT[:, :]), ld_ident, sig=c)
        POOL(lambda e: e.tensor_copy(MLB[:, :], CSM[:, 0:128]), ld_csm, sig=c)
        POOL(lambda e: e.tensor_copy(MRB[:, :], CSM[:, 128:256]), sig=c)
        POOL(lambda e: e.tensor_copy(UPPER[:, :], CSM[:, 256:384]), sig=c)
        POOL(lambda e: e.tensor_copy(ICNT[:, :, :].rearrange("p g t -> p (g t)"), CSM[:, 384:448]), sig=c)
        A.consts = POOL(lambda e: e.tensor_copy(SEL[:, :], CSM[:, 448:456]), sig=c)

    sink_ready = [onb_ready]

    def sink_parts():
        s0 = VEC(lambda e: e.tensor_copy(SKB[0:1, :], SKF[0:1, :]), ld_sink, ones_ready, sig=sg("dve_sk"))
        s1 = VEC(lambda e: e.tensor_tensor(SKT[0:1, :], SKF[0:1, :], SKB[0:1, :], ALU.subtract), s0, sig=sg("dve_sk"))
        s2 = VEC(lambda e: e.tensor_copy(SKB[32:33, :], SKT[0:1, :]), s1, sig=sg("dve_sk"))
        s2b = VEC(lambda e: e.tensor_copy(SKT2[0:1, :], SKT[0:1, :]), s1, sig=sg("dve_sk"))
        s3 = VEC(lambda e: e.tensor_tensor(SKT[0:1, :], SKT[0:1, :], SKT2[0:1, :], ALU.subtract), s2, s2b,
                 sig=sg("dve_sk"))
        sink_ready.append(VEC(lambda e: e.tensor_copy(SKB[64:65, :], SKT[0:1, :]), s3, sig=sg("dve_sk")))

    class Bag:
        pass

    A = Bag()
    A.tables = None
    SCA(lambda e: e.activation(RSC[:, 0, 0:1], HALF[:, :], ACT.Square), half_ready, sig=sg("act_first"))
    prep(0)
    k_mm(0)
    prep(1)
    k_mm(1)
    prep(2)
    k_mm(2)
    prep(3)
    square(0)
    square(1)
    k_mm(3)
    prep(4)
    k_mm(4)
    for kt in (5, 6, 7):
        prep(kt)
    W.lo_queue = POOL
    W.ahead(4)
    for kt in (2, 3, 4):
        square(kt)
    k_mm(5)
    W.ahead(5)
    W.lo_queue = VEC
    for kt in (5, 6, 7):
        square(kt)
    k_mm(6)
    k_mm(7)

    ld_xn = SP(lambda e: e.dma_start(XN[:, :, :], x[0].rearrange("(b p) c -> p b c", p=128)), h_ready, xs["sum"], xs["sq"],
               sig=sg("dma_xn"), by=16)

    rstd_use = [0]

    def rstd_tokens(sums, n, bank, done):
        nb = sums.shape[1] // 128
        i = rstd_use[0]
        rstd_use[0] += 1
        v, r = RSC[:, i, 0:nb], RSC[:, i, 4:4 + nb]
        for b in range(nb):
            m = PE(lambda e, b=b: e.matmul(B[bank][:, b:b + 1], sums[:, 128 * b:128 * b + 128], ONES[:, 0:1],
                                           start=True, stop=True), done, ones_ready, bank_free[bank],
                   sig=sg("pe_misc") if b == nb - 1 else None)
        a = VEC(lambda e: e.tensor_scalar(v, B[bank][:, 0:nb], 1.0 / n, EPS, ALU.mult, ALU.add), m, sig=sg("dve_row"))
        bank_free[bank] = [a]
        return r, POOL(lambda e: e.tensor_tensor(r, v, half_col([128, nb]), ALU.pow), a, sig=sg("pool_row"))

    def rstd_rows(dst, r, done, bank, dst_free):
        nb = r.shape[1]
        for b in range(nb):
            m = PE(lambda e, b=b: e.matmul(B[bank][:, 128 * b:128 * b + 128], r[:, b:b + 1].to_broadcast([128, 128]),
                                           IDENT[:, :], start=True, stop=True), done, ld_ident, bank_free[bank],
                   sig=sg("pe_misc") if b == nb - 1 else None)
        c = VEC(lambda e: e.tensor_copy(dst, B[bank][:, 0:128 * nb]), m, dst_free, sig=sg("dve_row"))
        bank_free[bank] = [c]
        return c

    def nat_rstd(r, done):
        a = VEC(lambda e: e.tensor_copy(RN[:, :], r), done, sig=sg("dve_rn"))
        return VEC(lambda e: e.tensor_scalar(RN8[:, :], RN[:, :], 0.125, None, ALU.mult), a, sig=sg("dve_rn"))

    t_ring = [3, 4]
    t_count = [0]

    def t_bank():
        bk = t_ring[t_count[0] % 2]
        t_count[0] += 1
        return bk

    A.q_ready, A.k_ready = {}, []
    A.qs_free = {}
    A.begun = False

    def v_evac(banks, vs, r, h0, nh, done, waits, ready):
        for bk in sorted({bk for bk, _ in banks}):
            mine = [(b, B[bk][:, off:off + 64 * nh].rearrange("p (h c) -> p h c", c=64))
                    for b, (bank, off) in enumerate(banks) if bank == bk]
            for b, src in mine:
                hi = SCA(lambda e, src=src, b=b: e.activation(vs[:, h0:h0 + nh, b, 0:64], src, ACT.Copy,
                                                              scale=r[:, b:b + 1]), done, waits, sig=sg("act_v"))
            yield
            for b, src in mine:
                tok = VEC(lambda e, src=src, b=b: e.scalar_tensor_tensor(
                    vs[:, h0:h0 + nh, b, 64:128], src, r[:, b:b + 1], f32(vs[:, h0:h0 + nh, b, 0:64]),
                    ALU.mult, ALU.subtract), hi, waits, sig=sg("dve_v"))
            bank_free[bk] = [tok]
        ready.append(tok)

    def rope(room, kind, banks, done, slot, turn):
        raw, wa_t, wb_t, stk, ssh_t, f16_t = room.tiles
        n_a = {"qa": 4, "qb": 0, "k": 2}[kind]
        scale = RN8 if kind == "qb" else RN
        ev = []
        for b in range(4):
            bk, off = banks[b]
            ev.append(SCA(lambda e, bk=bk, off=off, b=b: e.activation(
                raw[:, b, :], B[bk][:, off:off + 256], ACT.Copy, scale=scale[:, b:b + 1]),
                done, rn, room.qraw_free, sig=sg("act_q")))
        for b in range(4):
            bank_free[banks[b][0]] = [ev[b]]
        src_t = ev[3]
        yield
        q4 = raw[:, :, :].rearrange("p b (h c) -> p b h c", c=64)
        a4 = wa_t[:, :, :].rearrange("p b (h c) -> p b h c", c=64)
        b4 = wb_t[:, :, :].rearrange("p b (h c) -> p b h c", c=64)
        if n_a:
            ncol = 4 * n_a
            ssh = ssh_t[:, 0:ncol].rearrange("p (b h) -> p b h", b=4)
            f16 = f16_t[:, 0:ncol].rearrange("p (b h) -> p b h", b=4)
            sq = SCA(lambda e: e.activation(b4[:, :, 0:n_a, :], q4[:, :, 0:n_a, :], ACT.Square), src_t, room.wb_free,
                     sig=sg("act_qsq"))
            yield
            s = VEC(lambda e: e.tensor_reduce(ssh, b4[:, :, 0:n_a, :], AX.X, ALU.add), sq, sig=sg("dve_q"))
            if kind == "qa":
                s = VEC(lambda e: e.tensor_scalar(ssh, ssh, 1.0, 64 * EPS, ALU.mult, ALU.add), s, sig=sg("dve_q"))
            else:
                s = VEC(lambda e: e.tensor_scalar(ssh, ssh, 1.0 / 64, EPS, ALU.mult, ALU.add), s, sig=sg("dve_q"))
            yield
            for c in range(0, ncol, 8):
                f = POOL(lambda e, c=c: e.tensor_tensor(f16_t[:, c:c + 8], ssh_t[:, c:c + 8], half_col([128, 8]), ALU.pow),
                         s, sig=sg("pool_q"))
                yield
            fb = f16.unsqueeze(3).to_broadcast([128, 4, n_a, 64])
            src_t = VEC(lambda e: e.tensor_tensor(q4[:, :, 0:n_a, :], q4[:, :, 0:n_a, :], fb, ALU.mult), f, src_t,
                        sig=sg("dve_q"))
            yield
        parts = {"qa": [(0, 4, TQ1[:, :, :], TQ2[:, :, :])],
                 "qb": [(0, 4, TAB[:, 2, :, :], TAB[:, 3, :, :])],
                 "k": [(0, 2, TAB[:, 0, :, :], TAB[:, 1, :, :]), (2, 2, TAB[:, 2, :, :], TAB[:, 3, :, :])]}[kind]
        ta = []
        for h0, nh, t1, t2 in parts:
            for b0 in (0, 2):
                c1 = t1[:, b0:b0 + 2, :].unsqueeze(2).to_broadcast([128, 2, nh, 64])
                ta.append(POOL(lambda e, h0=h0, nh=nh, c1=c1, b0=b0: e.tensor_tensor(
                    a4[:, b0:b0 + 2, h0:h0 + nh, :], q4[:, b0:b0 + 2, h0:h0 + nh, :], c1, ALU.mult), src_t, A.tables,
                    room.wa_free, sig=sg("pool_q")))
            for s in range(2):
                a, z = 32 * s, 32 * (1 - s)
                c2 = t2[:, :, a:a + 32].unsqueeze(2).to_broadcast([128, 4, nh, 32])
                bq = POOL if s and slot in (4, 12) and kind != "k" else VEC
                ta.append(bq(lambda e, h0=h0, nh=nh, a=a, z=z, c2=c2: e.tensor_tensor(
                    b4[:, :, h0:h0 + nh, a:a + 32], q4[:, :, h0:h0 + nh, z:z + 32], c2, ALU.mult),
                    src_t, A.tables, room.wb_free, sig=sg(bq.name + "_q")))
                yield
        room.qraw_free = ta
        yield
        rq = POOL if slot in (4, 8) and kind != "k" else VEC
        rot = rq(lambda e: e.tensor_tensor(wa_t[:, :, :], wa_t[:, :, :], wb_t[:, :, :], ALU.add), ta, sig=sg(rq.name + "_q"))
        room.wb_free = rot
        yield
        assert not room.turning
        st = stk[:, :, :, :].rearrange("p b h c -> p (b h) c")
        wa = wa_t[:, :, :].rearrange("p b (h c) -> p (b h) c", c=64)
        if kind != "k":
            par = slot % 8 // 4
            oh, ol = 64 * par, 64 * (1 - par)
            hi = SCA(lambda e: e.activation(st[:, :, oh:oh + 64], wa, ACT.Copy), rot, room.stk_free, sig=sg("act_qh"))
            yield
            lo = VEC(lambda e: e.tensor_tensor(st[:, :, ol:ol + 64], wa, f32(st[:, :, oh:oh + 64]), ALU.subtract),
                    hi, rot, sig=sg("dve_q"))
        else:
            hi = SCA(lambda e: e.activation(st[:, :, 0:64], wa, ACT.Copy), rot, room.stk_free, sig=sg("act_qh"))
            hi2 = SCA(lambda e: e.activation(st[:, :, 64:128], wa, ACT.Copy), sig=sg("act_qh"))
            yield
            lo = VEC(lambda e: e.tensor_tensor(KLN[:, :, :].rearrange("p b (h c) -> p (b h) c", c=64), wa,
                                               f32(st[:, :, 0:64]), ALU.subtract), hi, rot, sig=sg("dve_q"))
            hi = hi2
        room.wa_free, room.turning = lo, True
        yield
        turns = [("s", b) for b in range(4)]
        if kind == "k":
            turns = [(w, b) for b in range(4) for w in ("s", "l")]
        evac = []
        for w, b in turns:
            bk = turn()
            nh = 4 if w == "s" else 2
            for h in range(nh):
                src = f32(stk[:, b, h, :]) if w == "s" else f32(KLN[:, b, 128 * h:128 * h + 128])
                tr = transpose(B[bk][:, 128 * h:128 * h + 128], src, lo, hi, bank_free[bk],
                               sig=sg("pe_tq") if h == nh - 1 else None)
            cols = slice(128 * b, 128 * b + 128)
            dst = K2[:, 0:2, cols] if w == "l" else K1[:, 0:4, cols] if kind == "k" else QS[:, slot % 8:slot % 8 + 4, cols]
            qs_free = [A.qs_free[slot + i - 8] for i in range(4)] if kind != "k" and slot >= 8 else None
            ev = SCA(lambda e, bk=bk, dst=dst, nh=nh: e.activation(
                dst, B[bk][:, 0:128 * nh].rearrange("p (h c) -> p h c", h=nh), ACT.Copy), tr, qs_free, sig=sg("act_qs"))
            bank_free[bk] = [ev]
            evac.append(ev)
            yield
        room.stk_free, room.turning = tr, False
        if kind == "k":
            A.k_ready = evac
        else:
            for i in range(4):
                A.q_ready[slot + i] = evac

    def nat_proj(banks, hs, res):
        for kh in range(2):
            j, wh, wl, wt = W.take()
            n = wh.shape[2]
            for k in range(4):
                kt = 4 * kh + k
                for b in range(4):
                    bk, off = banks[b]
                    tok = slice(128 * b, 128 * b + 128)
                    t = mm3(B[bk][:, off:off + n], (HH[:, kt, tok], HL[:, kt, tok]), (wh[:, k, :], wl[:, k, :]),
                            kt == 0 and off == 0, kt == 7 and (off > 0 or n > 256), hs[kt], wt, bank_free[bk] if kt == 0 else None,
                            sig=sg("pe_proj") if (k == 3 and b == 3) else None)
                    if b % 2:
                        yield
            W.free[j] = t
        res.append(t)

    PJ = [(6, 0), (6, 256), (7, 0), (7, 256)]

    def drain(gen):
        for _ in gen:
            pass

    class Side:

        def __init__(self):
            self.live = []

        def add(self, gen):
            self.live.append(gen)

        def step(self):
            while self.live:
                try:
                    return next(self.live[0])
                except StopIteration:
                    self.live.pop(0)

        def end(self):
            while self.live:
                self.step()

    side = Side()
    flip = [0]

    def turn34():
        if A.begun:
            return peek()
        flip[0] += 1
        return 3 + flip[0] % 2

    KB = [(0, 0), (0, 256), (1, 0), (1, 256)]
    QB = [(2, 0), (2, 256), (5, 0), (5, 256)]
    res_q, res_v, res_1 = [], [], []
    class Room:

        def __init__(self, tiles):
            self.tiles = tiles
            self.qraw_free = self.wa_free = self.wb_free = self.stk_free = None
            self.turning = False

    room_k = Room((KRAW, KWA, KWB, KST, SSH[1], FH16[1]))
    room_f = Room((FRAW, FWA, FWB, FST, SSH[2], FH16[2]))
    room_q = Room((QRAW, WA, WB, STK, SSH[0], FH16[0]))
    keys = rope(room_k, "k", KB, k_done, 0, turn34)
    first_q = rope(room_f, "qa", PJ, res_q, 0, turn34)
    for i, _ in enumerate(nat_proj(PJ, h_ready, res_q)):
        if i == 2:
            tables(0)
            rn = nat_rstd(*rstd_tokens(XSUM, D, 5, xs["sum"]))
            tables(1)
            room_q.wa_free = room_q.wb_free = rn
        if i in range(3, 14):
            next(keys)
    other_constants()
    room_q.stk_free = [A.consts, A.tables]
    second_q = rope(room_q, "qa", QB, res_1, 4, turn34)
    for i, _ in enumerate(nat_proj(QB, h_ready, res_1)):
        if i < 10:
            next(first_q)
        if i < 2 or i >= 8:
            next(keys, None)
    drain(keys)
    v_ready = []
    values1 = nat_proj(PJ, h_ready, res_v)
    for i in range(12):
        next(values1)
        if i < 2 or i >= 8:
            next(first_q, None)
        if 2 <= i < 7:
            next(second_q)
    drain(first_q)

    def peek():
        return 2

    class Attention:
        def __init__(self, units, P, OTs, vs):
            self.units, self.P, self.OTs, self.vs = units, P, OTs, vs

        def scores(self, i):
            u = self.units[i]
            u.bank = i % 2
            n = u.n
            dst = B[u.bank]
            w = [bank_free[u.bank], u.ready()]
            PE(lambda e: e.matmul(dst[:, 0:n], u.q, u.k1, start=True, stop=False), w)
            last = not u.extra
            u.s = PE(lambda e: e.matmul(dst[:, 0:n], u.qh, u.k2, start=False, stop=last),
                     sig=sg("pe_s") if last else None)
            for n_x, (c0, cn, lhs, rhs, wt) in enumerate(u.extra):
                end = n_x == len(u.extra) - 1
                u.s = PE(lambda e, c0=c0, cn=cn, lhs=lhs, rhs=rhs, end=end: e.matmul(
                    dst[:, c0:c0 + cn], lhs, rhs, start=False, stop=end), wt, sig=sg("pe_s") if end else None)
            u.scored(u.s)

        def maxes(self, i):
            u = self.units[i]
            c = i % 8
            u.max = VEC(lambda e: e.tensor_reduce(NM[:, c:c + 1], B[u.bank][:, 0:u.width], AX.X, ALU.max, negate=True),
                        u.s, self.units[i - 8].exp if i >= 8 else None, sig=sg("dve_max"))

        def exps(self, i):
            u = self.units[i]
            c = i % 8
            p = self.P[i % 4]
            u.exp = SCA(lambda e: e.activation(p[:, 0:u.width], B[u.bank][:, 0:u.width], ACT.Exp, bias=NM[:, c:c + 1],
                                               scale=1.0, accum_out=DEN[:, c:c + 1]),
                        u.max, self.units[i - 4].t if i >= 4 else u.p_free,
                        self.units[i - 8].rec if i >= 8 else None, sig=sg("act_exp"))
            bank_free[u.bank] = [u.exp]

        def norms(self, i):
            u = self.units[i]
            c = i % 8
            p = self.P[i % 4]
            u.rec = VEC(lambda e: e.reciprocal(RD[:, c:c + 1], DEN[:, c:c + 1]), u.exp,
                        self.units[i - 8].norm if i >= 8 else None, sig=sg("dve_rec"))
            u.norm = POOL(lambda e: e.tensor_scalar(p[:, 0:u.n], p[:, 0:u.n], RD[:, c:c + 1], 1.0, ALU.mult, ALU.mult),
                          u.rec, u.exp, sig=sg("pool_p"))

        def turns(self, i):
            u = self.units[i]
            p = self.P[i % 4]
            bk = t_bank()
            nb = u.n // 128
            for j in range(nb):
                u.t = transpose(B[bk][:, 128 * j:128 * j + 128], p[:, 128 * j:128 * j + 128], u.norm, bank_free[bk],
                                sig=sg("pe_t") if j == nb - 1 else None)
            s = u.pair % 2
            cols = slice(128 * (u.b % 2), 128 * (u.b % 2) + 128)
            u.src = B[bk][:, 0:u.n].rearrange("p (k c) -> p k c", c=128)
            u.t_bank = bk
            u.ph, u.pl = (t[s][:, u.kb:u.kb + nb, cols] for t in (PTH, PTL))
            u.pt_free = self.pv_tok.get(u.pair - 2, u.pt_free)
            u.hi = SCA(lambda e: e.activation(u.ph, u.src, ACT.Copy), u.t, u.pt_free, sig=sg("act_pt"))

        def lows(self, i):
            u = self.units[i]
            u.lo = VEC(lambda e: e.tensor_tensor(u.pl, u.src, f32(u.ph), ALU.subtract), u.hi, u.pt_free, sig=sg("dve_pt"))
            bank_free[u.t_bank] = [u.lo]

        def values(self, i):
            u1 = self.units[i]
            u0 = self.units[i - 1]
            assert u0.pair == u1.pair
            s = u1.pair % 2
            bk = 5
            dst = B[bk]
            kbs = sorted(set(range(u0.kb, u0.kb + u0.n // 128)) | set(range(u1.kb, u1.kb + u1.n // 128)))

            def cols(kb):
                has = [u.kb <= kb < u.kb + u.n // 128 for u in (u0, u1)]
                return (0 if has[0] else 128, 256 if has[1] else 128)

            kbs.sort(key=lambda kb: (cols(kb) != (0, 256), kb))
            assert cols(kbs[0]) == (0, 256)
            seq = [(kb, t) for kb in kbs for t in (PTH[s], PTL[s])]
            for n, (kb, t) in enumerate(seq):
                a, z = cols(kb)
                end = n == len(seq) - 1
                pv = PE(lambda e, kb=kb, t=t, a=a, z=z, n=n, end=end: e.matmul(
                    dst[:, a:z], self.vs[:, u1.v, kb, :], t[:, kb, a:z], start=n == 0, stop=end),
                    u0.lo, u1.lo, bank_free[bk], u1.v_ready, sig=sg("pe_pv") if end else None)
            self.pv_tok[u1.pair] = pv
            ot = self.OTs[u1.pair % 2]
            lowc = []

            def low():
                lowc.append(SCA(lambda e: e.activation(ot[0:64, :], dst[64:128, 0:256], ACT.Copy), pv,
                                self.ot_free.get(u1.pair - 2, u1.p_free), sig=sg("act_o")))

            def add():
                t = VEC(lambda e: e.tensor_tensor(u1.o, dst[0:64, 0:256], ot[0:64, :], ALU.add), lowc, u1.o_free,
                        sig=sg("dve_o"))
                self.ot_free[u1.pair] = t
                bank_free[bk] = [t]
                u1.done(t)
            self.low, self.add = low, add

        def run(self, fill, lo_queue):
            self.pv_tok, self.ot_free, self.low, self.add = {}, {}, None, None
            W.defer, W.lo_queue = True, lo_queue
            n = len(self.units)
            self.scores(0)
            for i in range(n + 7):
                low, add, self.low, self.add = self.low, self.add, None, None
                if i < n:
                    self.maxes(i)
                if 0 <= i - 4 < n:
                    self.lows(i - 4)
                if low:
                    low()
                    low = None
                if 0 <= i - 3 < n:
                    self.turns(i - 3)
                if i + 1 < n:
                    self.scores(i + 1)
                if i < n:
                    self.exps(i)
                if low:
                    low()
                if 1 <= i <= n:
                    self.norms(i - 1)
                if add:
                    add()
                k = i - 5
                if 0 <= k < n and k % 2 == 1:
                    self.values(k)
                W.drip()
                fill(i)
            W.defer, W.lo_queue = False, VEC

    class Unit:
        pass

    units = []
    o_done = {}
    for h in range(16):
        win = h >= 8
        kv = (h // 4)
        for b in range(4):
            u = Unit()
            u.h, u.b = h, b
            u.pair = 2 * h + b // 2
            s = kv % 2
            k0, k1 = (max(0, b - 1), min(4, b + 2)) if win else (0, 4)
            u.kb, u.n = k0, 128 * (k1 - k0)
            u.width = u.n + 1 if win else u.n
            slot = h % 8
            u.q = QS[:, slot, 128 * b:128 * b + 128]
            u.qh = QS[64 * s:64 * s + 64, slot, 128 * b:128 * b + 128]
            u.k1 = K1[:, kv, 128 * k0:128 * k1]
            u.k2 = K2[64 * s:64 * s + 64, kv // 2, 128 * k0:128 * k1]
            u.ready = lambda h=h: [A.q_ready[h], A.k_ready]
            u.v, u.v_ready = kv, v_ready
            u.scored = (lambda t, h=h: A.qs_free.setdefault(h, t)) if b == 3 else (lambda t: None)
            u.p_free, u.pt_free, u.o_free = None, None, None
            u.extra = []
            if win:
                if b > 0:
                    u.extra.append((0, 128, IDB[:, :], MLB[:, :], [A.consts]))
                if b < 3:
                    u.extra.append((u.n - 128, 128, IDB[:, :], MRB[:, :], [A.consts]))
                u.extra.append((u.n, 1, ONB[0:65, :], SKB[0:65, h - 8:h - 7], sink_ready))
            u.o = OR[64 * (h % 2):64 * (h % 2) + 64, h // 2, 256 * (b // 2):256 * (b // 2) + 256]
            u.done = lambda t, h=h: o_done.setdefault(h, []).append(t)
            units.append(u)

    hs_o = [None] * 8
    gn = {}

    SQ_POOL = (0, 1, 2, 3, 4, 5, 6)

    def o_tile(t):
        g, i = t // 4, t % 4
        w = [o_done[2 * t], o_done[2 * t + 1]]
        assert all(len(d) == 2 for d in w)
        hi = SCA(lambda e: e.activation(HH[:, t, :], OR[:, t, :], ACT.Copy, scale=gcol((G_A, G_B)[g], i)), w, A.h_free,
                 sig=sg("act_gn"))
        tmp = SQS[:, :] if i == 0 else (SQA, SQB)[g][i % 2]
        free = gn.get("sum") if i == 0 else gn.get((g, i - 2), [A.k_free, room_q.wb_free])
        if t in SQ_POOL:
            sq = POOL(lambda e: e.tensor_tensor(tmp, OR[:, t, :], OR[:, t, :], ALU.mult), w, free, sig=sg("pool_gn"))
        else:
            sq = SCA(lambda e: e.activation(tmp, OR[:, t, :], ACT.Square), w, free, sig=sg("act_gn"))
        yield
        hs_o[t] = VEC(lambda e: e.scalar_tensor_tensor(HL[:, t, :], OR[:, t, :], gcol((G_A, G_B)[g], i), f32(HH[:, t, :]),
                                                       ALU.mult, ALU.subtract), hi, w, A.h_free, sig=sg("dve_gn"))
        if i:
            q = POOL if t in SQ_POOL else VEC
            sq = q(lambda e: e.tensor_tensor(SQS[:, :], SQS[:, :], tmp, ALU.add), sq, gn["sum"], sig=sg(q.name + "_gn"))
        gn["sum"] = gn[g, i] = sq
        yield

    def group_rstd(g, bank):
        gn["r", g] = rstd_tokens(SQS[:, :], 512, bank, gn["sum"])
        gn["sum"] = gn["r", g][1]

    def spread(plan):
        given = [0] * len(plan)

        def go(i):
            for p, (gen, s0, s1, n) in enumerate(plan):
                if s0 <= i < s1:
                    want = -(-n * (i + 1 - s0) // (s1 - s0))
                    while given[p] < want:
                        given[p] += 1
                        next(gen, None)
                if i == s1 - 1 and all(g is not gen for g, *_ in plan[p + 1:]):
                    drain(gen)
        return go

    def tr_mm(dst, chunk, k, m, h, kt, cols, start, stop, *waits, sig=None):
        j, wh, wl, wt = chunk
        hh, hl = h
        return mm3(dst, (wh[:, k, 128 * m:128 * m + 128], wl[:, k, 128 * m:128 * m + 128]),
                   (hh[:, kt, cols], hl[:, kt, cols]), start, stop, wt, *waits, sig=sig)

    ALLC = slice(0, 512)
    HALVES = [slice(0, 256), slice(256, 512)]

    att = Attention(units, PR, OT, VS)
    OH = (HH, HL)
    TOK = [slice(128 * b, 128 * b + 128) for b in range(4)]
    FC = [slice(0, 512), slice(512, 1024)]
    mixa_tok, mixa_todo = {}, []

    def out_mm(dst, ch, k, t, b, start, stop, *waits, sig=None):
        return mm3(dst, (HH[:, t, TOK[b]], HL[:, t, TOK[b]]), (ch[1][:, k, :], ch[2][:, k, :]), start, stop, ch[3], hs_o[t],
                   *waits, sig=sig)

    def wo_a():
        for f in range(2):
            chs = [W.take(), W.take()]
            for b in range(4):
                bk = 6 + b % 2
                for k in range(4):
                    t = out_mm(B[bk][:, :], chs[k // 2], k % 2, k, b, k == 0, k == 3, bank_free[bk] if k == 0 else None,
                               sig=sg("pe_wo") if k % 2 == 1 else None)
                    if b == 3 and k % 2 == 1:
                        W.free[chs[k // 2][0]] = t
                    yield
                    if mixa_todo:
                        mixa_todo.pop(0)()

                def evac(b=b, f=f, bk=bk, t=t):
                    r, p = gn["r", 0]
                    mixa_tok[b, f] = SCA(lambda e: e.activation(MIXA[b][f], B[bk][:, :], ACT.Copy, scale=r[:, b:b + 1]), t, p,
                                         room_q.qraw_free, A.k_free, gn[0, 2], gn[0, 3], sig=sg("act_mixa"))
                    bank_free[bk] = [mixa_tok[b, f]]
                mixa_todo.append(evac)

    wo_ch, wo_done = {}, {}
    WOB = {(0, 0): 6, (1, 0): 7, (0, 1): 0, (1, 1): 1, (2, 0): 2, (3, 0): 3, (2, 1): 4, (3, 1): 5}

    def wo_b(f, ks, bs):
        if f not in wo_ch:
            wo_ch[f] = [W.take(), W.take()]
        for k in ks:
            for b in bs:
                bk = WOB[b, f]
                ch = wo_ch[f][k // 2]
                t = wo_done[b, f] = out_mm(B[bk][:, :], ch, k % 2, 4 + k, b, k == 0, k == 3, bank_free[bk] if k == 0 else None,
                                           sig=sg("pe_wo") if k % 2 == 1 else None)
                if b == 3 and k % 2 == 1:
                    W.free[ch[0]] = t
                yield

    def products1():
        yield from values1
        side.add(v_evac(PJ, VS, RN, 0, 4, res_v, rn, v_ready))
        yield
        for slot in (8, 12):
            res = []
            yield from nat_proj(PJ, h_ready, res)
            A.h_free = res
            side.add(rope(room_q, "qb", PJ, res, slot, peek))
            yield
        yield from wo_a()
        while mixa_todo:
            mixa_todo.pop(0)()
        yield
        yield from wo_b(0, (0, 1, 2), (0, 1))
        yield from wo_b(1, (0, 1, 2), (0, 1))

    A.begun = True
    gen1 = products1()
    plan1 = spread([(gen1, 0, 2, 5), (gen1, 3, 16, 17), (gen1, 17, 31, 17), (gen1, 39, 65, 32), (gen1, 65, 71, 12)])
    begun, ld = [], {}
    starts = dict(zip((34, 35, 37, 38, 47, 58, 63, 70), range(8)))

    def fill1(i):
        if i == 37:
            A.k_free.append(att.pv_tok[units[31].pair])
        if i == 31:
            A.k_free = [units[31].s]
        if i in starts:
            begun.append(o_tile(starts[i]))
        if i == 42:
            group_rstd(0, peek())
        for gen in begun:
            next(gen, None)
        if i < 2:
            plan1(i)
        side.step()
        next(second_q, None)
        if i == 20:
            sink_parts()
        if i == 60:
            ld["gp1"] = SP(lambda e: e.dma_start(GP1[:, :], norm_mix_post.broadcast_to([128, 1024])), room_q.stk_free,
                           sig=sg("dma_gp1"), by=16)
        if i >= 2:
            plan1(i)

    att.run(fill1, VEC)
    p_end = units[-1].t

    class Norm:

        def __init__(self, gain, g_next, h_free, waits):
            self.gain, self.g_next, self.h_free, self.waits = gain, g_next, h_free, waits
            self.sq, self.sq2, self.rp, self.x = {}, {}, {}, {}
            self.h = [[None, None] for _ in range(8)]
            self.tr = {}

        def squares(self, acc, b, f, src, tok, out):
            i = A.junk % 2
            A.junk += 1
            A.junk_tok[i] = out[b, f] = SCA(lambda e: e.activation(JNK[i][:, :], src, ACT.Square, scale=1.0 / 32,
                                                                   accum_out=acc[:, f, b:b + 1]), tok, A.junk_tok[i],
                                            self.waits, sig=sg("act_sq"))

        def square(self, b, f, src, tok):
            self.squares(SSA, b, f, src, tok, self.sq)

        def square2(self, b, f):
            self.squares(SSB, b, f, XN[:, b, FC[f]], self.x[b, f], self.sq2)

        def rms(self, b):
            v = VEC(lambda e: e.scalar_tensor_tensor(VA4[:, b:b + 1], SSA[:, 0, b:b + 1], EPS, SSA[:, 1, b:b + 1], ALU.add,
                                                     ALU.add), self.sq[b, 0], self.sq[b, 1], self.waits, sig=sg("dve_rms"))
            self.rp[b] = POOL(lambda e: e.tensor_tensor(RP4[:, b:b + 1], VA4[:, b:b + 1], HALF[:, :], ALU.pow), v, self.waits,
                              sig=sg("pool_rms"))

        def post(self, b, f, src, dst, free, queue):
            y = VEC(lambda e: e.scalar_tensor_tensor(dst, src, RP4[:, b:b + 1], self.gain[:, FC[f]], ALU.mult, ALU.mult),
                    self.rp[b], free, self.waits, sig=sg("dve_y"))
            xn = XN[:, b, FC[f]]
            self.x[b, f] = queue(lambda e: e.tensor_tensor(xn, xn, dst, ALU.add), y, ld_xn, sig=sg(queue.name + "_x"))
            return y

        def turn(self, hf, p, bank):
            for i in range(2):
                kt = 2 * p + i
                for z in range(2):
                    b = 2 * hf + z
                    self.tr[hf, p] = transpose(
                        B[bank][:, 256 * i + 128 * z:256 * i + 128 * z + 128], XN[:, b, 128 * kt:128 * kt + 128],
                        self.x[b, kt // 4], ld_ident, bank_free[bank], sig=sg("pe_tx") if i == z == 1 else None)

        def split(self, hf, p, bank):
            cols = HALVES[hf]
            hi = {}
            for i in range(2):
                kt = 2 * p + i
                hi[kt] = SCA(lambda e, kt=kt, i=i: e.activation(HH[:, kt, cols], B[bank][:, 256 * i:256 * i + 256], ACT.Copy,
                                                                scale=gcol(self.g_next, kt)), self.tr[hf, p], self.h_free[hf],
                             sig=sg("act_h"))
            for i in range(2):
                kt = 2 * p + i
                self.h[kt][hf] = VEC(lambda e, kt=kt, i=i: e.scalar_tensor_tensor(
                    HL[:, kt, cols], B[bank][:, 256 * i:256 * i + 256], gcol(self.g_next, kt), f32(HH[:, kt, cols]), ALU.mult,
                    ALU.subtract), hi[2 * p], hi[2 * p + 1], self.h_free[hf], sig=sg("dve_h"))
            bank_free[bank] = [self.h[2 * p + 1][hf]]

        def rms2(self):
            v = VEC(lambda e: e.scalar_tensor_tensor(VB4[:, :], SSB[:, 0, :], EPS, SSB[:, 1, :], ALU.add, ALU.add),
                    list(self.sq2.values()), sig=sg("dve_rms"))
            return RH4[:, :], POOL(lambda e: e.tensor_tensor(RH4[:, :], VB4[:, :], half_col([128, 4]), ALU.pow), v,
                             sig=sg("pool_rms"))

    A.junk, A.junk_tok = 0, [None, None]

    def by_halves(mm_next, plan):
        chs = []
        for n in range(16):
            for fn in plan.get(n, ()):
                fn()
            c = n % 8 // 2
            if n < 8 and n % 2 == 0:
                chs.append(W.take(0))
            for k in (0, 1) if n % 2 == 0 else (2, 3):
                mm_next(n // 8, c % 2, 4 * (c // 2) + k, chs[c])

    for gen in begun:
        drain(gen)
    group_rstd(1, 2)
    for b, f in ((0, 0), (0, 1), (1, 0), (1, 1)):
        drain(wo_b(f, (3,), (b,)))
    norm1 = Norm(GP1, G_FPRE, [wo_done[1, 1], None], [ld["gp1"], room_q.stk_free])

    def mix1(b, f):
        r, p = gn["r", 1]
        bk = WOB[b, f]
        c = VEC(lambda e: e.scalar_tensor_tensor(MIXA[b][f], B[bk][:, :], r[:, b:b + 1], MIXA[b][f], ALU.mult, ALU.add),
                wo_done[b, f], p, mixa_tok[b, f], sig=sg("dve_mix"))
        bank_free[bk] = [c]
        norm1.square(b, f, MIXA[b][f], c)

    def post1(bs, f, queues):
        for b, q in zip(bs, queues):
            norm1.post(b, f, MIXA[b][f], MIXA[b][f], norm1.sq[b, f], q)

    for b in range(2):
        for f in range(2):
            mix1(b, f)
    norm1.rms(0)
    norm1.rms(1)
    for f in range(2):
        post1((0, 1), f, (POOL, VEC))
    drain(wo_b(0, range(4), (2, 3)))
    W.begin(1, POOL)
    W.begin(2, POOL)
    W.drip()
    mix1(2, 0)
    mix1(3, 0)
    drain(wo_b(1, range(4), (2,)))
    mix1(2, 1)
    TB = (6, 0, 2, 4)
    for p in range(4):
        norm1.turn(0, p, TB[p])
    norm1.split(0, 0, TB[0])
    W.drip()
    norm1.split(0, 1, TB[1])
    W.drip()
    W.drip()
    drain(wo_b(1, range(4), (3,)))
    norm1.h_free[1] = wo_done[3, 1]
    W.begin(3, POOL)
    mix1(3, 1)
    norm1.rms(2)
    norm1.split(0, 2, TB[2])
    W.drip()
    W.drip()
    norm1.rms(3)
    norm1.split(0, 3, TB[3])
    W.begin(4, VEC)
    for f in range(2):
        post1((2, 3), f, (POOL, VEC))
    W.drip()
    for b in range(2):
        for f in range(2):
            norm1.square2(b, f)
    pair0 = {}
    P0B = [(1, 7), (3, 5)]

    def ffn_half(hf, c, kt, ch):
        bk = P0B[hf][c]
        for m in range(2):
            t = tr_mm(B[bk][:, 256 * m:256 * m + 256], ch, kt % 4, m, OH, kt, HALVES[hf], kt == 0 and m == 0,
                      kt == 7 and m == 1, norm1.h[kt][hf], bank_free[bk] if kt == 0 else None,
                      sig=sg("pe_ff") if (kt % 4 == 3 and m == 1) else None)
        if hf == 1 and kt % 4 == 3:
            W.free[ch[0]] = t
        pair0[hf] = t

    def turn1(*ps):
        for p in ps:
            norm1.turn(1, p, TB[p])

    def split1(*ps):
        for p in ps:
            norm1.split(1, p, TB[p])

    by_halves(ffn_half, {
        5: [lambda: turn1(0, 1), lambda: split1(0, 1)], 6: [lambda: turn1(2, 3), lambda: split1(2, 3)],
        8: [lambda: [norm1.square2(b, f) for b in (2, 3) for f in range(2)]],
        10: [lambda: W.begin(1, VEC)], 11: [W.drip], 12: [lambda: W.begin(2, VEC)], 13: [W.drip],
        14: [lambda: W.begin(3, VEC)], 15: [W.drip]})
    chain1_end = [norm1.x[b, f] for b in range(4) for f in range(2)]

    def glu(fi, n, cols, pg, pu, r, done, free, it):
        ts, tu = TS[it % 2], TU[it % 2]
        width = cols.stop - cols.start
        view = (lambda t: t[:, :].rearrange("p (m c) -> p m c", m=n)) if n > 1 else (lambda t: t[:, :])
        rv = r[:, cols].unsqueeze(1).to_broadcast([128, n, width]) if n > 1 else r[:, cols]
        hv = FFH[:, fi:fi + n, cols] if n > 1 else FFH[:, fi, cols]
        lv = FFL[:, fi:fi + n, cols] if n > 1 else FFL[:, fi, cols]
        t = VEC(lambda e: e.tensor_tensor(view(ts), view(pg), rv, ALU.mult), done, free, F.ts_free[it % 2], sig=sg("dve_ff"))
        u = VEC(lambda e: e.tensor_tensor(view(tu), view(pu), rv, ALU.mult), F.tu_free[it % 2], sig=sg("dve_ff"))
        s = SCA(lambda e: e.activation(ts[:, :], ts[:, :], ACT.Silu), t, sig=sg("act_ff"))
        f = VEC(lambda e: e.tensor_tensor(tu[:, :], ts[:, :], tu[:, :], ALU.mult), s, u, sig=sg("dve_ff"))
        F.ts_free[it % 2] = f
        hi = SCA(lambda e: e.activation(hv, view(tu), ACT.Copy), f, free, sig=sg("act_ff"))
        lo = VEC(lambda e: e.tensor_tensor(lv, view(tu), f32(hv), ALU.subtract), hi, f, sig=sg("dve_ff"))
        F.tu_free[it % 2] = lo
        return t, u, lo

    F = Bag()

    def ffn_pair(p, h_tok, bset, between):
        for gu in range(2):
            for kh in range(2):
                ch = W.take()
                for k in range(4):
                    kt = 4 * kh + k
                    for m in range(2):
                        bk = bset[2 * gu + m]
                        t = tr_mm(B[bk][:, :], ch, k, m, (HH, HL), kt, ALLC, kt == 0, kt == 7, h_tok(kt),
                                  bank_free[bk] if kt == 0 else None, sig=sg("pe_ff") if (k == 3 and m == 1) else None)
                W.free[ch[0]] = t
                between(2 * gu + kh)
        return t

    def ffn(h_tok, rms2, first, f_free, sets):
        F.ts_free, F.tu_free = [f_free, f_free], [f_free, f_free]
        f_ready = [None] * NF
        st = {}

        def between1(i):
            if i == 0:
                st["r"] = rms2()
            if i == 1:
                st["r2"] = rstd_rows(R2[:, :], *st["r"], sets[1][3], None)
                first(f_ready, st["r2"])

        for p in range(1, NF // 2):
            bset = sets[p % 2]
            t = ffn_pair(p, h_tok, bset, between1 if p == 1 else lambda i: None)
            for m in range(2):
                a, b_, lo = glu(2 * p + m, 1, ALLC, B[bset[m]], B[bset[2 + m]], R2, [t, st["r2"]], f_free, m)
                bank_free[bset[m]], bank_free[bset[2 + m]] = [a], [b_]
                f_ready[2 * p + m] = lo
        return f_ready, t

    f_free1 = chain1_end + [p_end]

    def first1(f_ready, r2):
        for hf in range(2):
            bg, bu = P0B[hf]
            a, b_, lo = glu(0, 2, HALVES[hf], B[bg], B[bu], R2, [pair0[0], pair0[1], r2], f_free1, hf)
            bank_free[bg], bank_free[bu] = [a], [b_]
            f_ready[0] = f_ready[1] = lo

    f_ready, ff_end = ffn(lambda kt: norm1.h[kt], norm1.rms2, first1, f_free1, [(1, 3, 5, 7), (0, 2, 4, 6)])
    ld_gp2 = SP(lambda e: e.dma_start(GP2[:, :], norm_ffn_post.broadcast_to([128, 1024])), chain1_end, gn["r", 1][1],
                sig=sg("dma_gp2"), by=16)

    def down_mm(ch, k, kt, b, bk, ready, sig):
        return mm3(B[bk][:, :], (FFH[:, kt, TOK[b]], FFL[:, kt, TOK[b]]), (ch[1][:, k, :], ch[2][:, k, :]), kt == 0,
                   kt == NF - 1, ch[3], ready[kt], bank_free[bk] if kt == 0 else None, sig=sg("pe_dn") if sig else None)

    def down_rows(n0, n1, banks, ready):
        for c in range(n0, n1):
            ch = W.take()
            for k in range(2):
                for b in range(4):
                    t = down_mm(ch, k, 2 * c + k, b, banks[b], ready, k == 1)
            W.free[ch[0]] = t
        return t

    NCH, HOLD = NF // 2, 4
    DNB = [(2, 4, 6, 0), (3, 5, 7, 1)]
    norm2 = Norm(GP2, G_N1, [ff_end, ff_end], [ld_gp2, ff_end])
    t = down_rows(0, NCH, DNB[0], f_ready)
    y_free = [f_ready, f_ready, f_ready, f_ready]

    def post2(b, queues):
        for f in range(2):
            i = 2 * (b % 2) + f
            y = norm2.post(b, f, B[DNB[f][b]][:, :], YB[i], y_free[i], queues[f])
            bank_free[DNB[f][b]] = [y]
            y_free[i] = norm2.x[b, f]

    for b in range(4):
        norm2.square(b, 0, B[DNB[0][b]][:, :], t)
    down_rows(0, NCH - HOLD, DNB[1], f_ready)
    hold = [W.take(2 if i == 0 else 0) for i in range(HOLD)]
    HK = [(i, k, 2 * (NCH - HOLD + i) + k) for i in range(HOLD) for k in range(2)]
    for b in range(2):
        for i, k, kt in HK:
            t = down_mm(hold[i], k, kt, b, DNB[1][b], f_ready, kt == NF - 1)
        norm2.square(b, 1, B[DNB[1][b]][:, :], t)
        norm2.rms(b)
        post2(b, (POOL, VEC))
    for i, k, kt in HK:
        if (i, k) == (2, 0):
            for p in range(2):
                norm2.turn(0, p, (2, 3)[p])
                norm2.split(0, p, (2, 3)[p])
        if (i, k) == (3, 0):
            for p in range(2, 4):
                norm2.turn(0, p, (2, 3)[p % 2])
                norm2.split(0, p, (2, 3)[p % 2])
        for b in (2, 3):
            t = down_mm(hold[i], k, kt, b, DNB[1][b], f_ready, k == 1)
            if kt == NF - 1:
                norm2.square(b, 1, B[DNB[1][b]][:, :], t)
        if k == 1:
            W.free[hold[i][0]] = t
            if i < 3:
                W.begin(i + 1, (VEC, POOL, VEC)[i])
                W.drip()
    for b in (2, 3):
        norm2.rms(b)
    for b in (2, 3):
        post2(b, (POOL, VEC))
    qk_t = {}

    def qk_half(hf, which, kt, ch):
        j, wh, wl, wt = ch
        bk = (4 + which) if hf == 0 else (6 + which)
        for bb in range(2):
            t = mm3(B[bk][:, 256 * bb:256 * bb + 256], (HH[:, kt, TOK[2 * hf + bb]], HL[:, kt, TOK[2 * hf + bb]]),
                    (wh[:, kt % 4, :], wl[:, kt % 4, :]), kt == 0 and bb == 0, kt == 7 and bb == 1, wt,
                    norm2.h[kt][hf], bank_free[bk] if kt == 0 else None,
                    sig=sg("pe_proj") if (kt % 4 == 3 and bb == 1) else None)
        if hf == 1 and kt % 4 == 3:
            W.free[j] = t
        qk_t[hf, which] = t

    def turn2x(*ps):
        for p in ps:
            norm2.turn(1, p, (2, 3)[p % 2])
            norm2.split(1, p, (2, 3)[p % 2])

    by_halves(qk_half, {
        0: [W.drip], 1: [lambda: W.begin(3, POOL)], 2: [W.drip], 3: [W.drip],
        5: [lambda: turn2x(0, 1)], 6: [lambda: turn2x(2, 3)],
        8: [lambda: [norm2.square2(b, f) for b in range(4) for f in range(2)]],
        10: [lambda: W.begin(1, VEC)], 11: [W.drip], 12: [lambda: W.begin(2, VEC)], 13: [W.drip],
        14: [lambda: W.begin(3, VEC)], 15: [W.drip]})
    f_end = t

    r_nat, r_tok = norm2.rms2()
    rn2 = nat_rstd(r_nat, [r_tok, rn])
    chain_end = [r_tok] + [norm2.x[b, f] for b in range(4) for f in range(2)] + norm2.h[7]

    A2 = Bag()
    A2.v_ready = [[], []]
    A2.q_ready, A2.k_ready = {}, {}
    st_free, kl_free = [chain_end, chain_end], [chain_end, chain_end]

    def turn2(bk, srcs, dst, lo):
        n = len(srcs)
        for h, src in enumerate(srcs):
            tr = transpose(B[bk][:, 128 * h:128 * h + 128], src, lo, bank_free[bk], sig=sg("pe_tq") if h == n - 1 else None)
        ev = SCA(lambda e: e.activation(dst, B[bk][:, 0:128 * n].rearrange("p (h c) -> p h c", h=n), ACT.Copy), tr, f_end,
                 sig=sg("act_qs"))
        bank_free[bk] = [ev]
        return tr, ev

    def q2_half(hf, bank, done, h0, turn):
        st = STK2[:, :, :, :].rearrange("p b (h s) c -> p b h s c", s=2)
        mine = [(2 * hf + i, s, B[bank][:, 256 * i:256 * i + 256].rearrange("p (h s c) -> p h s c", s=2, c=64)[:, :, s, :])
                for i in range(2) for s in range(2)]
        free = st_free[hf]
        for b, s, src in mine:
            hi = SCA(lambda e, b=b, s=s, src=src: e.activation(
                st[:, b, :, s, 64 * s:64 * s + 64], src, ACT.Copy, scale=RN8[:, b:b + 1]), done, rn2, free, sig=sg("act_q"))
        yield
        for b, s, src in mine:
            lo = VEC(lambda e, b=b, s=s, src=src: e.scalar_tensor_tensor(
                st[:, b, :, s, 64 - 64 * s:128 - 64 * s], src, RN8[:, b:b + 1],
                f32(st[:, b, :, s, 64 * s:64 * s + 64]), ALU.mult, ALU.subtract), hi, free, rn2, sig=sg("dve_q"))
        bank_free[bank] = [lo]
        yield
        for b in (2 * hf, 2 * hf + 1):
            yield
            st_free[hf], ev = turn2(turn(), [f32(STK2[:, b, h, :]) for h in range(4)],
                                    QS2[:, h0:h0 + 4, 128 * b:128 * b + 128], lo)
            for h in range(4):
                A2.q_ready.setdefault(h0 + h, []).append(ev)

    def k2_half(hf, bank, done, h0, turn, stk):
        mine = [(2 * hf + i, B[bank][:, 256 * i:256 * i + 256].rearrange("p (h c) -> p h c", c=64)) for i in range(2)]
        free = st_free[hf] if stk is STK2 else f_end
        for b, src in mine:
            hi = SCA(lambda e, b=b, src=src: e.activation(
                stk[:, b, :, :].rearrange("p h (s c) -> p h s c", s=2), src.unsqueeze(2).to_broadcast([128, 4, 2, 64]),
                ACT.Copy, scale=RN[:, b:b + 1]), done, rn2, free, sig=sg("act_q"))
        yield
        for b, src in mine:
            lo = VEC(lambda e, b=b, src=src: e.scalar_tensor_tensor(
                KLN2[:, b, :].rearrange("p (h c) -> p h c", c=64), src, RN[:, b:b + 1], f32(stk[:, b, :, 0:64]),
                ALU.mult, ALU.subtract), hi, kl_free[hf], rn2, sig=sg("dve_q"))
        bank_free[bank] = [lo]
        yield
        for b in (2 * hf, 2 * hf + 1):
            cols = slice(128 * b, 128 * b + 128)
            yield
            tr, e1 = turn2(turn(), [f32(stk[:, b, h, :]) for h in range(4)], K1B[:, h0:h0 + 4, cols], lo)
            if stk is STK2:
                st_free[hf] = tr
            else:
                A2.p_free = tr
            yield
            kl_free[hf], e2 = turn2(turn(), [f32(KLN2[:, b, 128 * h:128 * h + 128]) for h in range(2)],
                                    K2B[:, h0 // 2:h0 // 2 + 2, cols], lo)
            for h in range(4):
                A2.k_ready.setdefault(h0 + h, []).extend([e1, e2])

    h2r = norm2.h
    VBK = [(0, 0), (1, 0), (3, 0), (2, 0)]
    VA = [(5, 0), (5, 256), (7, 0), (7, 256)]
    turn_n = [0]

    def turn46():
        turn_n[0] += 1
        return (4, 6)[turn_n[0] % 2]

    early = [q2_half(0, 4, [qk_t[0, 0]], 0, turn46), q2_half(1, 6, [qk_t[1, 0]], 0, turn46),
             k2_half(0, 5, [qk_t[0, 1]], 0, turn46, STK3), k2_half(1, 7, [qk_t[1, 1]], 0, turn46, STK3)]
    for gen in early:
        next(gen)
        next(gen)
        side.add(gen)
    res = []
    for i, _ in enumerate(nat_proj(VBK, h2r, res)):
        if i >= 5:
            side.step()

    fl = None
    for b in range(4):
        bk = VBK[b][0]
        fl = VEC(lambda e, b=b, bk=bk: e.scalar_tensor_tensor(FLG[:, b, :], B[bk][:, 256:264], RN[:, b:b + 1], BF[:, :],
                                                             ALU.mult, ALU.add), ld_bf, res, rn2, f_end,
                 sig=sg("dve_f"))
    ct0 = POOL(lambda e: e.memset(f32(CT[:, :]), 0.0), f_end, sig=sg("pool_f"))

    def v(fn, *w):
        return VEC(fn, *w, sig=sg("dve_f"))

    t1 = v(lambda e: e.scalar_tensor_tensor(FL1[:, :, :], FLG[:, :, :], -1.0, FLG[:, :, :], ALU.mult, ALU.max), fl)
    ex = SCA(lambda e: e.activation(FL1[:, :, :], FL1[:, :, :], ACT.Exp, scale=-1.0), t1, sig=sg("act_f"))
    w1 = v(lambda e: e.tensor_scalar(FL2[:, :, :], FL1[:, :, :], 1.0, None, ALU.add), ex)
    ln = SCA(lambda e: e.activation(FL3[:, :, :], FL2[:, :, :], ACT.Ln), w1, sig=sg("act_f"))
    d1 = v(lambda e: e.scalar_tensor_tensor(FL1[:, :, :], FL2[:, :, :], -1.0, FL1[:, :, :], ALU.add, ALU.subtract), w1)
    rc = v(lambda e: e.reciprocal(FL2[:, :, :], FL2[:, :, :]), d1, ln)
    d2 = v(lambda e: e.tensor_tensor(FL1[:, :, :], FL1[:, :, :], FL2[:, :, :], ALU.mult), rc)
    l1 = v(lambda e: e.tensor_tensor(FL3[:, :, :], FL3[:, :, :], FL1[:, :, :], ALU.subtract), d2, ln)
    lf = v(lambda e: e.scalar_tensor_tensor(FLG[:, :, :], FLG[:, :, :], 0.0, FL3[:, :, :], ALU.min, ALU.subtract), l1)
    drain(v_evac(VBK, VSB, RN, 4, 4, res, [rn2, f_end, fl], A2.v_ready[1]))

    def running_sums():
        for a in range(4):
            cols = slice(128 * a, 128 * a + 128)
            cs = PE(lambda e, a=a, cols=cols: e.matmul(B[0][0:8, cols], FLG[:, a, :], UPPER[:, :], start=a == 0,
                                                       stop=a == 3), lf, A.consts, bank_free[0], sig=sg("pe_misc"))
            if a < 3:
                PE(lambda e, a=a: e.matmul(B[0][0:8, 128 * a + 128:512], FLG[:, a, :],
                                           ONES[:, 0:1].to_broadcast([128, 384 - 128 * a]), start=False, stop=False))
        ch = VEC(lambda e: e.tensor_scalar(CT[0:8, :], B[0][0:8, :], -1.0, None, ALU.mult), cs, ct0, sig=sg("dve_f"))
        ct = VEC(lambda e: e.scalar_tensor_tensor(CT[32:40, :], B[0][0:8, :], -1.0, f32(CT[0:8, :]), ALU.mult,
                                                  ALU.subtract), ch, f_end, sig=sg("dve_f"))
        bank_free[0] = [ct]
        SCA(lambda e: e.activation(CT[64:72, :], f32(CT[0:8, :]), ACT.Copy), ch, sig=sg("act_f"))
        return [ct, SCA(lambda e: e.activation(CT[96:104, :], f32(CT[32:40, :]), ACT.Copy), ct, sig=sg("act_f"))]

    res = []
    for i, _ in enumerate(nat_proj(VA, h2r, res)):
        side.step()
        if i == 11:
            side.end()
            ct = running_sums()
            r2 = rstd_rows(R2[:, :], r_nat, r_tok, 3, None)
    drain(v_evac(VA, VSB, RN, 0, 4, res, [rn2, f_end], A2.v_ready[0]))

    o2_done = {}
    units2 = []
    for h in range(8):
        for b in range(4):
            u = Unit()
            u.h, u.b, u.pair = h, b, 2 * h + b // 2
            s = h % 2
            u.kb, u.n = 0, 128 * (b + 1)
            u.width = u.n
            u.q = QS2[:, h, 128 * b:128 * b + 128]
            u.qh = QS2[64 * s:64 * s + 64, h, 128 * b:128 * b + 128]
            u.k1 = K1B[:, h, 0:u.n]
            u.k2 = K2B[64 * s:64 * s + 64, h // 2, 0:u.n]
            u.ready = lambda h=h: [A2.q_ready[h][:4], A2.k_ready[h][:8], ct]
            u.v, u.v_ready = h, A2.v_ready[h // 4]
            u.scored = lambda t: None
            u.p_free, u.pt_free, u.o_free = [f_end, A2.p_free], [f_end], [f_end]
            u.extra = [(0, u.n, SEL[64 * s:64 * s + 40, h:h + 1].to_broadcast([40, 128]),
                        CT[64 * s:64 * s + 40, 0:u.n], [ct]),
                       (128 * b, 128, IDB[:, :], MRB[:, :], None)]
            u.o = ORB[64 * s:64 * s + 64, h // 2, 256 * (b // 2):256 * (b // 2) + 256]
            u.done = lambda t, h=h: o2_done.setdefault(h, []).append(t)
            units2.append(u)

    att2 = Attention(units2, PRB, OTB, VSB)
    mix_ready = [None] * 8

    def o_split(i):
        src = ORB[:, i, :]
        assert len(o2_done[2 * i]) == len(o2_done[2 * i + 1]) == 2
        w = [o2_done[2 * i], o2_done[2 * i + 1], kl_free, units2[15 if i < 2 else 23].s]
        hi = SCA(lambda e: e.activation(AH[i][:, :], src, ACT.Copy), w, sig=sg("act_os"))

        def low():
            mix_ready[i] = VEC(lambda e: e.tensor_tensor(AL[i][:, :], src, f32(AH[i][:, :]), ALU.subtract), hi, w,
                               sig=sg("dve_os"))
        o_low.append(low)

    o_low = []

    mh = [AH[i] for i in range(4)] + [PLH[i] for i in range(4)]
    ml = [AL[i] for i in range(4)] + [PLL[i] for i in range(4)]
    X2B = [(6, 7, 0, 1), (2, 3, 4, 5)]
    wo2_ch, wo2_done = {}, {}

    def wo2(f, cs, bs):
        for c in cs:
            if (f, c) not in wo2_ch:
                wo2_ch[f, c] = W.take()
            j, wh, wl, wt = wo2_ch[f, c]
            for b in bs:
                bk = X2B[f][b]
                for n, k in enumerate((1, 0) if c < 2 else (0, 1)):
                    kt = (6, 4, 0, 2)[c] + k
                    t = mm3(B[bk][:, :], (mh[kt][:, TOK[b]], ml[kt][:, TOK[b]]), (wh[:, k, :], wl[:, k, :]),
                            c == 0 and n == 0, c == 3 and n == 1, wt, mix_ready[kt],
                            bank_free[bk] if c == 0 and n == 0 else None, sig=sg("pe_wo") if n == 1 else None)
                    yield
                wo2_done[b, f] = t
            if bs[-1] == 3:
                W.free[j] = t

    def proj_half(chs, bank, hf, done):
        for kt in range(8):
            j, wh, wl, wt = chs[kt // 4]
            for i in range(2):
                tok = slice(256 * hf + 128 * i, 256 * hf + 128 * i + 128)
                t = mm3(B[bank][:, 256 * i:256 * i + 256], (HH[:, kt, tok], HL[:, kt, tok]),
                        (wh[:, kt % 4, :], wl[:, kt % 4, :]), kt == 0 and i == 0, kt == 7 and i == 1, h2r[kt], wt,
                        bank_free[bank] if kt == 0 else None, sig=sg("pe_proj") if kt % 4 == 3 and i == 1 else None)
            if hf and kt % 4 == 3:
                W.free[j] = t
            yield
        done.append(t)

    def u_tile(chs, m, done):
        bank = 7 - m
        for kt in range(8):
            t = tr_mm(B[bank][:, :], chs[kt // 4], kt % 4, m, (HH, HL), kt, ALLC, kt == 0, kt == 7, h2r[kt],
                      bank_free[bank] if kt == 0 else None, sig=sg("pe_u") if kt % 4 == 3 else None)
            if m == 0 and kt % 4 == 3:
                W.free[chs[kt // 4][0]] = t
            yield
        done.append(t)

    pool_in = [None] * 4
    last_pd = [None]

    def means(g, bank, done):
        w = [units2[15].s, last_pd[0], chain_end]
        src = UR[:, g, :]
        ur = VEC(lambda e: e.tensor_tensor(src, B[bank][:, :], R2[:, :], ALU.mult), done, r2, st_free, sig=sg("dve_u"))
        bank_free[bank] = [ur]
        yield
        last, cur_t = ur, src
        for lvl in range(g + 1):
            sh = 1 << lvl
            dst = (PS1, PS2)[lvl % 2]
            first = last
            head = VEC(lambda e, dst=dst, cur_t=cur_t, sh=sh: e.tensor_copy(dst[:, 0:sh], cur_t[:, 0:sh]), first, w,
                       sig=sg("dve_u"))
            last = [head, VEC(lambda e, dst=dst, cur_t=cur_t, sh=sh: e.tensor_tensor(
                dst[:, sh:512], cur_t[:, sh:512], cur_t[:, 0:512 - sh], ALU.add), first, w, sig=sg("dve_u"))]
            cur_t = dst[:, :]
            yield
        wide = 1 << (g + 1)
        a = VEC(lambda e: e.tensor_tensor(PD[:, 0:16], cur_t[:, 0:16], ICNT[:, g, :], ALU.mult), last, w, sig=sg("dve_u"))
        b = VEC(lambda e: e.scalar_tensor_tensor(PD[:, 16:512], cur_t[:, 16:512], 1.0 / wide, src[:, 16:512], ALU.mult,
                                                 ALU.subtract), last, w, sig=sg("dve_u"))
        a = VEC(lambda e: e.tensor_tensor(PD[:, 0:16], PD[:, 0:16], src[:, 0:16], ALU.subtract), a, sig=sg("dve_u"))
        yield
        hi = SCA(lambda e: e.activation(PLH[g][:, :], PD[:, :], ACT.Copy), a, b, w, sig=sg("act_u"))
        yield
        pool_in[g] = last_pd[0] = VEC(lambda e: e.tensor_tensor(PLL[g][:, :], PD[:, :], f32(PLH[g][:, :]), ALU.subtract),
                                      hi, w, sig=sg("dve_u"))
        yield

    def pooled(g, bank, t):
        hi = SCA(lambda e: e.activation(PLH[g][:, :], B[bank][:, :], ACT.Copy, scale=gcol(G_PS, g)), t, sig=sg("act_u"))
        yield
        mix_ready[4 + g] = VEC(lambda e: e.scalar_tensor_tensor(
            PLL[g][:, :], B[bank][:, :], gcol(G_PS, g), f32(PLH[g][:, :]), ALU.mult, ALU.subtract), hi, t, sig=sg("dve_u"))
        bank_free[bank] = [mix_ready[4 + g]]
        yield

    def under2():
        for which in ("q", "k"):
            chs = [W.take(), W.take()]
            for hf in range(2):
                done = []
                for n, _ in enumerate(proj_half(chs, 6 + hf, hf, done)):
                    if n in ((1, 3, 4, 5, 7) if which == "q" else (1, 3, 5, 7)):
                        side.step()
                    yield
                side.add(q2_half(hf, 6 + hf, done, 4, peek) if which == "q" else
                         k2_half(hf, 6 + hf, done, 4, peek, STK2))
        for c in (1, 0):
            chs = [W.take(), W.take()]
            for m in (1, 0):
                done = []
                for _ in u_tile(chs, m, done):
                    side.step()
                    yield
                gen = means(2 * c + m, 7 - m, done)
                next(gen)
                side.add(gen)
        ch = W.take()
        outs = Side()
        for g in (3, 2, 1, 0):
            while pool_in[g] is None:
                outs.step()
                side.step()
                yield
            if g == 0:
                outs.step()
                yield
            outs.end()
            bk = 7 - g % 2
            t = mm3(B[bk][:, :], (ch[1][:, g, :], ch[2][:, g, :]), (PLH[g][:, :], PLL[g][:, :]), True, True, ch[3],
                    pool_in[g], bank_free[bk], sig=sg("pe_u"))
            outs.add(pooled(g, bk, t))
            yield
        W.free[ch[0]] = t
        outs.end()
        yield from wo2(0, (0, 1), (0, 1))

    gen2 = under2()
    plan2 = spread([(gen2, 0, 15, 34), (gen2, 15, 38, 54)])

    def fill2(i):
        while o_low:
            o_low.pop()()
        if i in (24, 21, 37, 38):
            o_split((24, 21, 37, 38).index(i))
        plan2(i)

    att2.run(fill2, POOL)
    o_low.pop()()

    h3 = [None] * 8
    norm3 = Norm(None, G_N2, None, [st_free, kl_free, chain_end, last_pd])

    def res2(b, f):
        bk = X2B[f][b]
        norm3.x[b, f] = VEC(lambda e: e.tensor_tensor(XN[:, b, FC[f]], B[bk][:, :], XN[:, b, FC[f]], ALU.add),
                            wo2_done[b, f], sig=sg("dve_x3"))
        bank_free[bk] = [norm3.x[b, f]]

    def turn3(kt, bank):
        for b in range(4):
            tr = transpose(B[bank][:, TOK[b]], XN[:, b, 128 * kt:128 * kt + 128], norm3.x[b, kt // 4], bank_free[bank],
                           sig=sg("pe_tx") if b == 3 else None)
        hi = SCA(lambda e: e.activation(HH[:, kt, :], B[bank][:, :], ACT.Copy, scale=gcol(G_N2, kt)), tr, sig=sg("act_h"))
        h3[kt] = VEC(lambda e: e.scalar_tensor_tensor(HL[:, kt, :], B[bank][:, :], gcol(G_N2, kt), f32(HH[:, kt, :]),
                                                      ALU.mult, ALU.subtract), hi, tr, sig=sg("dve_h"))
        bank_free[bank] = [h3[kt]]

    ALLB = (0, 1, 2, 3)
    drain(wo2(0, (0, 1), (2, 3)))
    drain(wo2(0, (2, 3), ALLB))
    for b in range(4):
        res2(b, 0)
    drain(wo2(1, (0,), ALLB))
    for kt in range(4):
        turn3(kt, X2B[0][kt])
    drain(wo2(1, (1, 2, 3), ALLB))
    for b in range(4):
        norm3.square2(b, 0)
    for b in range(4):
        res2(b, 1)
    wo2_end = wo2_done[3, 1]

    chs = [W.take() for _ in range(4)]
    for c, ch in enumerate(chs):
        kh, gu = c // 2, c % 2
        for k in range(4):
            kt = 4 * kh + k
            for m in range(2):
                bk = X2B[0][2 * gu + m]
                t = tr_mm(B[bk][:, :], ch, k, m, (HH, HL), kt, ALLC, kt == 0, kt == 7, h3[kt],
                          bank_free[bk] if kt == 0 else None, sig=sg("pe_ff") if (k == 3 and m == 1) else None)
        W.free[ch[0]] = t
        if c == 0:
            for kt in range(4, 8):
                turn3(kt, X2B[1][kt - 4])
            for b in range(4):
                norm3.square2(b, 1)

    def first2(f_ready, r2):
        for m in range(2):
            a, b_, lo = glu(m, 1, ALLC, B[X2B[0][m]], B[X2B[0][2 + m]], R2, [t, r2], f_free2, m)
            bank_free[X2B[0][m]], bank_free[X2B[0][2 + m]] = [a], [b_]
            f_ready[m] = lo

    f_free2 = [wo2_end, chain_end]
    f_ready2, ff_end2 = ffn(lambda kt: h3[kt], norm3.rms2, first2, f_free2, X2B)

    ld_fg = SP(lambda e: e.dma_start(FG[:, :], final_g_2.unsqueeze(0).broadcast_to([128, 1024])),
               [wo2_end, last_pd, chain_end], sig=sg("dma_fg"), by=16)
    x4 = {}
    sqf, x4g, sq0 = {}, {}, {}

    def finish(b, q, bank, done):
        cols = slice(512 * q, 512 * q + 512)
        x4[b, q] = VEC(lambda e: e.tensor_tensor(XN[:, b, cols], B[bank][:, :], XN[:, b, cols], ALU.add), done,
                       sig=sg("dve_x4"))
        bank_free[bank] = [x4[b, q]]
        i = A.junk % 2
        A.junk += 1
        A.junk_tok[i] = sqf[b, q] = SCA(lambda e: e.activation(JNK[i][:, :], XN[:, b, cols], ACT.Square, scale=1.0 / 32,
                                                               accum_out=SSF[:, 2 * b + q:2 * b + q + 1]), x4[b, q],
                                        A.junk_tok[i], ld_fg, sig=sg("act_sf"))
        x4g[b, q] = VEC(lambda e: e.tensor_tensor(YO[:, b, cols], XN[:, b, cols], FG[:, cols], ALU.mult), x4[b, q],
                        ld_fg, ff_end2, sig=sg("dve_x4"))

    dsets = [X2B[1], X2B[0]]
    t = down_rows(0, NCH, dsets[0], f_ready2)
    for b in range(4):
        finish(b, 0, dsets[0][b], t)
        sq0[b] = VEC(lambda e, b=b: e.tensor_scalar(SSG[:, b:b + 1], SSF[:, 2 * b:2 * b + 1], 1.0, EPS, ALU.mult, ALU.add),
                     sqf[b, 0], sig=sg("dve_fin"))
    down_rows(0, NCH - HOLD, dsets[1], f_ready2)
    hold = [W.take() for _ in range(HOLD)]
    for b in range(4):
        tok = slice(128 * b, 128 * b + 128)
        bk = dsets[1][b]
        for i, k, kt in HK:
            t = down_mm(hold[i], k, kt, b, bk, f_ready2, kt == NF - 1)
        finish(b, 1, bk, t)
        s = VEC(lambda e, b=b: e.tensor_tensor(SSG[:, b:b + 1], SSG[:, b:b + 1], SSF[:, 2 * b + 1:2 * b + 2], ALU.add),
                sqf[b, 1], sq0[b], sig=sg("dve_fin"))
        p = POOL(lambda e, b=b: e.tensor_tensor(RFN[:, b:b + 1], SSG[:, b:b + 1], HALF[:, :], ALU.pow), s, sig=sg("pool_fin"))
        y0 = SCA(lambda e, b=b: e.activation(YO[:, b, 0:512], YO[:, b, 0:512], ACT.Copy, scale=RFN[:, b:b + 1]), p, x4g[b, 0],
                 sig=sg("act_fin"))
        y1 = VEC(lambda e, b=b: e.tensor_scalar(YO[:, b, 512:1024], YO[:, b, 512:1024], RFN[:, b:b + 1], 1.0, ALU.mult,
                                                ALU.mult), p, x4g[b, 1], sig=sg("dve_fin"))
        for cols, y in ((FC[1], y1), (FC[0], y0)):
            SP(lambda e, b=b, cols=cols: e.dma_start(out[0, 128 * b:128 * b + 128, cols], YO[:, b, cols]), y,
               sig=sg("dma_out"), by=16)
    for c in hold:
        W.free[c[0]] = t
    SP(lambda e: e.wait_ge(signals["dma_out"].handle, 128))
    assert W.next == len(chunks)

    with nc.Block() as block:
        @block.sync
        def _(e):
            SP.play(e)

        @block.scalar
        def _(e):
            SCA.play(e)

        @block.vector
        def _(e):
            VEC.play(e)

        @block.gpsimd
        def _(e):
            POOL.play(e)

        @block.tensor
        def _(e):
            PE.play(e)


_INS = ["w_in", "q_norm_a", "k_norm_a", "sink_b", "w_out", "w_gate", "w_up", "w_down", "w_in_2", "b_forget_2",
        "w_pool_2", "w_out_2", "w_gate_2", "w_up_2", "w_down_2", "final_g_2"]
_GAINS = ["norm_mix_pre", "norm_ffn_pre", "norm1_g_2", "norm2_g_2", "group_norm_a",
          "group_norm_b", "pool_scale_2"]


def kernel(**inputs):
    import concourse.bacc as _bacc
    from concourse.bass_utils import run_bass_kernel_spmd as _run

    nc = _bacc.Bacc("TRN2", target_bir_lowering=False, num_devices=1)
    arrays, args = {}, []
    laid = {"x": np.ascontiguousarray(inputs["x"]),
            "x_t": np.ascontiguousarray(np.asarray(inputs["x"])[0].T.reshape(8, 128, 512).transpose(1, 0, 2)),
            "gain_cols": np.ascontiguousarray(np.concatenate(
                [np.asarray(inputs[n])[0].reshape(-1, 128) for n in _GAINS], axis=0).T)}
    laid.update({n: np.ascontiguousarray(inputs[n]) for n in ("norm_mix_post", "norm_ffn_post")})
    laid.update({n: np.ascontiguousarray(inputs[n]) for n in _INS})
    laid.update(zip(("c_ident", "c_small", "c_rope"), rope_and_masks()))
    for name, a in laid.items():
        arrays[f"in_{name}_dram"] = a
        args.append(nc.dram_tensor(f"in_{name}_dram", a.shape, mybir.dt.from_np(a.dtype), kind="ExternalInput").ap())
    args.append(nc.dram_tensor("out_0_dram", (1, 512, 1024), F32, kind="ExternalOutput").ap())
    program(nc, *args)
    r = _run(nc, [arrays], core_ids=[0])
    return r.results[0]["out_0_dram"]
```
